# Optimizing a Trainium2 kernel written in Bass

```python
import math
import jax, jax.numpy as jnp
from jax import lax
import numpy as np

D_MODEL = 1024
BATCH = 1
SEQ = 512
DEPTH = 1

GRID_W = 64
CTX_LEN = 256
MIX_WIDTH = D_MODEL
HEAD_DIM = 64
ATTN_WIDTH = MIX_WIDTH // 2
N_Q_HEADS = ATTN_WIDTH // HEAD_DIM
N_KV_HEADS = max(1, N_Q_HEADS // 4)
GROUP = N_Q_HEADS // N_KV_HEADS
KV_WIDTH = N_KV_HEADS * HEAD_DIM
HYENA_WIDTH = MIX_WIDTH - ATTN_WIDTH
IN_WIDTH = ATTN_WIDTH + 2 * KV_WIDTH + 3 * HYENA_WIDTH
WINDOW = 128
ATTN_BLOCK = 128
ATTN_SCALE = HEAD_DIM ** -0.5
ROPE_BASE = 10000.0
SHORT_CONV = 3
POS_EMB_DIM = 33
POS_BANDS = (POS_EMB_DIM - 1) // 2
FILTER_FFN = 64
DECAY_TARGET = 1e-2
FAST_DECAY_PCT = 0.3
SLOW_DECAY_PCT = 1.5
MAX_DECAY = -math.log(DECAY_TARGET) / FAST_DECAY_PCT
MIN_DECAY = -math.log(DECAY_TARGET) / SLOW_DECAY_PCT
N_EXPERTS = 32
TOP_K = 4
D_FF = D_MODEL
SWIGLU_LIMIT = 7.0
SWIGLU_ALPHA = 1.702
EXPERT_BLOCK = 128
EPS = 1e-6
NEG_INF = -1e30

kernel_name = 'hymba_hyena_swa_moe_dit_layer'

def rmsnorm(x, g):
    xf = x.astype(jnp.float32)
    y = xf * lax.rsqrt(jnp.mean(xf * xf, axis=-1, keepdims=True) + EPS)
    return y.astype(x.dtype) * g

def modulate(h, shift, scale):
    return h * (1 + scale) + shift

def adaln(cond, w, b):
    return jax.nn.silu(cond) @ w + b

def split_projection(p):
    return jnp.split(p, [ATTN_WIDTH, ATTN_WIDTH + KV_WIDTH, ATTN_WIDTH + 2 * KV_WIDTH], axis=-1)

def axial_rope(x):
    L = x.shape[1]
    rows = L // GRID_W
    row = jnp.repeat(jnp.arange(rows, dtype=jnp.float32), GRID_W)
    col = jnp.tile(jnp.arange(GRID_W, dtype=jnp.float32), rows)
    half = HEAD_DIM // 2
    n_freq = half // 2
    inv_freq = ROPE_BASE ** (-jnp.arange(n_freq, dtype=jnp.float32) / n_freq)

    def rotate(xa, pos):
        ang = pos[:, None] * inv_freq[None, :]
        cos = jnp.cos(ang)[None, :, None, :].astype(x.dtype)
        sin = jnp.sin(ang)[None, :, None, :].astype(x.dtype)
        x1, x2 = xa[..., :n_freq], xa[..., n_freq:]
        return jnp.concatenate([x1 * cos - x2 * sin, x1 * sin + x2 * cos], axis=-1)

    return jnp.concatenate([rotate(x[..., :half], row), rotate(x[..., half:], col)], axis=-1)

def windowed_attention(q, k, v, kc, vc, sink):
    B, L = q.shape[:2]
    Lc = kc.shape[1]
    nb = L // ATTN_BLOCK
    nk = 3 * ATTN_BLOCK
    qb = q.reshape(B, nb, ATTN_BLOCK, N_KV_HEADS, GROUP, HEAD_DIM)

    def band(t):
        tp = jnp.pad(t, ((0, 0), (ATTN_BLOCK, ATTN_BLOCK), (0, 0), (0, 0)))
        tp = tp.reshape(B, nb + 2, ATTN_BLOCK, N_KV_HEADS, HEAD_DIM)
        return jnp.concatenate([tp[:, :-2], tp[:, 1:-1], tp[:, 2:]], axis=2)

    kw, vw = band(k), band(v)
    s_loc = jnp.einsum('bnqhgd,bnkhd->bnhgqk', qb, kw).astype(jnp.float32) * ATTN_SCALE
    i = jnp.arange(ATTN_BLOCK)[:, None]
    j = jnp.arange(nk)[None, :]
    key_pos = (jnp.arange(nb)[:, None, None] - 1) * ATTN_BLOCK + j[None]
    valid = (jnp.abs(j - ATTN_BLOCK - i) <= WINDOW)[None] & (key_pos >= 0) & (key_pos < L)
    s_loc = jnp.where(valid[None, :, None, None], s_loc, NEG_INF)
    s_ctx = jnp.einsum('bnqhgd,bchd->bnhgqc', qb, kc).astype(jnp.float32) * ATTN_SCALE
    s_sink = jnp.broadcast_to(sink.astype(jnp.float32).reshape(1, 1, N_KV_HEADS, GROUP, 1, 1),
                              s_loc.shape[:-1] + (1,))
    p = jax.nn.softmax(jnp.concatenate([s_loc, s_ctx, s_sink], axis=-1), axis=-1)
    p_loc = p[..., :nk].astype(v.dtype)
    p_ctx = p[..., nk:nk + Lc].astype(v.dtype)
    out = (jnp.einsum('bnhgqk,bnkhd->bnqhgd', p_loc, vw)
           + jnp.einsum('bnhgqc,bchd->bnqhgd', p_ctx, vc))
    return out.reshape(B, L, ATTN_WIDTH)

def context_attention(qc, kc, vc, sink):
    B, Lc = qc.shape[:2]
    qg = qc.reshape(B, Lc, N_KV_HEADS, GROUP, HEAD_DIM)
    s = jnp.einsum('bqhgd,bkhd->bhgqk', qg, kc).astype(jnp.float32) * ATTN_SCALE
    s_sink = jnp.broadcast_to(sink.astype(jnp.float32).reshape(1, N_KV_HEADS, GROUP, 1, 1),
                              s.shape[:-1] + (1,))
    p = jax.nn.softmax(jnp.concatenate([s, s_sink], axis=-1), axis=-1)[..., :Lc].astype(vc.dtype)
    return jnp.einsum('bhgqk,bkhd->bqhgd', p, vc).reshape(B, Lc, ATTN_WIDTH)

def short_conv(u, w, b):
    L = u.shape[1]
    pad = SHORT_CONV // 2
    up = jnp.pad(u, ((0, 0), (pad, pad), (0, 0)))
    y = b
    for tap in range(SHORT_CONV):
        y = y + up[:, tap:tap + L] * w[tap]
    return y

def implicit_filter(L, w1, b1, w2, b2, w3, b3, w4, freq):
    f32 = jnp.float32
    t = jnp.linspace(0.0, 1.0, L, dtype=f32)[:, None]
    w = 2.0 * math.pi * jnp.arange(L, dtype=f32)[:, None] / L
    bands = jnp.linspace(1e-4, POS_BANDS - 1, POS_BANDS, dtype=f32)[None, :]
    z = jnp.concatenate([t, jnp.cos(bands * w), -jnp.sin(bands * w)], axis=-1)
    fr = freq.astype(f32)
    h = jnp.sin(fr * (z @ w1.astype(f32) + b1.astype(f32)))
    h = jnp.sin(fr * (h @ w2.astype(f32) + b2.astype(f32)))
    h = jnp.sin(fr * (h @ w3.astype(f32) + b3.astype(f32)))
    k = h @ w4.astype(f32)
    deltas = jnp.linspace(MIN_DECAY, MAX_DECAY, HYENA_WIDTH, dtype=f32)
    decay = jnp.exp(-t * deltas[None, :])
    k_fwd = k[:, :HYENA_WIDTH] * decay
    k_bwd = k[:, HYENA_WIDTH:] * decay
    k_circ = jnp.concatenate([k_fwd, jnp.zeros((1, HYENA_WIDTH), f32), k_bwd[:0:-1]], axis=0)
    return k_circ * lax.rsqrt(jnp.sum(k_circ * k_circ, axis=0, keepdims=True) + EPS)

def bidir_fftconv(u, k_circ, bias):
    L = u.shape[1]
    n = 2 * L
    uf32 = u.astype(jnp.float32)
    uf = jnp.fft.rfft(uf32, n=n, axis=1)
    kf = jnp.fft.rfft(k_circ, n=n, axis=0)
    y = jnp.fft.irfft(uf * kf[None], n=n, axis=1)[:, :L]
    return (y + uf32 * bias.astype(jnp.float32)).astype(u.dtype)

def hyena_mixer(u, conv_w, conv_b, filt, filt_bias):
    L = u.shape[1]
    x0, x1, v = jnp.split(short_conv(u, conv_w, conv_b), 3, axis=-1)
    k_circ = implicit_filter(L, *filt)
    return x0 * bidir_fftconv(x1 * v, k_circ, filt_bias)

def merge_groups(a, y, g_a, g_y, w_out):
    return jnp.concatenate([rmsnorm(a, g_a), rmsnorm(y, g_y)], axis=-1) @ w_out

def moe(h, w_router, b_router, w_gu, b_gu, w_down, b_down):
    B, L, D = h.shape
    T = B * L
    ht = h.reshape(T, D)
    logits = (ht @ w_router + b_router).astype(jnp.float32)
    top_val, top_idx = lax.top_k(logits, TOP_K)
    gates = jax.nn.softmax(top_val, axis=-1)
    A = T * TOP_K
    flat_e = top_idx.reshape(A)
    flat_tok = jnp.arange(A, dtype=jnp.int32) // TOP_K
    flat_g = gates.reshape(A)
    order = jnp.argsort(flat_e)
    se = flat_e[order]
    counts = jnp.bincount(flat_e, length=N_EXPERTS)
    starts = jnp.cumsum(counts) - counts
    pcounts = (counts + EXPERT_BLOCK - 1) // EXPERT_BLOCK * EXPERT_BLOCK
    pends = jnp.cumsum(pcounts)
    pstarts = pends - pcounts
    dest = pstarts[se] + (jnp.arange(A, dtype=jnp.int32) - starts[se])
    n_blocks = (A + EXPERT_BLOCK - 1) // EXPERT_BLOCK + N_EXPERTS
    P = n_blocks * EXPERT_BLOCK
    slot_tok = jnp.full((P,), T, dtype=jnp.int32).at[dest].set(flat_tok[order])
    slot_g = jnp.zeros((P,), jnp.float32).at[dest].set(flat_g[order])
    block_e = jnp.minimum(jnp.searchsorted(pends, jnp.arange(n_blocks) * EXPERT_BLOCK, side='right'),
                          N_EXPERTS - 1)
    xs = jnp.concatenate([ht, jnp.zeros((1, D), ht.dtype)], axis=0)[slot_tok]
    xs = xs.reshape(n_blocks, EXPERT_BLOCK, D)

    def expert_block(args):
        xb, e = args
        gu = xb @ w_gu[e] + b_gu[e]
        gate, up = gu[:, :D_FF], gu[:, D_FF:]
        gate = jnp.minimum(gate, SWIGLU_LIMIT)
        up = jnp.clip(up, -SWIGLU_LIMIT, SWIGLU_LIMIT)
        glu = gate * jax.nn.sigmoid(SWIGLU_ALPHA * gate)
        return ((up + 1) * glu) @ w_down[e] + b_down[e]

    ys = lax.map(expert_block, (xs, block_e)).reshape(P, D)
    out = jax.ops.segment_sum(ys * slot_g[:, None].astype(ys.dtype), slot_tok, num_segments=T + 1)[:T]
    return out.reshape(B, L, D)

def setup_inputs(seed: int = 0) -> dict:
    key = jax.random.key(seed)
    ks = jax.random.split(key, 40)

    def normal(idx, shape, scale=1.0):
        return scale * jax.random.normal(ks[idx], shape, jnp.float32)

    def gain(idx, shape):
        return 1.0 + normal(idx, shape, 0.02)

    return {
        'x': normal(0, (BATCH, SEQ, D_MODEL)),
        'c': normal(1, (BATCH, D_MODEL)),
        'ctx': normal(2, (BATCH, CTX_LEN, D_MODEL)),
        'c_ctx': normal(3, (D_MODEL,)),
        'w_mod': normal(4, (DEPTH, D_MODEL, 6 * D_MODEL), D_MODEL ** -0.5),
        'b_mod': normal(5, (DEPTH, 6 * D_MODEL), 0.01),
        'norm1': gain(6, (DEPTH, D_MODEL)),
        'norm2': gain(7, (DEPTH, D_MODEL)),
        'w_in': normal(8, (DEPTH, D_MODEL, IN_WIDTH), D_MODEL ** -0.5),
        'q_norm': gain(9, (DEPTH, HEAD_DIM)),
        'k_norm': gain(10, (DEPTH, HEAD_DIM)),
        'sink': normal(11, (DEPTH, N_Q_HEADS), 0.5),
        'conv_w': normal(12, (DEPTH, SHORT_CONV, 3 * HYENA_WIDTH), SHORT_CONV ** -0.5),
        'conv_b': normal(13, (DEPTH, 3 * HYENA_WIDTH), 0.01),
        'filt_w1': normal(14, (DEPTH, POS_EMB_DIM, FILTER_FFN), POS_EMB_DIM ** -0.5),
        'filt_b1': normal(15, (DEPTH, FILTER_FFN), 0.1),
        'filt_w2': normal(16, (DEPTH, FILTER_FFN, FILTER_FFN), FILTER_FFN ** -0.5),
        'filt_b2': normal(17, (DEPTH, FILTER_FFN), 0.1),
        'filt_w3': normal(18, (DEPTH, FILTER_FFN, FILTER_FFN), FILTER_FFN ** -0.5),
        'filt_b3': normal(19, (DEPTH, FILTER_FFN), 0.1),
        'filt_w4': normal(20, (DEPTH, FILTER_FFN, 2 * HYENA_WIDTH), FILTER_FFN ** -0.5),
        'filt_freq': gain(21, (DEPTH, FILTER_FFN)),
        'filt_bias': normal(22, (DEPTH, HYENA_WIDTH), 0.1),
        'attn_out_norm': gain(23, (DEPTH, ATTN_WIDTH)),
        'hyena_out_norm': gain(24, (DEPTH, HYENA_WIDTH)),
        'w_out': normal(25, (DEPTH, MIX_WIDTH, D_MODEL), MIX_WIDTH ** -0.5),
        'w_router': normal(26, (DEPTH, D_MODEL, N_EXPERTS), D_MODEL ** -0.5),
        'b_router': normal(27, (DEPTH, N_EXPERTS), 0.01),
        'w_gu': normal(28, (DEPTH, N_EXPERTS, D_MODEL, 2 * D_FF), D_MODEL ** -0.5),
        'b_gu': normal(29, (DEPTH, N_EXPERTS, 2 * D_FF), 0.01),
        'w_down': normal(30, (DEPTH, N_EXPERTS, D_FF, D_MODEL), D_FF ** -0.5),
        'b_down': normal(31, (DEPTH, N_EXPERTS, D_MODEL), 0.01),
    }

def reference(x, c, ctx, c_ctx, w_mod, b_mod, norm1, norm2, w_in, q_norm, k_norm, sink,
              conv_w, conv_b, filt_w1, filt_b1, filt_w2, filt_b2, filt_w3, filt_b3, filt_w4,
              filt_freq, filt_bias, attn_out_norm, hyena_out_norm, w_out,
              w_router, b_router, w_gu, b_gu, w_down, b_down):
    B, L, _ = x.shape
    Lc = ctx.shape[1]
    for l in range(DEPTH):
        last = l == DEPTH - 1
        mod = adaln(c, w_mod[l], b_mod[l])[:, None, :]
        mod_c = adaln(c_ctx[None], w_mod[l], b_mod[l])[:, None, :]
        sh1, sc1, g1, sh2, sc2, g2 = jnp.split(mod, 6, axis=-1)
        csh1, csc1, cg1, csh2, csc2, cg2 = jnp.split(mod_c, 6, axis=-1)
        filt = (filt_w1[l], filt_b1[l], filt_w2[l], filt_b2[l], filt_w3[l], filt_b3[l],
                filt_w4[l], filt_freq[l])
        experts = (w_router[l], b_router[l], w_gu[l], b_gu[l], w_down[l], b_down[l])

        h = modulate(rmsnorm(x, norm1[l]), sh1, sc1)
        q, k, v, u = split_projection(h @ w_in[l])
        q = axial_rope(rmsnorm(q.reshape(B, L, N_Q_HEADS, HEAD_DIM), q_norm[l]))
        k = axial_rope(rmsnorm(k.reshape(B, L, N_KV_HEADS, HEAD_DIM), k_norm[l]))
        v = v.reshape(B, L, N_KV_HEADS, HEAD_DIM)

        hc = modulate(rmsnorm(ctx, norm1[l]), csh1, csc1)
        if last:
            kc, vc = jnp.split(hc @ w_in[l][:, ATTN_WIDTH:ATTN_WIDTH + 2 * KV_WIDTH], 2, axis=-1)
        else:
            qc, kc, vc, uc = split_projection(hc @ w_in[l])
        kc = rmsnorm(kc.reshape(B, Lc, N_KV_HEADS, HEAD_DIM), k_norm[l])
        vc = vc.reshape(B, Lc, N_KV_HEADS, HEAD_DIM)

        a = windowed_attention(q, k, v, kc, vc, sink[l])
        y = hyena_mixer(u, conv_w[l], conv_b[l], filt, filt_bias[l])
        x_new = x + g1 * merge_groups(a, y, attn_out_norm[l], hyena_out_norm[l], w_out[l])
        x_new = x_new + g2 * moe(modulate(rmsnorm(x_new, norm2[l]), sh2, sc2), *experts)

        if not last:
            qc = rmsnorm(qc.reshape(B, Lc, N_Q_HEADS, HEAD_DIM), q_norm[l])
            ac = context_attention(qc, kc, vc, sink[l])
            yc = hyena_mixer(uc, conv_w[l], conv_b[l], filt, filt_bias[l])
            ctx = ctx + cg1 * merge_groups(ac, yc, attn_out_norm[l], hyena_out_norm[l], w_out[l])
            ctx = ctx + cg2 * moe(modulate(rmsnorm(ctx, norm2[l]), csh2, csc2), *experts)
        x = x_new
    return x


_drawn_inputs = setup_inputs


def setup_inputs(seed=0):
    import zlib

    import numpy as np

    out = dict(_drawn_inputs(seed))
    spreads = {}
    factors = {'q_norm': 3.999,
     'k_norm': 6.676,
     'sink': 8.0,
     'conv_b': 2.782,
     'filt_freq': 2.794,
     'attn_out_norm': 9.074,
     'hyena_out_norm': 10.302,
     'b_router': 13.788,
     'b_gu': 23.628,
     'b_down': 33.773,
     'norm2': 2.976}
    for name, (base, spread) in spreads.items():
        noise = np.random.default_rng([zlib.crc32(name.encode()), seed]).standard_normal(out[name].shape)
        drawn = base * np.exp(spread * noise) if base else spread * noise
        out[name] = __import__('jax').numpy.asarray(drawn.astype(out[name].dtype))
    for name, factor in factors.items():
        out[name] = (out[name] * factor).astype(out[name].dtype)
    return out
```

```python
from contextlib import ExitStack

import concourse.bass as bass
from concourse import mybir

P = 128
D = 1024
L = 512
LC = 256
TT = L // P
CT = LC // P
KD = D // P
HD = 64
NQ = 8
NKV = 2
AW = NQ * HD
KVW = NKV * HD
HW = D - AW
HC = HW // P
QKV = AW + 2 * KVW
NE = 32
TOPK = 4
FF = 1024
KF = FF // P
SLOTS = P
BLOCKS = (L * TOPK + NE * (SLOTS - 1)) // SLOTS
BW = BLOCKS + 1
EPS = 1e-6
ATTN_SCALE = HD ** -0.5
LIMIT = 7.0
ALPHA = 1.702
PIECE = 2048
RING = 12
FRONT_RING = 4
TWO_PI_HI = 6.28125
TWO_PI_LO = 6.283185307179586 - TWO_PI_HI
ROUND = 12582912.0
PI_BOUND = 3.1415925

C_BMOD, C_N1, C_N2, C_CW, C_CB, C_FB, C_AG, C_HG = 0, 48, 56, 64, 100, 112, 116, 120
NCOLS = 124
K_ID, K_TRI, K_MASK, K_RC, K_RS = 0, 128, 256, 640, 896
K_SLOT, K_BN, K_VAL, K_ROW, K_TRE, K_JN = 1152, 1280, 1344, 1348, 1349, 1413
NK = 1417
R_QN, R_KN, R_SINK, R_BR = 0, 64, 128, 136
NR = 168


def layer_kernel(nc, t_x, t_ctx, t_cc, t_cols, t_rows, t_konst, t_z, t_w1, t_w23, t_fcol, t_w4,
                 t_decay, t_dft, t_idft, t_wmod, t_brows, t_win, t_wout, t_wr, t_bgu, t_wgu,
                 t_wdown, t_bdown, t_out):
    f32, i32, u32 = mybir.dt.float32, mybir.dt.int32, mybir.dt.uint32
    ALU = mybir.AluOpType
    ACT = mybir.ActivationFunctionType
    X = mybir.AxisListType.X

    d_hn = nc.dram_tensor("normed_rows", [L, D], f32, kind="Internal").ap()
    d_acc = nc.dram_tensor("sums", [L + SLOTS, D], f32, kind="Internal").ap()

    with ExitStack() as ctx:
        def sb(name, shape, dt=f32):
            return ctx.enter_context(nc.sbuf_tensor(name, shape, dt))

        def sem(name):
            return ctx.enter_context(nc.semaphore(name))

        ring = sb("ring", [P, RING, PIECE])
        xt = sb("xt", [P, TT, D])
        big = sb("big", [P, 4096])
        half = sb("half", [P, 2048])
        uT = sb("uT", [P, 3, HC, L])
        qkv = sb("qkv", [P, TT, QKV])
        kvc = sb("kvc", [P, CT, 2 * KVW])
        kT = sb("kT", [P, NKV, L + LC])
        work = sb("work", [P, 2560])
        gB = sb("gB", [P, 2, D])
        cols = sb("cols", [P, NCOLS])
        rows = sb("rows", [P, NR])
        konst = sb("konst", [P, NK])
        ones = sb("ones", [P, P])
        cc = sb("cc", [P, KD, 2])
        cs = sb("cs", [P, KD, 2])
        modc = sb("modc", [P, 32, 2])
        st = sb("st", [P, 192])
        tabs = sb("tabs", [P, BW])
        idx = sb("idx", [P, 2, BW], i32)
        blk = sb("blk", [1, BW + 1], i32)
        icur = sb("icur", [P, 2], i32)
        att_m = sb("att_m", [P, 32])
        att_m2 = st[:, 132:164]
        att_neg = sb("att_neg", [P, 32])
        att_l = sb("att_l", [P, 3, 32])

        ident = konst[:, K_ID:K_ID + P]
        slab = ring[:, 4:6, :].rearrange("p a n -> p (a n)")
        dft = ring[:, 6:8, :].rearrange("p a n -> p (a n)").rearrange("p (t f) -> p t f", t=TT)
        idft = ring[:, 8:10, :].rearrange("p a n -> p (a n)").rearrange("p (f t) -> p f t", f=8)
        kspec = ring[:, 10:12, :].rearrange("p a n -> p (a n)").rearrange("p (f c) -> p f c", f=8)
        xn = ring[:, 8:10, :].rearrange("p a n -> p (a n)").rearrange("p (t d) -> p t d", t=TT)
        hT = big[:, :].rearrange("p (k t) -> p k t", k=KD)
        uspec = big[:, :].rearrange("p (f c) -> p f c", f=8)
        sq = big[:, :].rearrange("p (f c) -> p f c", f=8)
        hcT = half[:, :].rearrange("p (k t) -> p k t", k=KD)
        ztok = half[:, :].rearrange("p (t c) -> p t c", t=TT)
        decay, fa, fb = uT[:, 0], uT[:, 1], uT[:, 2]
        x0, z, v2 = uT[:, 0], uT[:, 1], uT[:, 2]
        cn = qkv[:, :, :].rearrange("p t n -> p (t n)")[:, 0:CT * D].rearrange("p (t d) -> p t d", t=CT)
        qT = slab[:, 0:2048].rearrange("p (j t) -> p j t", j=4)
        aT = slab[:, 2048:4096].rearrange("p (j t) -> p j t", j=4)
        w4 = work[0:64, 0:1024]
        zin = work[0:33, 1024:1536]
        fh = [work[0:64, 1536:2048], work[0:64, 2048:2560]]
        w1 = slab[0:33, 2048:2112]
        w23 = slab[0:64, 2112:2240].rearrange("p (a n) -> p a n", a=2)
        fcol = slab[0:64, 2240:2244]
        ftmp = [slab[0:64, 1024:1536], slab[0:64, 1536:2048]]
        fpair = slab[:, 0:1024].rearrange("p (a n) -> p a n", a=2)
        square = slab[:, 3072:4096]
        rot = [work[:, :].rearrange("p (t n) -> p t n", t=TT), slab[:, 0:2560].rearrange("p (t n) -> p t n", t=TT)]
        kd = slab[:, 2560:4096].rearrange("p (t k r d) -> p t k r d", t=TT + CT, k=NKV, r=2)
        ctxt = gB
        crep = kT[:, :, :].rearrange("p a n -> p (a n)")[:, 0:KD * P].rearrange("p (k m) -> p k m", k=KD)
        hn = xn
        bgu = work[:, 0:NE * 2 * KF].rearrange("p (e j) -> p e j", e=NE)
        wr = work[:, 512:768].rearrange("p (k e) -> p k e", k=KD)
        wtmp = work[:, 1024:2048].rearrange("p (a n) -> p a n", a=2)
        moe = uT[:, :, :, :].rearrange("p a c n -> p (a c n)")
        xs = moe[:, 0:D]
        xsT = moe[:, 1024:2048].rearrange("p (k s) -> p k s", k=KD)
        gh = moe[:, 2048:3072].rearrange("p (k s) -> p k s", k=KF)
        yb = moe[:, 3072:4096]
        gu = moe[:, 4096:5120].rearrange("p (a q s) -> p a q s", a=2, q=4)
        sg = moe[:, 5120:5632].rearrange("p (a q s) -> p a q s", a=2, q=2)
        bcur = moe[:, 5632:5648]
        gcur = moe[:, 5648:5649]

        def pbuf(u):
            return work[:, (u % 2) * 640:(u % 2 + 1) * 640]

        def ptbuf(u):
            return work[:, 1280 + (u % 2) * 640:1280 + (u % 2 + 1) * 640]

        class R:
            a = ring[:, 6:8, :].rearrange("p a n -> p (a n)")
            b = ring[:, 10:12, :].rearrange("p a n -> p (a n)")
            lg = a[:, 0:128].rearrange("p (t e) -> p t e", t=TT)
            v8 = a[:, 128:160].rearrange("p (t e) -> p t e", t=TT)
            i8 = a[:, 160:192].bitcast(u32).rearrange("p (t e) -> p t e", t=TT)
            i8f = a[:, 192:224].rearrange("p (t e) -> p t e", t=TT)
            ex = a[:, 224:240].rearrange("p (t k) -> p t k", t=TT)
            gate = a[:, 240:256].rearrange("p (t k) -> p t k", t=TT)
            OH = a[:, 256:768].rearrange("p (t k e) -> p t k e", t=TT, k=TOPK)
            M = a[:, 768:896].rearrange("p (t e) -> p t e", t=TT)
            G = a[:, 896:1024].rearrange("p (t e) -> p t e", t=TT)
            OHS = a[:, 1024:1536].rearrange("p (t k e) -> p t k e", t=TT, k=TOPK)
            slot_of = a[:, 1536:1664].rearrange("p (t e) -> p t e", t=TT)
            slot = a[:, 1664:1680]
            GE = a[:, 1680:1680 + 16 * (BW + 1)].rearrange("p (i b) -> p i b", i=16)
            bs = a[:, 2480:2544]
            nb4 = a[0:NE, 2560:2564]
            nb = a[0:NE, 2564:2565]
            within = a[:, 2576:2592]
            GT = a[0:NE, 2592:3104]
            sums = a[:, 3104:3120]
            tok = a[:, 3120:3120 + BW]
            S1 = b[:, 0:2048].rearrange("p (i s) -> p i s", i=16)
            B2 = b[:, 2048:2048 + 16 * 2 * BW].rearrange("p (i b) -> p i b", i=16)
            nbrep = b[0:NE, 3600:3728]
            bd = half[0:NE, 0:D]
            blkcmp = slab[0:1, 1024:1024 + BW * NE].rearrange("p (b e) -> p b e", b=BW)
            blkf = a[0:1, 3200:3200 + BW + 1]


        bank = [ctx.enter_context(nc.psum_tensor(f"bank{i}", [P, 512], f32)) for i in range(8)]

        names = """x_in small_in filter_in ctx_in dft_in idft_in decay_in xn_free
            chain_v chain_a chain_p
            ones_ok silu fnet_mm fnet_lin fnet_sin filt_mm filt_pair filt_tile filt_sq fspec_mm
            fspec_out nsum_mm nsum_out moda_mm moda_out stat_x xn_ok cn_ok hT_mm hT_ok hcT_mm hcT_ok
            piece_used unit_mm unit_out modb_mm modb_out crep_ok
            z_ok zT_mm zT_ok uspec_mm uspec_out yspec inv_mm y_ok ysq ysum_mm ysum_out yT_ok
            qk_ok kd_ok qkT_mm qkT_ok s_mm s_max p_ok pT_mm pT_ok pv_mm l_sink a_ok a_mul aT_mm aT_ok
            wo_mm xnew stat2 hn_ok hn_stored h2T_mm h2T_ok lg_mm route_exp route_shift cntc_mm nbrep
            bs_mm pos_mm onehot tab_mm gmat gT_mm gT_ok bd_mm acc_ok acc_in tables
            free_ring gathered xs_used xsT_mm xsT_ok gu_mm sig gate_ready h_ok down_mm y_out scattered
            out_done glu_p late_in brow_in xs_sq y_mul yr_lin yr_sqrt ns_lin ns_sqrt x_lin x_sqrt silu_s
            qk_lin qk_sqrt s_local l_exp a_lin a_sqrt n2_sq n2_lin n2_sqrt gexp_in pool_step cs_ok""".split()
        S = {n: sem(n) for n in names}
        stream = [sem(f"stream{i}") for i in range(FRONT_RING)]
        full = [sem(f"full{i}") for i in range(RING)]

        block = ctx.enter_context(nc.Block())

        ORDER = ([("A", k) for k in range(8)] + [("W", i) for i in (3, 4, 5, 6, 7, 8, 0, 1, 2)]
                 + [("B", i) for i in range(16)] + [("O", i) for i in range(4)])
        AT = {w: n for n, w in enumerate(ORDER)}

        def piece_src(what, i):
            if what == "A":
                return t_wmod[i * P:(i + 1) * P, 0:2048]
            if what == "W":
                return t_win.rearrange("(k p) n -> p k n", p=P)[:, :, i * 256:(i + 1) * 256]
            if what == "B":
                k, h = i // 2, i % 2
                return t_wmod[k * P:(k + 1) * P, 2048 + h * 2048:4096 + h * 2048]
            return t_wout[i * 256:(i + 1) * 256, :].rearrange("(c p) n -> p c n", p=P)

        def piece(what, i):
            return ring[:, AT[what, i] % FRONT_RING, :]

        def piece_ready(eng, what, i):
            n = AT[what, i]
            eng.wait_ge(stream[n % FRONT_RING], 16 * (n // FRONT_RING + 1))

        UNITS = ([(i, "u", c) for i in (3, 4, 5, 6, 7, 8) for c in range(2)]
                 + [(i, "q", t) for i in (0, 1) for t in range(TT)]
                 + [(2, "q", t) for t in range(TT)] + [(2, "c", t) for t in range(CT)])
        def used(what, i):
            if what == "W":
                return S["unit_mm"], 1 + max(n for n, u in enumerate(UNITS) if u[0] == i)
            return S["piece_used"], i + 1 + (8 if what == "B" else 0)

        ATT = [(qb, h) for qb in range(TT) for h in range(NQ)]

        def local_keys(qb):
            return max(0, qb - 1) * P, min(TT, qb + 2) * P

        @block.sync
        def _(sp):
            sp.dma_start(xt[:, :, :], t_x.rearrange("(t p) d -> p t d", p=P)).then_inc(S["x_in"], 16)
            sp.dma_start(dft[:, :, :], t_dft.rearrange("(t p) f -> p t f", p=P)).then_inc(S["dft_in"], 16)
            sp.dma_start(decay, t_decay.rearrange("(t p) c -> p t c", p=P)).then_inc(S["decay_in"], 16)
            for n, w in enumerate(ORDER):
                if n >= FRONT_RING:
                    sp.wait_ge(*used(*ORDER[n - FRONT_RING]))
                dst = ring[:, n % FRONT_RING, :]
                if w[0] == "W":
                    dst = dst.rearrange("p (k n) -> p k n", k=KD)
                if w[0] == "O":
                    dst = dst.rearrange("p (c n) -> p c n", c=2)
                sp.dma_start(dst, piece_src(*w)).then_inc(stream[n % FRONT_RING], 16)
                if w == ("W", 8):
                    sp.wait_ge(S["cn_ok"], CT)
                    sp.dma_start(gB[:, :, :].rearrange("p a n -> p (a n)"), t_brows.to_broadcast([P, 2 * D])).then_inc(S["brow_in"], 16)
                    sp.wait_ge(S["hT_mm"], KD)
                    sp.dma_start(idft[:, :, :], t_idft.rearrange("(f p) t -> p f t", p=P)).then_inc(S["idft_in"], 16)
            sp.wait_ge(S["a_ok"], TT)
            sp.dma_start(bgu, t_bgu).then_inc(S["late_in"], 16)
            sp.dma_start(wr, t_wr.rearrange("(k p) e -> p k e", p=P)).then_inc(S["late_in"], 16)
            sp.wait_ge(S["yT_ok"], HC)
            sp.dma_start(R.bd, t_bdown).then_inc(S["late_in"], 16)
            sp.wait_ge(S["tables"], 1)
            sp.wait_ge(S["hn_stored"], 16 * TT)
            nblk = sp.value_load(blk[0:1, BW:BW + 1], min_val=1, max_val=BLOCKS)
            with sp.Fori(0, BLOCKS) as b:
                with sp.If(b < nblk):
                    e = sp.value_load(blk[0:1, bass.ds(b, 1)], min_val=0, max_val=NE - 1)
                    for s in range(RING):
                        if s == KD - 1:
                            sp.wait_ge(S["gu_mm"], b * 4)
                        elif s == RING - 1:
                            sp.wait_ge(S["down_mm"], b)
                        else:
                            sp.wait_ge(S["free_ring"], b * (RING - 2) + (s + 1 if s < KD else s))
                        if s < KD:
                            src = t_wgu[bass.ds(e * KD + s, 1), :, :].rearrange("o p n -> (o p) n")
                            sp.dma_start(ring[:, s, :], src).then_inc(full[s], 16)
                        else:
                            src = t_wdown[bass.ds(e * 4 + s - KD, 1), :, :, :].rearrange("o c p n -> p (o c) n")
                            sp.dma_start(ring[:, s, :].rearrange("p (c n) -> p c n", c=2), src).then_inc(full[s], 16)

        @block.tensor
        def _(pe):
            mm, tr = nc.tensor.matmul, nc.tensor.transpose
            pe.wait_ge(S["filter_in"], 80)
            mm(bank[0][0:64, :], w1, zin, start=True, stop=True).then_inc(S["fnet_mm"], 1)
            for i in range(2):
                pe.wait_ge(S["fnet_sin"], i + 1)
                mm(bank[0][0:64, :], w23[:, i, :], fh[i], start=True, stop=True).then_inc(S["fnet_mm"], 1)
            pe.wait_ge(S["fnet_sin"], 3)
            for t in range(TT):
                if t >= 2:
                    pe.wait_ge(S["filt_pair"], t - 1)
                for h in range(2):
                    last = mm(bank[1 + 2 * (t % 2) + h][:, :], fh[0][:, t * P:(t + 1) * P],
                              w4[:, h * HW:(h + 1) * HW], start=True, stop=True)
                last.then_inc(S["filt_mm"], 1)
            pe.wait_ge(S["filt_tile"], TT)
            pe.wait_ge(S["dft_in"], 16)
            for f in range(9):
                src = fa if f < 4 or f == 8 else fb
                if f >= 3:
                    pe.wait_ge(S["fspec_out"], f - 2)
                dst = bank[5 + f % 3]
                for t in range(TT):
                    if f < 8:
                        last = mm(dst[:, :], dft[:, t, f * P:(f + 1) * P], src[:, t, :], start=t == 0, stop=t == TT - 1)
                    else:
                        last = mm(dst[0:1, :], dft[:, t, L:L + 1], src[:, t, :], start=t == 0, stop=t == TT - 1)
                last.then_inc(S["fspec_mm"], 1)
            pe.wait_ge(S["filt_sq"], 2 * TT)
            pe.wait_ge(S["ones_ok"], 1)
            for c in range(HC):
                for n in range(2 * TT):
                    last = mm(bank[1][:, c:c + 1], sq[:, n, c * P:(c + 1) * P], ones[:, 0:1], start=n == 0, stop=n == 2 * TT - 1)
            last.then_inc(S["nsum_mm"], 1)
            pe.wait_ge(S["silu"], 1)
            for k in range(8):
                piece_ready(pe, "A", k)
                for j in range(16):
                    last = mm(bank[0][:, 2 * j:2 * j + 2], piece("A", k)[:, j * P:(j + 1) * P], cs[:, k, :],
                              start=k == 0 and j == 0, stop=k == 7, skip_group_check=True)
                last.then_inc(S["piece_used"], 1)
            pe.wait_ge(S["xn_ok"], TT)
            pe.wait_ge(S["fspec_out"], 9)
            pe.wait_ge(S["filt_pair"], TT)
            for k in range(KD):
                if k >= 4:
                    pe.wait_ge(S["hT_ok"], k - 3)
                for t in range(TT):
                    last = tr(bank[2 + k % 4][:, t * P:(t + 1) * P], xn[:, t, k * P:(k + 1) * P], ident)
                last.then_inc(S["hT_mm"], 1)
            pe.wait_ge(S["cn_ok"], CT)
            for k in range(KD):
                if k >= 2:
                    pe.wait_ge(S["hcT_ok"], k - 1)
                for t in range(CT):
                    last = tr(bank[6 + k % 2][:, t * P:(t + 1) * P], cn[:, t, k * P:(k + 1) * P], ident)
                last.then_inc(S["hcT_mm"], 1)
            pe.wait_ge(S["hT_ok"], KD)
            pe.wait_ge(S["hcT_ok"], KD)
            pe.wait_ge(S["moda_out"], 1)
            pe.wait_ge(S["nsum_out"], 1)
            for n, (i, kind, c) in enumerate(UNITS):
                if n >= 4:
                    pe.wait_ge(S["unit_out"], n - 3)
                if n == 0 or UNITS[n - 1][0] != i:
                    piece_ready(pe, "W", i)
                w = piece("W", i).rearrange("p (k n) -> p k n", k=KD)
                for k in range(KD):
                    a, z0 = k == 0, k == KD - 1
                    if kind == "u":
                        last = mm(bank[n % 4][:, :], w[:, k, c * P:(c + 1) * P], hT[:, k, :], start=a, stop=z0)
                    elif kind == "q":
                        last = mm(bank[n % 4][:, 0:256], hT[:, k, c * P:(c + 1) * P], w[:, k, :], start=a, stop=z0)
                    else:
                        last = mm(bank[n % 4][:, 0:256], hcT[:, k, c * P:(c + 1) * P], w[:, k, :], start=a, stop=z0)
                last.then_inc(S["unit_mm"], 1)
            for t in range(TT):
                if t == 0:
                    pe.wait_ge(S["z_ok"], HC)
                for c in range(HC):
                    last = tr(bank[4 + t][:, c * P:(c + 1) * P], z[:, c, t * P:(t + 1) * P], ident)
                last.then_inc(S["zT_mm"], 1)
            pe.wait_ge(S["zT_ok"], TT)
            pe.wait_ge(S["unit_out"], len(UNITS))
            for f in range(8):
                if f >= 4:
                    pe.wait_ge(S["uspec_out"], f - 3)
                for t in range(TT):
                    last = mm(bank[f % 4][:, :], dft[:, t, f * P:(f + 1) * P], ztok[:, t, :], start=t == 0, stop=t == TT - 1)
                last.then_inc(S["uspec_mm"], 1)
            pe.wait_ge(S["crep_ok"], 1)
            pe.wait_ge(S["uspec_out"], 8)
            for i in range(16):
                k, h = i // 2, i % 2
                piece_ready(pe, "B", i)
                w = piece("B", i)
                rows_at, cols_at = (0, 1024) if h == 0 else (1024, 0)
                for n in range(2):
                    mm(bank[2 * h + n][:, :], crep[:, k, :], w[:, rows_at + n * 512:rows_at + (n + 1) * 512],
                       start=k == 0, stop=k == 7)
                for j in range(8):
                    q = h * 8 + j
                    last = mm(bank[4][:, 2 * q:2 * q + 2], w[:, cols_at + j * P:cols_at + (j + 1) * P], cs[:, k, :],
                              start=i == 0 and j == 0, stop=k == 7, skip_group_check=True)
                last.then_inc(S["piece_used"], 1)
            pe.wait_ge(S["yspec"], 4)
            pe.wait_ge(S["idft_in"], 16)
            for c in range(HC):
                if c >= 2:
                    pe.wait_ge(S["y_ok"], c - 1)
                for f in range(8):
                    last = mm(bank[5 + c % 2][:, :], uspec[:, f, c * P:(c + 1) * P], idft[:, f, :], start=f == 0, stop=f == 7)
                last.then_inc(S["inv_mm"], 1)
            pe.wait_ge(S["ysq"], HC)
            for c in range(HC):
                last = mm(bank[7][:, :], ones[:, :], ztok[:, c, :], start=c == 0, stop=c == HC - 1)
            last.then_inc(S["ysum_mm"], 1)
            pe.wait_ge(S["qk_ok"], 1)
            pe.wait_ge(S["modb_out"], 1)
            n = 0
            for j in range(8):
                if j >= 4:
                    pe.wait_ge(S["qkT_ok"], j - 3)
                dst = bank[j % 4]
                if j < 4:
                    for t in range(TT):
                        last = tr(dst[:, t * P:(t + 1) * P], qkv[:, t, j * P:(j + 1) * P], ident)
                else:
                    kv, part = (j - 4) // 2, (j - 4) % 2
                    for t in range(TT if part == 0 else CT):
                        last = tr(dst[:, t * P:(t + 1) * P], kd[:, t + TT * part, kv].rearrange("p r d -> p (r d)"), ident)
                last.then_inc(S["qkT_mm"], 1)
            pe.wait_ge(S["qkT_ok"], 8)
            pe.wait_ge(S["y_ok"], HC)
            pe.wait_ge(S["ysum_out"], 1)

            def scores(u):
                qb, h = ATT[u]
                lo, hi = local_keys(qb)
                r = 64 * (h % 2)
                if u >= 2:
                    pe.wait_ge(S["p_ok"], u - 1)
                q = qT[r:r + 64, h // 2, qb * P:(qb + 1) * P]
                mm(bank[2 * (u % 2)][:, 0:hi - lo], q, kT[r:r + 64, h // 4, lo:hi], start=True, stop=True)
                mm(bank[2 * (u % 2) + 1][:, 0:LC], q, kT[r:r + 64, h // 4, L:L + LC], start=True, stop=True)\
                    .then_inc(S["s_mm"], 1)

            def weights_T(u):
                qb, h = ATT[u]
                lo, hi = local_keys(qb)
                pe.wait_ge(S["p_ok"], u + 1)
                if u >= 1:
                    pe.wait_ge(S["pT_ok"], u)
                for j in range((hi - lo + LC) // P):
                    dst = bank[4][:, j * P:(j + 1) * P] if j < 4 else bank[5][:, 0:P]
                    last = tr(dst, pbuf(u)[:, j * P:(j + 1) * P], ident)
                last.then_inc(S["pT_mm"], 1)

            def values(u):
                qb, h = ATT[u]
                lo, hi = local_keys(qb)
                pe.wait_ge(S["pT_ok"], u + 1)
                if h == 0 and qb >= 2:
                    pe.wait_ge(S["a_ok"], qb - 1)
                n = (hi - lo) // P
                kv = h // 4
                for j in range(n + CT):
                    v = (qkv[:, lo // P + j, AW + KVW + kv * HD:AW + KVW + (kv + 1) * HD] if j < n
                         else kvc[:, j - n, KVW + kv * HD:KVW + (kv + 1) * HD])
                    last = mm(bank[6 + qb % 2][:, h * HD:(h + 1) * HD], ptbuf(u)[:, j * P:(j + 1) * P], v,
                              start=j == 0, stop=j == n + CT - 1)
                last.then_inc(S["pv_mm"], 1)

            scores(0)
            for u in range(len(ATT)):
                if u + 1 < len(ATT):
                    scores(u + 1)
                weights_T(u)
                if u >= 1:
                    values(u - 1)
            values(len(ATT) - 1)
            pe.wait_ge(S["a_mul"], TT)
            for j in range(4):
                for t in range(TT):
                    last = tr(bank[j][:, t * P:(t + 1) * P], qkv[:, t, j * P:(j + 1) * P], ident)
                last.then_inc(S["aT_mm"], 1)
            pe.wait_ge(S["aT_ok"], 4)
            pe.wait_ge(S["yT_ok"], HC)
            for i in range(4):
                piece_ready(pe, "O", i)
            for t in range(TT):
                if t >= 2:
                    pe.wait_ge(S["xnew"], t - 1)
                for n in range(2):
                    for c in range(8):
                        w = piece("O", c // 2)[:, (c % 2) * D + n * 512:(c % 2) * D + (n + 1) * 512]
                        src = aT[:, c, t * P:(t + 1) * P] if c < 4 else v2[:, c - 4, t * P:(t + 1) * P]
                        last = mm(bank[4 + 2 * (t % 2) + n][:, :], src, w, start=c == 0, stop=c == 7)
                last.then_inc(S["wo_mm"], 1)
            pe.wait_ge(S["hn_ok"], TT)
            for k in range(KD):
                if k >= 4:
                    pe.wait_ge(S["h2T_ok"], k - 3)
                for t in range(TT):
                    last = tr(bank[k % 4][:, t * P:(t + 1) * P], hn[:, t, k * P:(k + 1) * P], ident)
                last.then_inc(S["h2T_mm"], 1)
            pe.wait_ge(S["h2T_ok"], KD)
            pe.wait_ge(S["late_in"], 48)
            for t in range(TT):
                for k in range(KD):
                    last = mm(bank[4][:, t * NE:(t + 1) * NE], hT[:, k, t * P:(t + 1) * P], wr[:, k, :], start=k == 0, stop=k == KD - 1)
            last.then_inc(S["lg_mm"], 1)
            pe.wait_ge(S["onehot"], 1)
            for t in range(TT):
                last = mm(bank[5][0:NE, 0:1], R.M[:, t, :], ones[:, 0:1], start=t == 0, stop=t == TT - 1)
            last.then_inc(S["cntc_mm"], 1)
            for t in range(TT):
                for s in range(t + 1):
                    last = mm(bank[6][:, t * NE:(t + 1) * NE], ones[:, :] if s < t else konst[:, K_TRI:K_TRI + P],
                              R.M[:, s, :], start=s == 0, stop=s == t)
            last.then_inc(S["pos_mm"], 1)
            pe.wait_ge(S["nbrep"], 1)
            mm(bank[7][:, 0:2 * NE], R.nbrep, konst[0:NE, K_TRE:K_TRE + 2 * NE], start=True, stop=True).then_inc(S["bs_mm"], 1)
            pe.wait_ge(S["gmat"], 1)
            for t in range(TT):
                last = tr(bank[0][0:NE, t * P:(t + 1) * P], R.G[:, t, :], ident)
            last.then_inc(S["gT_mm"], 1)
            pe.wait_ge(S["onehot"], 2)
            for i in range(TT * TOPK):
                last = mm(bank[5][:, 0:2 * BW], R.S1[:, i, :], R.B2[:, i, :], start=i == 0, stop=i == TT * TOPK - 1)
            last.then_inc(S["tab_mm"], 1)
            pe.wait_ge(S["gT_ok"], 1)
            for t in range(TT):
                if t >= 1:
                    pe.wait_ge(S["acc_ok"], t)
                for n in range(2):
                    last = mm(bank[1 + n][:, :], R.GT[:, t * P:(t + 1) * P], R.bd[:, n * 512:(n + 1) * 512], start=True, stop=True)
                last.then_inc(S["bd_mm"], 1)
            pe.wait_ge(S["acc_ok"], TT)
            pe.wait_ge(S["tables"], 2)
            pe.sem_inc(S["free_ring"], RING - 2)

            def slots_T():
                for k in range(KD):
                    last = tr(bank[6 + k // 4][:, (k % 4) * P:(k % 4 + 1) * P], xs[:, k * P:(k + 1) * P], ident)
                last.then_inc(S["xsT_mm"], 1)

            pe.wait_ge(S["gathered"], 16)
            slots_T()
            nblk = pe.value_load(blk[0:1, BW:BW + 1], min_val=1, max_val=BLOCKS)
            with pe.Fori(0, BLOCKS) as b:
                with pe.If(b < nblk):
                    pe.wait_ge(S["xsT_ok"], 2 * b + 2)
                    for k in range(KD):
                        pe.wait_ge(full[k], 16 * b + 16)
                        for i in range(4):
                            if k == 0:
                                pe.wait_ge(S["gate_ready"], 4 * b + i + 1)
                            for q in range(4):
                                f = (q % 2) * FF + (2 * i + q // 2) * P
                                last = mm(bank[i][:, q * P:(q + 1) * P], ring[:, k, f:f + P], xsT[:, k, :],
                                          start=k == 0 and q == 0, stop=k == KD - 1, skip_group_check=True)
                            if k == KD - 1:
                                last.then_inc(S["gu_mm"], 1)
                        if k < KD - 1:
                            last.then_inc(S["free_ring"], 1)
                    pe.wait_ge(S["gathered"], 16 * b + 32)
                    slots_T()
                    pe.wait_ge(S["y_out"], b)
                    for s in range(4):
                        pe.wait_ge(S["h_ok"], 4 * b + s + 1)
                        pe.wait_ge(full[KD + s], 16 * b + 16)
                        for c in range(2):
                            for n in range(2):
                                last = mm(bank[4 + n][:, :], gh[:, 2 * s + c, :],
                                          ring[:, KD + s, c * D + n * 512:c * D + (n + 1) * 512],
                                          start=s + c == 0, stop=s + c == 4)
                        last.then_inc(S["free_ring" if s < 3 else "down_mm"], 1)

        @block.vector
        def _(v):
            dve = nc.vector
            steps = [0]

            def link(ins):
                steps[0] += 1
                ins.then_inc(S["chain_v"], 1)
                v.wait_ge(S["chain_v"], steps[0])

            v.wait_ge(S["filter_in"], 80)
            for i in range(3):
                v.wait_ge(S["fnet_mm"], i + 1)
                a, n = ftmp
                link(dve.tensor_scalar(a, bank[0][0:64, :], fcol[:, i:i + 1], fcol[:, 3:4], ALU.add, ALU.mult))
                link(dve.tensor_scalar(n, a, 1.0 / (TWO_PI_HI + TWO_PI_LO), ROUND, ALU.mult, ALU.add))
                link(dve.tensor_scalar(n, n, -ROUND, None, ALU.add))
                link(dve.scalar_tensor_tensor(a, n, -TWO_PI_HI, a, ALU.mult, ALU.add))
                link(dve.scalar_tensor_tensor(a, n, -TWO_PI_LO, a, ALU.mult, ALU.add))
                dve.tensor_scalar(a, a, PI_BOUND, -PI_BOUND, ALU.min, ALU.max).then_inc(S["fnet_lin"], 1)
            v.wait_ge(S["small_in"], 64)
            v.wait_ge(S["silu_s"], 1)
            dve.tensor_tensor(cs[:, :, :], cc[:, :, :], cs[:, :, :], ALU.mult).then_inc(S["silu"], 1)
            v.wait_ge(S["xs_sq"], 1)
            dve.tensor_scalar(st[:, 0:6], st[:, 0:6], 1.0 / D, EPS, ALU.mult, ALU.add).then_inc(S["x_lin"], 1)
            v.wait_ge(S["decay_in"], 16)
            for t in range(TT):
                v.wait_ge(S["filt_mm"], t + 1)
                dve.tensor_tensor(fpair[:, 0], bank[1 + 2 * (t % 2)][:, :], decay[:, t], ALU.mult)
                dve.tensor_tensor(fpair[:, 1], bank[2 + 2 * (t % 2)][:, :], decay[:, t], ALU.mult).then_inc(S["filt_pair"], 1)
                v.wait_ge(S["filt_pair"], t + 1)
                if t == 0:
                    link(dve.memset(fpair[0:1, 1, :], 0.0))
                link(dve.tensor_tensor(fa[:, t], fpair[:, 0], fpair[:, 1], ALU.add))
                dve.tensor_tensor(fb[:, t], fpair[:, 0], fpair[:, 1], ALU.subtract).then_inc(S["filt_tile"], 1)
                v.wait_ge(S["filt_tile"], t + 1)
            v.wait_ge(S["x_sqrt"], 1)
            link(dve.reciprocal(st[:, 8:14], st[:, 0:6]))
            for t in range(TT):
                dve.tensor_scalar(xn[:, t], xt[:, t], st[:, 8 + t:9 + t], None, ALU.mult).then_inc(S["xn_ok"], 1)
            for t in range(CT):
                dve.tensor_scalar(cn[:, t], ctxt[:, t], st[:, 12 + t:13 + t], None, ALU.mult).then_inc(S["cn_ok"], 1)
            v.wait_ge(S["nsum_mm"], 1)
            dve.tensor_scalar(st[:, 16:20], bank[1][:, 0:HC], 0.5, EPS, ALU.mult, ALU.add).then_inc(S["ns_lin"], 1)
            v.wait_ge(S["ns_sqrt"], 1)
            dve.reciprocal(st[:, 20:24], st[:, 16:20]).then_inc(S["nsum_out"], 1)
            v.wait_ge(S["piece_used"], 8)
            link(dve.tensor_tensor(modc[:, 0:16, :], bank[0][:, 0:32].rearrange("p (j m) -> p j m", m=2),
                                   cols[:, C_BMOD:C_BMOD + 16].unsqueeze(2).to_broadcast([P, 16, 2]), ALU.add))
            link(dve.tensor_scalar(modc[:, 8:16, :], modc[:, 8:16, :], 1.0, None, ALU.add))
            dve.tensor_tensor(modc[:, 8:16, :], modc[:, 8:16, :],
                              cols[:, C_N1:C_N1 + 8].unsqueeze(2).to_broadcast([P, 8, 2]), ALU.mult).then_inc(S["moda_out"], 1)
            v.wait_ge(S["moda_out"], 1)
            for k in range(KD):
                v.wait_ge(S["hT_mm"], k + 1)
                dve.tensor_scalar(hT[:, k, :], bank[2 + k % 4][:, :], modc[:, 8 + k, 0:1], modc[:, k, 0:1],
                                  ALU.mult, ALU.add).then_inc(S["hT_ok"], 1)
            dve.tensor_copy(crep, cs[:, :, 0:1].to_broadcast([P, KD, P])).then_inc(S["crep_ok"], 1)
            uflat = uT[:, :, :, :].rearrange("p a c n -> p (a c) n")
            for n in range(3 * HC):
                v.wait_ge(S["unit_mm"], n + 1)
                src, dst = bank[n % 4], uflat[:, n]
                tap = [cols[:, C_CW + 12 * i + n:C_CW + 12 * i + n + 1] for i in range(3)]
                link(dve.tensor_scalar(dst, src[:, :], tap[1], cols[:, C_CB + n:C_CB + n + 1], ALU.mult, ALU.add))
                link(dve.scalar_tensor_tensor(dst[:, 1:L], src[:, 0:L - 1], tap[0], dst[:, 1:L], ALU.mult, ALU.add))
                dve.scalar_tensor_tensor(dst[:, 0:L - 1], src[:, 1:L], tap[2], dst[:, 0:L - 1], ALU.mult, ALU.add)\
                   .then_inc(S["unit_out"], 1)
                v.wait_ge(S["unit_out"], n + 1)
            for c in range(HC):
                dve.tensor_tensor(z[:, c], z[:, c], v2[:, c], ALU.mult).then_inc(S["z_ok"], 1)
            v.wait_ge(S["fspec_out"], 9)
            t1, t2, keep = work[:, 0:512], work[:, 512:1024], work[0:1, 1024:1536]
            for f in range(4):
                v.wait_ge(S["uspec_out"], f + 5)
                ur, ui, kr, ki = uspec[:, f], uspec[:, 4 + f], kspec[:, f], kspec[:, 4 + f]
                dve.tensor_tensor(t1, ui, ki, ALU.mult)
                link(dve.tensor_tensor(t2, ur, ki, ALU.mult))
                if f == 0:
                    link(dve.tensor_copy(keep, t1[0:1, :]))
                    link(dve.memset(t1[0:1, :], 0.0))
                dve.tensor_tensor(ur, ur, kr, ALU.mult)
                link(dve.tensor_tensor(ui, ui, kr, ALU.mult))
                dve.tensor_tensor(ur, ur, t1, ALU.subtract)
                if f == 0:
                    link(dve.tensor_tensor(ui, ui, t2, ALU.add))
                    dve.tensor_copy(ui[0:1, :], keep).then_inc(S["yspec"], 1)
                else:
                    dve.tensor_tensor(ui, ui, t2, ALU.add).then_inc(S["yspec"], 1)
                v.wait_ge(S["yspec"], f + 1)
            v.wait_ge(S["unit_out"], len(UNITS))
            qk = qkv[:, :, 0:AW + KVW]
            qk4 = qk.rearrange("p t (h d) -> p t h d", d=HD)
            kc = kvc[:, :, 0:KVW]
            kc4 = kc.rearrange("p t (h d) -> p t h d", d=HD)
            kc_sq = rot[1][:, 0:CT, 0:KVW]
            dve.tensor_tensor(rot[0], qk, qk, ALU.mult)
            link(dve.tensor_tensor(kc_sq, kc, kc, ALU.mult))
            dve.tensor_reduce(st[:, 32:72].rearrange("p (t h) -> p t h", t=TT), rot[0].rearrange("p t (h d) -> p t h d", d=HD), X, ALU.add)
            link(dve.tensor_reduce(st[:, 72:76].rearrange("p (t h) -> p t h", t=CT), kc_sq.rearrange("p t (h d) -> p t h d", d=HD), X, ALU.add))
            dve.tensor_scalar(st[:, 32:76], st[:, 32:76], 1.0 / HD, EPS, ALU.mult, ALU.add).then_inc(S["qk_lin"], 1)
            v.wait_ge(S["qk_sqrt"], 1)
            link(dve.reciprocal(st[:, 80:124], st[:, 32:76]))
            dve.tensor_tensor(qk4, qk4, st[:, 80:120].rearrange("p (t h) -> p t h", t=TT).unsqueeze(3).to_broadcast([P, TT, NQ + NKV, HD]), ALU.mult)
            link(dve.tensor_tensor(kc4, kc4, st[:, 120:124].rearrange("p (t h) -> p t h", t=CT).unsqueeze(3).to_broadcast([P, CT, NKV, HD]), ALU.mult))

            def gain(at, t, h):
                return rows[:, at:at + HD].unsqueeze(1).unsqueeze(1).to_broadcast([P, t, h, HD])

            dve.tensor_tensor(qk4[:, :, 0:NQ], qk4[:, :, 0:NQ], gain(R_QN, TT, NQ), ALU.mult)
            dve.tensor_tensor(qk4[:, :, NQ:], qk4[:, :, NQ:], gain(R_KN, TT, NKV), ALU.mult)
            link(dve.tensor_tensor(kc4, kc4, gain(R_KN, CT, NKV), ALU.mult))
            pairs = qk.rearrange("p t (g j i) -> p t g j i", j=2, i=HD // 4)
            swapped = rot[0].rearrange("p t (g j i) -> p t g j i", j=2, i=HD // 4)
            dve.tensor_copy(swapped[:, :, :, 0], pairs[:, :, :, 1])
            link(dve.tensor_copy(swapped[:, :, :, 1], pairs[:, :, :, 0]))

            def turn(at):
                return konst[:, at:at + TT * HD].rearrange("p (t d) -> p t d", t=TT).unsqueeze(2).to_broadcast([P, TT, NQ + NKV, HD])

            rot4 = [r.rearrange("p t (h d) -> p t h d", d=HD) for r in rot]
            dve.tensor_tensor(rot4[0], rot4[0], turn(K_RS), ALU.mult)
            link(dve.tensor_tensor(rot4[1], qk4, turn(K_RC), ALU.mult))
            link(dve.tensor_tensor(qk4, rot4[0], rot4[1], ALU.add))
            for r in range(2):
                dve.tensor_copy(kd[:, 0:TT, :, r], qk4[:, :, NQ:])
                last = dve.tensor_copy(kd[:, TT:, :, r], kc4)
            last.then_inc(S["qk_ok"], 1)
            v.wait_ge(S["piece_used"], 24)
            v.wait_ge(S["brow_in"], 16)
            for h in range(2):
                for n in range(2):
                    g = gB[:, h, n * 512:(n + 1) * 512]
                    dve.tensor_tensor(g, g, bank[2 * h + n][:, :], ALU.add)
            link(dve.tensor_tensor(modc[:, 16:32, :], bank[4][:, 0:32].rearrange("p (j m) -> p j m", m=2),
                                   cols[:, C_BMOD + 24:C_BMOD + 40].unsqueeze(2).to_broadcast([P, 16, 2]), ALU.add))
            link(dve.tensor_scalar(modc[:, 24:32, :], modc[:, 24:32, :], 1.0, None, ALU.add))
            dve.tensor_tensor(modc[:, 24:32, :], modc[:, 24:32, :],
                              cols[:, C_N2:C_N2 + 8].unsqueeze(2).to_broadcast([P, 8, 2]), ALU.mult).then_inc(S["modb_out"], 1)
            for c in range(HC):
                link(dve.tensor_scalar(z[:, c], z[:, c], cols[:, C_FB + c:C_FB + c + 1], None, ALU.mult))
                v.wait_ge(S["inv_mm"], c + 1)
                dve.scalar_tensor_tensor(v2[:, c], bank[5 + c % 2][:, :], st[:, 20 + c:21 + c], z[:, c], ALU.mult, ALU.add).then_inc(S["y_ok"], 1)
                v.wait_ge(S["y_ok"], c + 1)
                dve.tensor_tensor(v2[:, c], v2[:, c], x0[:, c], ALU.mult).then_inc(S["y_mul"], 1)
            yr = half[:, 0:512]
            v.wait_ge(S["ysum_mm"], 1)
            dve.tensor_scalar(yr, bank[7][:, :], 1.0 / HW, EPS, ALU.mult, ALU.add).then_inc(S["ysum_out"], 1)
            v.wait_ge(S["yr_sqrt"], 1)
            link(dve.reciprocal(yr, yr))
            for c in range(HC):
                dve.scalar_tensor_tensor(v2[:, c], v2[:, c], cols[:, C_HG + c:C_HG + c + 1], yr, ALU.mult, ALU.mult).then_inc(S["yT_ok"], 1)
            sink8 = st[:, 124:132]
            link(dve.tensor_scalar(sink8, rows[:, R_SINK:R_SINK + NQ], 1.0 / ATTN_SCALE, None, ALU.mult))
            top, top2, neg, lsink = att_m, att_m2, att_neg, att_l

            def maxima(u):
                qb, h = ATT[u]
                lo, hi = local_keys(qb)
                v.wait_ge(S["s_mm"], u + 1)
                if u >= 2:
                    v.wait_ge(S["pT_mm"], u - 1)
                m0 = K_MASK + (P if qb == 0 else 0)
                dve.tensor_tensor_reduce(out=pbuf(u)[:, 0:hi - lo], in0=bank[2 * (u % 2)][:, 0:hi - lo],
                                         in1=konst[:, m0:m0 + hi - lo], scale=1.0, scalar=sink8[:, h:h + 1],
                                         op0=ALU.add, op1=ALU.max, accum_out=top[:, u:u + 1])
                link(dve.tensor_reduce(top2[:, u:u + 1], bank[2 * (u % 2) + 1][:, 0:LC], X, ALU.max))
                dve.tensor_scalar(neg[:, u:u + 1], top[:, u:u + 1], top2[:, u:u + 1], -ATTN_SCALE, ALU.max, ALU.mult)\
                   .then_inc(S["s_max"], 1)

            def copy_T(u):
                qb, h = ATT[u]
                lo, hi = local_keys(qb)
                v.wait_ge(S["pT_mm"], u + 1)
                if u >= 2:
                    v.wait_ge(S["pv_mm"], u - 1)
                n = (hi - lo + LC) // P
                last = dve.tensor_copy(ptbuf(u)[:, 0:4 * P], bank[4][:, 0:4 * P])
                if n > 4:
                    last = dve.tensor_copy(ptbuf(u)[:, 4 * P:5 * P], bank[5][:, 0:P])
                last.then_inc(S["pT_ok"], 1)

            def finish(qb):
                r = slice(NQ * qb, NQ * qb + NQ)
                v.wait_ge(S["s_max"], NQ * qb + NQ)
                dve.scalar_tensor_tensor(lsink[:, 2, r], sink8, ATTN_SCALE, neg[:, r], ALU.mult, ALU.add).then_inc(S["l_sink"], 1)
                v.wait_ge(S["l_exp"], qb + 1)
                link(dve.tensor_tensor(lsink[:, 0, r], lsink[:, 0, r], lsink[:, 1, r], ALU.add))
                link(dve.tensor_tensor(lsink[:, 0, r], lsink[:, 0, r], lsink[:, 2, r], ALU.add))
                link(dve.reciprocal(lsink[:, 0, r], lsink[:, 0, r]))
                v.wait_ge(S["pv_mm"], NQ * qb + NQ)
                dve.tensor_tensor(qkv[:, qb, 0:AW].rearrange("p (h d) -> p h d", h=NQ),
                                  bank[6 + qb % 2][:, :].rearrange("p (h d) -> p h d", h=NQ),
                                  lsink[:, 0, r].unsqueeze(2).to_broadcast([P, NQ, HD]), ALU.mult).then_inc(S["a_ok"], 1)
                v.wait_ge(S["a_ok"], qb + 1)
                link(dve.tensor_tensor_reduce(out=z[:, 0], in0=qkv[:, qb, 0:AW], in1=qkv[:, qb, 0:AW], scale=1.0, scalar=0.0,
                                              op0=ALU.mult, op1=ALU.add, accum_out=st[:, 24 + qb:25 + qb]))

            for u in range(len(ATT)):
                maxima(u)
                if u >= 1:
                    copy_T(u - 1)
                if u >= NQ and u % NQ == 0:
                    finish(u // NQ - 1)
            copy_T(len(ATT) - 1)
            finish(TT - 1)
            dve.tensor_scalar(st[:, 24:28], st[:, 24:28], 1.0 / AW, EPS, ALU.mult, ALU.add).then_inc(S["a_lin"], 1)
            v.wait_ge(S["a_sqrt"], 1)
            link(dve.reciprocal(st[:, 28:32], st[:, 24:28]))
            for t in range(TT):
                dve.tensor_scalar(qkv[:, t, 0:AW], qkv[:, t, 0:AW], st[:, 28 + t:29 + t], None, ALU.mult).then_inc(S["a_mul"], 1)
            for t in range(TT):
                v.wait_ge(S["wo_mm"], t + 1)
                for n in range(2):
                    last = dve.tensor_tensor(wtmp[:, n], bank[4 + 2 * (t % 2) + n][:, :], gB[:, 0, n * 512:(n + 1) * 512], ALU.mult)
                link(last)
                dve.tensor_tensor(xt[:, t], xt[:, t], wtmp.rearrange("p a n -> p (a n)"), ALU.add).then_inc(S["xnew"], 1)
                v.wait_ge(S["xnew"], t + 1)
            v.wait_ge(S["n2_sq"], 1)
            dve.tensor_scalar(st[:, 0:4], st[:, 0:4], 1.0 / D, EPS, ALU.mult, ALU.add).then_inc(S["n2_lin"], 1)
            v.wait_ge(S["n2_sqrt"], 1)
            link(dve.reciprocal(st[:, 8:12], st[:, 0:4]))
            for t in range(TT):
                dve.tensor_scalar(hn[:, t], xt[:, t], st[:, 8 + t:9 + t], None, ALU.mult).then_inc(S["hn_ok"], 1)
            for k in range(KD):
                v.wait_ge(S["h2T_mm"], k + 1)
                dve.tensor_scalar(hT[:, k, :], bank[k % 4][:, :], modc[:, 24 + k, 0:1], modc[:, 16 + k, 0:1],
                                  ALU.mult, ALU.add).then_inc(S["h2T_ok"], 1)
            v.wait_ge(S["lg_mm"], 1)
            link(dve.tensor_tensor(R.lg, bank[4][:, 0:TT * NE].rearrange("p (t e) -> p t e", t=TT),
                                   rows[:, R_BR:R_BR + NE].unsqueeze(1).to_broadcast([P, TT, NE]), ALU.add))
            for t in range(TT):
                last = dve.max(R.v8[:, t], R.lg[:, t])
            link(last)
            for t in range(TT):
                last = dve.max_index(R.i8[:, t], R.v8[:, t], R.lg[:, t])
            link(last)
            dve.tensor_tensor(R.ex, R.v8[:, :, 0:TOPK], R.v8[:, :, 0:1].to_broadcast([P, TT, TOPK]), ALU.subtract).then_inc(S["route_shift"], 1)
            link(dve.tensor_copy(R.i8f, R.i8))
            link(dve.tensor_tensor(R.OH, R.i8f[:, :, 0:TOPK].unsqueeze(3).to_broadcast([P, TT, TOPK, NE]),
                                   konst[:, K_SLOT:K_SLOT + NE].unsqueeze(1).unsqueeze(1).to_broadcast([P, TT, TOPK, NE]), ALU.is_equal))
            dve.tensor_reduce(R.M, R.OH.rearrange("p t k e -> p t e k"), X, ALU.add).then_inc(S["onehot"], 1)
            v.wait_ge(S["cntc_mm"], 1)
            link(dve.tensor_tensor(R.nb4, bank[5][0:NE, 0:1].to_broadcast([NE, 4]), konst[0:NE, K_JN:K_JN + 4], ALU.is_gt))
            link(dve.tensor_reduce(R.nb, R.nb4, X, ALU.add))
            dve.tensor_copy(R.nbrep, R.nb.to_broadcast([NE, P])).then_inc(S["nbrep"], 1)
            v.wait_ge(S["route_exp"], 1)
            link(dve.tensor_reduce(R.sums[:, 0:4], R.ex, X, ALU.add))
            link(dve.reciprocal(R.sums[:, 4:8], R.sums[:, 0:4]))
            link(dve.tensor_tensor(R.gate, R.ex, R.sums[:, 4:8].unsqueeze(2).to_broadcast([P, TT, TOPK]), ALU.mult))
            link(dve.tensor_tensor(R.OHS, R.OH, R.gate.unsqueeze(3).to_broadcast([P, TT, TOPK, NE]), ALU.mult))
            dve.tensor_reduce(R.G, R.OHS.rearrange("p t k e -> p t e k"), X, ALU.add).then_inc(S["gmat"], 1)
            v.wait_ge(S["gmat"], 1)
            v.wait_ge(S["bs_mm"], 1)
            link(dve.tensor_copy(R.bs, bank[7][:, 0:2 * NE]))
            link(dve.scalar_tensor_tensor(R.slot_of, R.bs[:, 0:NE].unsqueeze(1).to_broadcast([P, TT, NE]), float(SLOTS),
                                          bank[6][:, 0:TT * NE].rearrange("p (t e) -> p t e", t=TT), ALU.mult, ALU.add))
            link(dve.tensor_tensor(R.OHS, R.OH, R.slot_of.unsqueeze(2).to_broadcast([P, TT, TOPK, NE]), ALU.mult))
            link(dve.tensor_reduce(R.slot, R.OHS.rearrange("p t k e -> p (t k) e"), X, ALU.add))
            link(dve.tensor_tensor(R.GE, R.slot.unsqueeze(2).to_broadcast([P, 16, BW + 1]),
                                   konst[:, K_BN:K_BN + BW + 1].unsqueeze(1).to_broadcast([P, 16, BW + 1]), ALU.is_ge))
            link(dve.tensor_reduce(R.within, R.GE, X, ALU.add))
            link(dve.tensor_scalar(R.within, R.within, -float(SLOTS), float(SLOTS), ALU.mult, ALU.add))
            link(dve.tensor_tensor(R.within, R.within, R.slot, ALU.add))
            link(dve.tensor_tensor(R.S1, R.within.unsqueeze(2).to_broadcast([P, 16, SLOTS]),
                                   konst[:, K_SLOT:K_SLOT + SLOTS].unsqueeze(1).to_broadcast([P, 16, SLOTS]), ALU.is_equal))
            link(dve.tensor_tensor(R.B2[:, :, 0:BW], R.GE[:, :, 0:BW], R.GE[:, :, 1:BW + 1], ALU.subtract))
            link(dve.tensor_tensor(R.B2[:, :, BW:2 * BW], R.B2[:, :, 0:BW],
                                   R.gate.rearrange("p t k -> p (t k)").unsqueeze(2).to_broadcast([P, 16, BW]), ALU.mult))
            B4 = R.B2[:, :, 0:BW].rearrange("p (t k) b -> p t k b", t=TT)
            dve.tensor_tensor(B4, B4, konst[:, K_VAL:K_VAL + TT].unsqueeze(2).unsqueeze(3).to_broadcast([P, TT, TOPK, BW]),
                              ALU.mult).then_inc(S["onehot"], 1)
            link(dve.tensor_tensor(R.blkcmp, R.bs[0:1, NE:2 * NE].unsqueeze(1).to_broadcast([1, BW, NE]),
                                   konst[0:1, K_SLOT:K_SLOT + BW].unsqueeze(2).to_broadcast([1, BW, NE]), ALU.is_le))
            link(dve.tensor_reduce(R.blkf[:, 0:BW], R.blkcmp, X, ALU.add))
            link(dve.tensor_scalar(R.blkf[:, 0:BW], R.blkf[:, 0:BW], float(NE - 1), None, ALU.min))
            dve.tensor_copy(blk[:, 0:BW], R.blkf[:, 0:BW])
            dve.tensor_copy(blk[:, BW:BW + 1], R.bs[0:1, 2 * NE - 1:2 * NE]).then_inc(S["tables"], 1)
            v.wait_ge(S["tab_mm"], 1)
            link(dve.tensor_scalar(R.tok, bank[5][:, 0:BW], float(2 * L), None, ALU.add))
            dve.tensor_scalar(idx[:, 0], R.tok, float(L - 1), None, ALU.min)
            dve.tensor_scalar(idx[:, 1], R.tok, konst[:, K_ROW:K_ROW + 1], None, ALU.min)
            dve.tensor_copy(tabs[:, :], bank[5][:, BW:2 * BW]).then_inc(S["tables"], 1)
            v.wait_ge(S["gT_mm"], 1)
            dve.tensor_copy(R.GT, bank[0][0:NE, :]).then_inc(S["gT_ok"], 1)
            for t in range(TT):
                v.wait_ge(S["bd_mm"], t + 1)
                for n in range(2):
                    last = dve.tensor_tensor(wtmp[:, n], bank[1 + n][:, :], gB[:, 1, n * 512:(n + 1) * 512], ALU.mult)
                link(last)
                dve.tensor_tensor(xt[:, t], xt[:, t], wtmp.rearrange("p a n -> p (a n)"), ALU.add).then_inc(S["acc_ok"], 1)
                v.wait_ge(S["acc_ok"], t + 1)

            v.sem_inc(S["gate_ready"], 4)
            v.wait_ge(S["tables"], 2)
            nblk = v.value_load(blk[0:1, BW:BW + 1], min_val=1, max_val=BLOCKS)
            base = steps[0]
            PER = 14
            with v.Fori(0, BLOCKS) as b:
                with v.If(b < nblk):
                    n = [0]

                    def step(ins):
                        n[0] += 1
                        ins.then_inc(S["chain_v"], 1)
                        v.wait_ge(S["chain_v"], b * PER + (base + n[0]))

                    e = v.value_load(blk[0:1, bass.ds(b, 1)], min_val=0, max_val=NE - 1)
                    dve.tensor_copy(gcur, tabs[:, bass.ds(b, 1)])
                    step(dve.tensor_copy(bcur, bgu[:, bass.ds(e, 1), :].rearrange("p o j -> p (o j)")))

                    def bounds(i):
                        s = gu[:, i % 2]
                        v.wait_ge(S["gu_mm"], 4 * b + i + 1)
                        if i >= 2:
                            v.wait_ge(S["h_ok"], 4 * b + i - 1)
                        dve.tensor_tensor(s, bank[i][:, :].rearrange("p (q s) -> p q s", q=4),
                                          bcur[:, 4 * i:4 * i + 4].unsqueeze(2).to_broadcast([P, 4, SLOTS]), ALU.add)\
                           .then_inc(S["gate_ready"], 1)
                        v.wait_ge(S["gate_ready"], 4 * b + i + 5)
                        g = s.rearrange("p (c r) s -> p c r s", r=2)
                        dve.tensor_scalar(g[:, :, 0], g[:, :, 0], LIMIT, None, ALU.min).then_inc(S["glu_p"], 1)
                        step(dve.tensor_scalar(g[:, :, 1], g[:, :, 1], LIMIT, -LIMIT, ALU.min, ALU.max))

                    def gates(i):
                        g = gu[:, i % 2].rearrange("p (c r) s -> p c r s", r=2)
                        v.wait_ge(S["sig"], 4 * b + i + 1)
                        step(dve.tensor_tensor(g[:, :, 0], g[:, :, 0], sg[:, i % 2], ALU.mult))
                        dve.scalar_tensor_tensor(gh[:, 2 * i:2 * i + 2, :], g[:, :, 1], 1.0, g[:, :, 0], ALU.add, ALU.mult)\
                           .then_inc(S["h_ok"], 1)

                    for i in range(4):
                        bounds(i)
                        if i >= 1:
                            gates(i - 1)
                    gates(3)
                    v.wait_ge(S["down_mm"], b + 1)
                    v.wait_ge(S["scattered"], 16 * b)
                    dve.scalar_tensor_tensor(yb[:, 0:512], bank[4][:, :], gcur, gB[:, 1, 0:512], ALU.mult, ALU.mult)
                    dve.scalar_tensor_tensor(yb[:, 512:D], bank[5][:, :], gcur, gB[:, 1, 512:D], ALU.mult, ALU.mult)\
                       .then_inc(S["y_out"], 1)
                    v.wait_ge(S["y_out"], b + 1)
                    for _ in range(PER - n[0]):
                        v.sem_inc(S["chain_v"], 1)

        @block.scalar
        def _(act):
            f = nc.scalar.activation
            steps = [0]

            def link(ins):
                steps[0] += 1
                ins.then_inc(S["chain_a"], 1)
                act.wait_ge(S["chain_a"], steps[0])

            act.dma_start(zin, t_z).then_inc(S["filter_in"], 16)
            act.dma_start(w1, t_w1).then_inc(S["filter_in"], 16)
            act.dma_start(w23, t_w23).then_inc(S["filter_in"], 16)
            act.dma_start(fcol, t_fcol).then_inc(S["filter_in"], 16)
            act.dma_start(w4, t_w4).then_inc(S["filter_in"], 16)
            act.dma_start(konst[:, :], t_konst).then_inc(S["small_in"], 16)
            act.dma_start(cc[:, :, :], t_cc).then_inc(S["small_in"], 16)
            act.dma_start(cols[:, :], t_cols).then_inc(S["small_in"], 16)
            act.dma_start(rows[:, :], t_rows.to_broadcast([P, NR])).then_inc(S["small_in"], 16)
            act.dma_start(ctxt[:, :, :], t_ctx.rearrange("(t p) d -> p t d", p=P)).then_inc(S["ctx_in"], 16)
            act.wait_ge(S["small_in"], 64)
            f(cs[:, :, :], cc[:, :, :], ACT.Sigmoid).then_inc(S["silu_s"], 1)
            for i in range(3):
                act.wait_ge(S["fnet_lin"], i + 1)
                f(fh[i % 2], ftmp[0], ACT.Sin).then_inc(S["fnet_sin"], 1)
            act.wait_ge(S["x_in"], 16)
            act.wait_ge(S["ctx_in"], 16)
            for t in range(TT + CT):
                src = xt[:, t] if t < TT else ctxt[:, t - TT]
                last = f(square, src, ACT.Square, accum_out=st[:, t:t + 1])
                if t < TT + CT - 1:
                    link(last)
            last.then_inc(S["xs_sq"], 1)
            act.wait_ge(S["x_lin"], 1)
            f(st[:, 0:6], st[:, 0:6], ACT.Sqrt).then_inc(S["x_sqrt"], 1)
            for n in range(9):
                act.wait_ge(S["fspec_mm"], n + 1)
                if n < 8:
                    f(kspec[:, n], bank[5 + n % 3][:, :], ACT.Copy).then_inc(S["fspec_out"], 1)
                else:
                    act.wait_ge(S["fspec_out"], 8)
                    f(kspec[0:1, 4], bank[5 + n % 3][0:1, :], ACT.Copy).then_inc(S["fspec_out"], 1)
            act.wait_ge(S["ns_lin"], 1)
            f(st[:, 16:20], st[:, 16:20], ACT.Sqrt).then_inc(S["ns_sqrt"], 1)
            act.wait_ge(S["moda_out"], 1)
            for k in range(KD):
                act.wait_ge(S["hcT_mm"], k + 1)
                f(hcT[:, k, :], bank[6 + k % 2][:, 0:LC], ACT.Identity, bias=modc[:, k, 1:2], scale=modc[:, 8 + k, 1:2])\
                    .then_inc(S["hcT_ok"], 1)
            act.wait_ge(S["unit_out"], 3 * HC)
            for n in range(3 * HC, len(UNITS)):
                i, kind, t = UNITS[n]
                act.wait_ge(S["unit_mm"], n + 1)
                dst = kvc[:, t] if kind == "c" else qkv[:, t, i * 256:(i + 1) * 256]
                f(dst, bank[n % 4][:, 0:256], ACT.Copy).then_inc(S["unit_out"], 1)
            for t in range(TT):
                act.wait_ge(S["zT_mm"], t + 1)
                f(ztok[:, t], bank[4 + t][:, :], ACT.Copy).then_inc(S["zT_ok"], 1)
            for n in range(8):
                act.wait_ge(S["uspec_mm"], n + 1)
                f(uspec[:, n], bank[n % 4][:, :], ACT.Copy).then_inc(S["uspec_out"], 1)
            act.wait_ge(S["qk_lin"], 1)
            f(st[:, 32:76], st[:, 32:76], ACT.Sqrt).then_inc(S["qk_sqrt"], 1)
            for c in range(HC):
                act.wait_ge(S["y_mul"], c + 1)
                f(ztok[:, c], v2[:, c], ACT.Square).then_inc(S["ysq"], 1)
            act.wait_ge(S["ysum_out"], 1)
            f(half[:, 0:512], half[:, 0:512], ACT.Sqrt).then_inc(S["yr_sqrt"], 1)
            for j in range(8):
                act.wait_ge(S["qkT_mm"], j + 1)
                if j < 4:
                    dst, n = qT[:, j], L
                else:
                    kv, part = (j - 4) // 2, (j - 4) % 2
                    dst, n = (kT[:, kv, 0:L], L) if part == 0 else (kT[:, kv, L:L + LC], LC)
                f(dst, bank[j % 4][:, 0:n], ACT.Copy).then_inc(S["qkT_ok"], 1)

            def sink_exp(qb):
                r = slice(NQ * qb, NQ * qb + NQ)
                act.wait_ge(S["l_sink"], qb + 1)
                f(att_l[:, 2, r], att_l[:, 2, r], ACT.Exp).then_inc(S["l_exp"], 1)

            for u in range(len(ATT)):
                qb, h = ATT[u]
                lo, hi = local_keys(qb)
                w = hi - lo
                act.wait_ge(S["s_max"], u + 1)
                f(pbuf(u)[:, 0:w], pbuf(u)[:, 0:w], ACT.Exp, bias=att_neg[:, u:u + 1], scale=ATTN_SCALE, accum_out=att_l[:, 0, u:u + 1])
                f(pbuf(u)[:, w:w + LC], bank[2 * (u % 2) + 1][:, 0:LC], ACT.Exp, bias=att_neg[:, u:u + 1], scale=ATTN_SCALE,
                  accum_out=att_l[:, 1, u:u + 1]).then_inc(S["p_ok"], 1)
                if u >= NQ and u % NQ == 0:
                    sink_exp(u // NQ - 1)
            sink_exp(TT - 1)
            act.wait_ge(S["a_lin"], 1)
            f(st[:, 24:28], st[:, 24:28], ACT.Sqrt).then_inc(S["a_sqrt"], 1)
            for j in range(4):
                act.wait_ge(S["aT_mm"], j + 1)
                f(aT[:, j], bank[j][:, :], ACT.Copy, scale=cols[:, C_AG + j:C_AG + j + 1]).then_inc(S["aT_ok"], 1)
            for t in range(TT):
                act.wait_ge(S["xnew"], t + 1)
                last = f(slab[:, 0:D], xt[:, t], ACT.Square, accum_out=st[:, t:t + 1])
                if t < TT - 1:
                    link(last)
            last.then_inc(S["n2_sq"], 1)
            act.wait_ge(S["n2_lin"], 1)
            f(st[:, 0:4], st[:, 0:4], ACT.Sqrt).then_inc(S["n2_sqrt"], 1)
            for t in range(TT):
                act.wait_ge(S["hn_ok"], t + 1)
                act.dma_start(d_hn[t * P:(t + 1) * P, :], hn[:, t]).then_inc(S["hn_stored"], 16)
            act.wait_ge(S["route_shift"], 1)
            f(R.ex, R.ex, ACT.Exp).then_inc(S["route_exp"], 1)
            for t in range(TT):
                act.wait_ge(S["acc_ok"], t + 1)
                act.dma_start(d_acc[t * P:(t + 1) * P, :], xt[:, t]).then_inc(S["acc_in"], 16)
            act.dma_start(d_acc[L:L + SLOTS, :], xt[:, 0]).then_inc(S["acc_in"], 16)

            def modulate(at):
                act.wait_ge(S["xsT_mm"], at)
                for k in range(KD):
                    last = f(xsT[:, k], bank[6 + k // 4][:, (k % 4) * P:(k % 4 + 1) * P], ACT.Identity,
                             bias=modc[:, 16 + k, 0:1], scale=modc[:, 24 + k, 0:1])
                    if k % 4 == 3:
                        last.then_inc(S["xsT_ok"], 1)

            modulate(1)
            act.wait_ge(S["tables"], 2)
            nblk = act.value_load(blk[0:1, BW:BW + 1], min_val=1, max_val=BLOCKS)
            with act.Fori(0, BLOCKS) as b:
                with act.If(b < nblk):
                    for i in range(4):
                        g = gu[:, i % 2].rearrange("p (c r) s -> p c r s", r=2)
                        act.wait_ge(S["glu_p"], 4 * b + i + 1)
                        f(sg[:, i % 2], g[:, :, 0], ACT.Sigmoid, scale=ALPHA).then_inc(S["sig"], 1)
                    modulate(b + 2)
            act.wait_ge(S["scattered"], 16)

        @block.gpsimd
        def _(pool):
            nc.gpsimd.memset(ones[:, :], 1.0).then_inc(S["ones_ok"], 1)
            for t in range(TT):
                pool.wait_ge(S["filt_tile"], t + 1)
                nc.gpsimd.tensor_tensor(sq[:, t], fa[:, t], fa[:, t], ALU.mult).then_inc(S["filt_sq"], 1)
                nc.gpsimd.tensor_tensor(sq[:, TT + t], fb[:, t], fb[:, t], ALU.mult).then_inc(S["filt_sq"], 1)

            def gather():
                pool.indirect_dma_start(out=xs, out_offset=None, in_=d_hn,
                                        in_offset=bass.IndirectOffsetOnAxis(ap=icur[:, 0:1].bitcast(u32), axis=0)).then_inc(S["gathered"], 16)

            pool.wait_ge(S["tables"], 2)
            pool.wait_ge(S["hn_stored"], 16 * TT)
            pool.wait_ge(S["wo_mm"], TT)
            nc.gpsimd.tensor_copy(icur[:, 0:1], idx[:, 0, 0:1]).then_inc(S["chain_p"], 1)
            pool.wait_ge(S["chain_p"], 1)
            gather()
            pool.wait_ge(S["acc_in"], 16 * (TT + 1))
            nblk = pool.value_load(blk[0:1, BW:BW + 1], min_val=1, max_val=BLOCKS)
            with pool.Fori(0, BLOCKS) as b:
                with pool.If(b < nblk):
                    pool.wait_ge(S["xsT_mm"], b + 1)
                    pool.sem_inc(S["pool_step"], 1)
                    nc.gpsimd.tensor_copy(icur[:, 0:1], idx[:, 0, bass.ds(b + 1, 1)]).then_inc(S["chain_p"], 1)
                    pool.wait_ge(S["chain_p"], 2 * b + 2)
                    pool.sem_inc(S["pool_step"], 1)
                    gather()
                    pool.wait_ge(S["scattered"], 16 * b)
                    pool.sem_inc(S["pool_step"], 1)
                    nc.gpsimd.tensor_copy(icur[:, 1:2], idx[:, 1, bass.ds(b, 1)]).then_inc(S["chain_p"], 1)
                    pool.wait_ge(S["chain_p"], 2 * b + 3)
                    pool.wait_ge(S["y_out"], b + 1)
                    pool.sem_inc(S["pool_step"], 1)
                    pool.indirect_dma_start(out=d_acc, out_offset=bass.IndirectOffsetOnAxis(ap=icur[:, 1:2].bitcast(u32), axis=0),
                                            in_=yb, in_offset=None, compute_op=ALU.add).then_inc(S["scattered"], 16)
            pool.wait_ge(S["scattered"], nblk * 16)
            pool.sem_inc(S["pool_step"], 1)
            pool.dma_start(t_out, d_acc[0:L, :]).then_inc(S["out_done"], 16)
            pool.wait_ge(S["out_done"], 16)


def _constants():
    import numpy as np
    f32 = np.float32
    n = 2 * L
    t = np.arange(L)
    ang = 2.0 * np.pi * ((t[:, None] * np.arange(L)[None, :]) % n) / n
    nyq = np.where(t % 2 == 0, 1.0, -1.0)
    cos, sin = np.cos(ang), -np.sin(ang)
    sin[:, 0] = nyq
    dft = np.concatenate([cos, sin], axis=1)
    scale = np.full((n, 1), 2.0 / n)
    scale[0] = scale[L] = 1.0 / n
    idft = dft.T * scale
    konst = np.zeros((P, NK), f32)
    i = np.arange(P)
    konst[:, K_ID:K_ID + P] = np.eye(P)
    konst[:, K_TRI:K_TRI + P] = i[:, None] < i[None, :]
    konst[:, K_MASK:K_MASK + P] = np.where(i[None, :] >= i[:, None], 0.0, -1e30)
    konst[:, K_MASK + 2 * P:K_MASK + 3 * P] = np.where(i[None, :] <= i[:, None], 0.0, -1e30)
    nf = HD // 4
    inv = (f32(10000.0) ** (-np.arange(nf, dtype=f32) / f32(nf))).astype(f32)
    for tile in range(TT):
        pos = tile * P + i
        for j, p in enumerate((pos // 64, pos % 64)):
            a = (p[:, None].astype(f32) * inv[None, :]).astype(f32)
            at = tile * HD + j * 2 * nf
            for r in range(2):
                konst[:, K_RC + at + r * nf:K_RC + at + (r + 1) * nf] = np.cos(a)
                konst[:, K_RS + at + r * nf:K_RS + at + (r + 1) * nf] = (-1.0, 1.0)[r] * np.sin(a)
    konst[:, K_SLOT:K_SLOT + SLOTS] = np.arange(SLOTS)
    konst[:, K_BN:K_BN + 64] = SLOTS * np.arange(64)
    konst[:, K_VAL:K_VAL + TT] = np.arange(TT)[None, :] * P + i[:, None] - 2 * L
    konst[:, K_ROW] = L + i
    e = np.arange(NE)
    konst[0:NE, K_TRE:K_TRE + NE] = e[:, None] < e[None, :]
    konst[0:NE, K_TRE + NE:K_TRE + 2 * NE] = e[:, None] <= e[None, :]
    konst[:, K_JN:K_JN + 4] = SLOTS * np.arange(4)
    tl = np.linspace(0.0, 1.0, L, dtype=f32)[:, None]
    w = (f32(2.0 * np.pi) * np.arange(L, dtype=f32)[:, None] / f32(L)).astype(f32)
    bands = np.linspace(1e-4, 15, 16, dtype=f32)[None, :]
    zf = np.concatenate([tl, np.cos(bands * w), -np.sin(bands * w)], axis=1).astype(f32)
    lo, hi = -np.log(1e-2) / 1.5, -np.log(1e-2) / 0.3
    deltas = np.linspace(lo, hi, HW, dtype=f32)
    decay = np.exp(-tl * deltas[None, :]).astype(f32)
    return konst, zf.T.copy(), decay, dft.astype(f32), idft.astype(f32)


def kernel(**inputs):
    import numpy as np
    import concourse.bacc as bacc
    from concourse.bass_utils import run_bass_kernel_spmd

    g = {k: np.asarray(v) for k, v in inputs.items()}
    konst, zf, decay, dft, idft = _constants()

    def columns(a):
        return a.reshape(-1, P).T

    cols = np.concatenate([columns(g[k]) for k in ("b_mod", "norm1", "norm2", "conv_w", "conv_b", "filt_bias",
                                                    "attn_out_norm", "hyena_out_norm")], axis=1)
    rows = np.concatenate([g[k].reshape(1, -1) for k in ("q_norm", "k_norm", "sink", "b_router")], axis=1)
    cc = np.stack([g["c"].reshape(KD, P), g["c_ctx"].reshape(KD, P)], axis=-1).transpose(1, 0, 2)
    bgu = g["b_gu"].reshape(NE, 2, KF, P).transpose(3, 0, 2, 1).reshape(P, NE, 2 * KF)
    arrays = {
        "x": g["x"].reshape(L, D), "ctx": g["ctx"].reshape(LC, D), "cc": cc, "cols": cols, "rows": rows,
        "konst": konst, "z": zf, "w1": g["filt_w1"][0], "w23": np.stack([g["filt_w2"][0], g["filt_w3"][0]], axis=1),
        "fcol": np.stack([g[k][0] for k in ("filt_b1", "filt_b2", "filt_b3", "filt_freq")], axis=1),
        "w4": g["filt_w4"][0], "decay": decay, "dft": dft, "idft": idft, "wmod": g["w_mod"][0],
        "brows": np.concatenate([g["b_mod"][:, 2 * D:3 * D], g["b_mod"][:, 5 * D:6 * D]], axis=1),
        "win": g["w_in"][0], "wout": g["w_out"][0], "wr": g["w_router"][0], "bgu": bgu,
        "wgu": g["w_gu"].reshape(NE * KD, P, 2 * FF), "wdown": g["w_down"].reshape(NE * 4, 2, P, D),
        "bdown": g["b_down"][0],
    }
    nc = bacc.Bacc("TRN2", target_bir_lowering=False, num_devices=1)
    arrays = {f"in_{k}": np.ascontiguousarray(a) for k, a in arrays.items()}
    args = [nc.dram_tensor(k, a.shape, mybir.dt.from_np(a.dtype), kind="ExternalInput").ap() for k, a in arrays.items()]
    args.append(nc.dram_tensor("out", (L, D), mybir.dt.float32, kind="ExternalOutput").ap())
    layer_kernel(nc, *args)
    r = run_bass_kernel_spmd(nc, [arrays], core_ids=[0])
    return r.results[0]["out"].reshape(1, L, D)
```

```python
from contextlib import ExitStack

import concourse.bass as bass
from concourse import mybir

P = 128
D = 1024
L = 512
LC = 256
TT = L // P
CT = LC // P
KD = D // P
HD = 64
NQ = 8
NKV = 2
AW = NQ * HD
KVW = NKV * HD
HW = D - AW
HC = HW // P
QKV = AW + 2 * KVW
NE = 32
TOPK = 4
FF = 1024
KF = FF // P
SLOTS = P
BLOCKS = (L * TOPK + NE * (SLOTS - 1)) // SLOTS
BW = BLOCKS + 1
EPS = 1e-6
ATTN_SCALE = HD ** -0.5
LIMIT = 7.0
ALPHA = 1.702
HALF = SLOTS // 2
PIECE = 2048
RING = 12
FRONT_RING = 4
TWO_PI_HI = 6.28125
TWO_PI_LO = 6.283185307179586 - TWO_PI_HI
ROUND = 12582912.0
PI_BOUND = 3.1415925

C_BMOD, C_N1, C_N2, C_CW, C_CB, C_FB, C_AG, C_HG = 0, 48, 56, 64, 100, 112, 116, 120
NCOLS = 124
K_ID, K_TRI, K_MASK, K_RC, K_RS = 0, 128, 256, 640, 896
K_SLOT, K_BN, K_VAL, K_ROW, K_TRE, K_JN, K_Q4 = 1152, 1280, 1344, 1348, 1349, 1413, 1417
NK = 1418
R_QN, R_KN, R_SINK, R_BR = 0, 64, 128, 136
NR = 168


def layer_kernel(nc, t_x, t_ctx, t_cc, t_cols, t_rows, t_konst, t_z, t_w1, t_w23, t_fcol, t_w4,
                 t_decay, t_dft, t_idft, t_wmod, t_brows, t_win, t_wout, t_wr, t_bgu, t_wgu,
                 t_wdown, t_bdown, t_out):
    f32, i32, u32 = mybir.dt.float32, mybir.dt.int32, mybir.dt.uint32
    ALU = mybir.AluOpType
    ACT = mybir.ActivationFunctionType
    X = mybir.AxisListType.X

    d_hn = nc.dram_tensor("normed_rows", [L, D], f32, kind="Internal").ap()
    d_acc = nc.dram_tensor("sums", [L + SLOTS, D], f32, kind="Internal").ap()

    with ExitStack() as ctx:
        def sb(name, shape, dt=f32):
            return ctx.enter_context(nc.sbuf_tensor(name, shape, dt))

        def sem(name):
            return ctx.enter_context(nc.semaphore(name))

        ring = sb("ring", [P, RING, PIECE])
        xt = sb("xt", [P, TT, D])
        big = sb("big", [P, 4096])
        half = sb("half", [P, 2048])
        uT = sb("uT", [P, 3, HC, L])
        qkv = sb("qkv", [P, TT, QKV])
        kvc = sb("kvc", [P, CT, 2 * KVW])
        kT = sb("kT", [P, NKV, L + LC])
        work = sb("work", [P, 2560])
        gB = sb("gB", [P, 2, D])
        cols = sb("cols", [P, NCOLS])
        rows = sb("rows", [P, NR])
        konst = sb("konst", [P, NK])
        ones = sb("ones", [P, P])
        cc = sb("cc", [P, KD, 2])
        sig_c = sb("sig_c", [P, KD, 2])
        modc = sb("modc", [P, 32, 2])
        st = sb("st", [P, 192])
        tabs = sb("tabs", [P, BW])
        idx = sb("idx", [P, 2, BW], i32)
        blk = sb("blk", [1, BW + NE], i32)
        more = sb("more", [P, BW], i32)
        icur = sb("icur", [P, 2], i32)
        att_m = tabs[:, 0:32]
        att_m2 = st[:, 132:164]
        att_neg = sb("att_neg", [P, 32])
        att_l = idx[:, :, :].rearrange("p a b -> p (a b)")[:, 0:96].bitcast(f32).rearrange("p (a b) -> p a b", a=3)

        ident = konst[:, K_ID:K_ID + P]
        slab = ring[:, 4:6, :].rearrange("p a n -> p (a n)")
        dft = ring[:, 6:8, :].rearrange("p a n -> p (a n)").rearrange("p (t f) -> p t f", t=TT)
        idft = ring[:, 8:10, :].rearrange("p a n -> p (a n)").rearrange("p (f t) -> p f t", f=8)
        kspec = ring[:, 10:12, :].rearrange("p a n -> p (a n)").rearrange("p (f c) -> p f c", f=8)
        xn = ring[:, 8:10, :].rearrange("p a n -> p (a n)").rearrange("p (t d) -> p t d", t=TT)
        hT = big[:, :].rearrange("p (k t) -> p k t", k=KD)
        uspec = big[:, :].rearrange("p (f c) -> p f c", f=8)
        sq = big[:, :].rearrange("p (f c) -> p f c", f=8)
        hcT = half[:, :].rearrange("p (k t) -> p k t", k=KD)
        ztok = half[:, :].rearrange("p (t c) -> p t c", t=TT)
        decay, fa, fb = uT[:, 0], uT[:, 1], uT[:, 2]
        x0, z, v2 = uT[:, 0], uT[:, 1], uT[:, 2]
        cn = qkv[:, :, :].rearrange("p t n -> p (t n)")[:, 0:CT * D].rearrange("p (t d) -> p t d", t=CT)
        qT = slab[:, 0:2048].rearrange("p (j t) -> p j t", j=4)
        aT = slab[:, 2048:4096].rearrange("p (j t) -> p j t", j=4)
        w4 = work[0:64, 0:1024]
        zin = work[0:33, 1024:1536]
        fh = [work[0:64, 1536:2048], work[0:64, 2048:2560]]
        w1 = slab[0:33, 2048:2112]
        w23 = slab[0:64, 2112:2240].rearrange("p (a n) -> p a n", a=2)
        fcol = slab[0:64, 2240:2244]
        ftmp = [slab[0:64, 1024:1536], slab[0:64, 1536:2048]]
        fpair = slab[:, 0:1024].rearrange("p (a n) -> p a n", a=2)
        square = slab[:, 3072:4096]
        rot = [work[:, :].rearrange("p (t n) -> p t n", t=TT), slab[:, 0:2560].rearrange("p (t n) -> p t n", t=TT)]
        kd = slab[:, 2560:4096].rearrange("p (t k r d) -> p t k r d", t=TT + CT, k=NKV, r=2)
        ctxt = gB
        cs = slab[:, 2816:3072].rearrange("p (k m) -> p k m", k=KD)
        nrow = slab[:, 1024:1536]
        mrow_a = slab[:, 2304:2816]
        kflat = kT[:, :, :].rearrange("p a n -> p (a n)")
        sel = kflat[:, 0:512].rearrange("p (j m) -> p j m", j=4)
        mrow_b = [kflat[:, 512:1024], kflat[:, 1024:1536]]
        kz = [kT, half[:, 512:2048].rearrange("p (a n) -> p a n", a=NKV)]
        hn = xn
        bgu = work[:, 0:NE * 2 * KF].rearrange("p (e j) -> p e j", e=NE)
        wr = work[:, 512:768].rearrange("p (k e) -> p k e", k=KD)
        wtmp = work[:, 1024:2048].rearrange("p (a n) -> p a n", a=2)
        moe = uT[:, :, :, :].rearrange("p a c n -> p (a c n)")
        xs = moe[:, 0:D]
        xsT = moe[:, 1024:2048].rearrange("p (k s) -> p k s", k=KD)
        gh = moe[:, 2048:3072].rearrange("p (k s) -> p k s", k=KF)
        yb = moe[:, 3072:4096]
        gu = moe[:, 4096:5120].rearrange("p (a q s) -> p a q s", a=2, q=4)
        sg = moe[:, 5120:5632].rearrange("p (a q s) -> p a q s", a=2, q=2)
        gusb = qkv[:, :, :].rearrange("p t n -> p (t n)")[:, 0:1024].rearrange("p (g n) -> p g n", g=2)
        bcur = moe[:, 5632:5648]
        gcur = moe[:, 5648:5649]
        gcur2 = moe[:, 5649:5650]

        def pbuf(u):
            return big[:, 2560 + (u % 2) * 641:2560 + (u % 2 + 1) * 641]

        pt = [big[:, 0:2560].rearrange("p (j n) -> p j n", j=5), work[:, :].rearrange("p (j n) -> p j n", j=5)]
        asq = big[:, 0:2048].rearrange("p (j t) -> p j t", j=4)
        ar = big[:, 2048:2560]

        class R:
            a = ring[:, 6:8, :].rearrange("p a n -> p (a n)")
            b = ring[:, 10:12, :].rearrange("p a n -> p (a n)")
            lg = a[:, 0:128].rearrange("p (t e) -> p t e", t=TT)
            v8 = a[:, 128:160].rearrange("p (t e) -> p t e", t=TT)
            i8 = a[:, 160:192].bitcast(u32).rearrange("p (t e) -> p t e", t=TT)
            i8f = a[:, 192:224].rearrange("p (t e) -> p t e", t=TT)
            ex = a[:, 224:240].rearrange("p (t k) -> p t k", t=TT)
            gate = a[:, 240:256].rearrange("p (t k) -> p t k", t=TT)
            OH = a[:, 256:768].rearrange("p (t k e) -> p t k e", t=TT, k=TOPK)
            M = a[:, 768:896].rearrange("p (t e) -> p t e", t=TT)
            G = a[:, 896:1024].rearrange("p (t e) -> p t e", t=TT)
            OHS = a[:, 1024:1536].rearrange("p (t k e) -> p t k e", t=TT, k=TOPK)
            slot_of = a[:, 1536:1664].rearrange("p (t e) -> p t e", t=TT)
            slot = a[:, 1664:1680]
            GE = a[:, 1680:1680 + 16 * (BW + 1)].rearrange("p (i b) -> p i b", i=16)
            bs = a[:, 2480:2544]
            nb4 = a[0:NE, 2560:2564]
            nb = a[0:NE, 2564:2565]
            within = a[:, 2576:2592]
            GT = a[0:NE, 2592:3104]
            sums = a[:, 3104:3120]
            tok = a[:, 3120:3120 + BW]
            S1 = b[:, 0:2048].rearrange("p (i s) -> p i s", i=16)
            B2 = b[:, 2048:2048 + 16 * 2 * BW].rearrange("p (i b) -> p i b", i=16)
            nbrep = b[0:NE, 3600:3728]
            bd = half[0:NE, 0:D]
            blkcmp = qkv[0:1, :, :].rearrange("p t n -> p (t n)")[:, 0:BW * NE].rearrange("p (b e) -> p b e", b=BW)
            blkf = a[0:1, 3200:3200 + BW + 1]


        bank = [ctx.enter_context(nc.psum_tensor(f"bank{i}", [P, 512], f32)) for i in range(8)]

        names = """x_in small_in filter_in ctx_in dft_in idft_in decay_in xn_free
            chain_v chain_a chain_p
            ones_ok silu fnet_mm fnet_lin fnet_sin filt_mm filt_pair filt_tile filt_sq fspec_mm
            fspec_out nsum_mm nsum_out moda_mm moda_out stat_x xn_ok cn_ok hT_mm hT_ok hcT_mm hcT_ok
            piece_used unit_mm unit_out modb_mm modb_out crep_ok
            z_ok zT_mm zT_ok uspec_mm uspec_out yspec inv_mm y_ok ysq ysum_mm ysum_out yT_ok
            qk_ok kd_ok qkT_mm qkT_ok s_mm s_max p_ok pT_mm pT_ok pv_mm l_sink a_ok a_mul aT_mm aT_ok
            wo_mm xnew stat2 hn_ok hn_stored h2T_mm h2T_ok lg_mm route_exp route_shift cntc_mm nbrep
            bs_mm pos_mm onehot tab_mm gmat gT_mm gT_ok bd_mm acc_ok acc_in tables
            free_ring gathered xs_used xsT_mm xsT_ok gu_mm sig gate_ready h_ok down_mm y_out scattered
            out_done nrow_ok mrow_ok mcol_mm sel_ok kz_ok p_exp rl_ok asum_mm asum_out ar_sqrt asq qk_factor dve_step glu_p gu_sb gu_T late_in brow_in xs_sq y_mul yr_lin yr_sqrt ns_lin ns_sqrt x_lin x_sqrt silu_s
            qk_lin qk_sqrt s_local l_exp a_lin a_sqrt n2_sq n2_lin n2_sqrt gexp_in pool_step cs_ok""".split()
        S = {n: sem(n) for n in names}
        stream = [sem(f"stream{i}") for i in range(FRONT_RING)]
        full = [sem(f"full{i}") for i in range(RING)]

        block = ctx.enter_context(nc.Block())

        WS = (3, 4, 5, 6, 7, 8, 0, 1, 2)
        ORDER = [("A", k) for k in range(8)]
        for n, i in enumerate(WS):
            ORDER += [("W", i)] + ([("B", 2 * n), ("B", 2 * n + 1)] if n < 8 else [])
        ORDER += [("O", i) for i in range(4)]
        AT = {w: n for n, w in enumerate(ORDER)}

        def piece_src(what, i):
            if what == "A":
                return t_wmod[i * P:(i + 1) * P, 0:2048]
            if what == "W":
                return t_win.rearrange("(k p) n -> p k n", p=P)[:, :, i * 256:(i + 1) * 256]
            if what == "B":
                k, h = i // 2, i % 2
                return t_wmod[k * P:(k + 1) * P, 2048 + h * 2048:4096 + h * 2048]
            return t_wout[i * 256:(i + 1) * 256, :].rearrange("(c p) n -> p c n", p=P)

        def piece(what, i):
            return ring[:, AT[what, i] % FRONT_RING, :]

        def piece_ready(eng, what, i):
            n = AT[what, i]
            eng.wait_ge(stream[n % FRONT_RING], 16 * (n // FRONT_RING + 1))

        UNITS = ([(i, "u", c) for i in (3, 4, 5, 6, 7, 8) for c in range(2)]
                 + [(i, "q", t) for i in (0, 1) for t in range(TT)]
                 + [(2, "q", t) for t in range(TT)] + [(2, "c", t) for t in range(CT)])
        def used(what, i):
            if what == "W":
                return S["unit_mm"], 1 + max(n for n, u in enumerate(UNITS) if u[0] == i)
            return S["piece_used"], i + 1 + (8 if what == "B" else 0)

        ATT = [(qb, h) for qb in range(TT) for h in range(NQ)]

        def local_keys(qb):
            return max(0, qb - 1) * P, min(TT, qb + 2) * P

        @block.sync
        def _(sp):
            sp.dma_start(xt[:, :, :], t_x.rearrange("(t p) d -> p t d", p=P)).then_inc(S["x_in"], 16)
            sp.dma_start(dft[:, :, :], t_dft.rearrange("(t p) f -> p t f", p=P)).then_inc(S["dft_in"], 16)
            sp.dma_start(decay, t_decay.rearrange("(t p) c -> p t c", p=P)).then_inc(S["decay_in"], 16)
            for n, w in enumerate(ORDER):
                if n >= FRONT_RING:
                    sp.wait_ge(*used(*ORDER[n - FRONT_RING]))
                dst = ring[:, n % FRONT_RING, :]
                if w[0] == "W":
                    dst = dst.rearrange("p (k n) -> p k n", k=KD)
                if w[0] == "O":
                    dst = dst.rearrange("p (c n) -> p c n", c=2)
                sp.dma_start(dst, piece_src(*w)).then_inc(stream[n % FRONT_RING], 16)
                if w == ("W", 8):
                    sp.wait_ge(S["cn_ok"], CT)
                    sp.dma_start(gB[:, :, :].rearrange("p a n -> p (a n)"), t_brows.to_broadcast([P, 2 * D])).then_inc(S["brow_in"], 16)
                    sp.wait_ge(S["hT_mm"], KD)
                    sp.dma_start(idft[:, :, :], t_idft.rearrange("(f p) t -> p f t", p=P)).then_inc(S["idft_in"], 16)
            sp.wait_ge(S["a_ok"], TT)
            sp.dma_start(bgu, t_bgu).then_inc(S["late_in"], 16)
            sp.dma_start(wr, t_wr.rearrange("(k p) e -> p k e", p=P)).then_inc(S["late_in"], 16)
            sp.wait_ge(S["yT_ok"], HC)
            sp.dma_start(R.bd, t_bdown).then_inc(S["late_in"], 16)

            def load(e, s):
                if s < KD:
                    src = t_wgu[bass.ds(e * KD + s, 1), :, :].rearrange("o p n -> (o p) n")
                    sp.dma_start(ring[:, s, :], src).then_inc(full[s], 16)
                else:
                    src = t_wdown[bass.ds(e * 4 + s - KD, 1), :, :, :].rearrange("o c p n -> p (o c) n")
                    sp.dma_start(ring[:, s, :].rearrange("p (c n) -> p c n", c=2), src).then_inc(full[s], 16)

            sp.wait_ge(S["wo_mm"], TT)
            sp.wait_ge(S["n2_sq"], 1)
            for s in range(6):
                load(0, s)
            sp.wait_ge(S["hn_stored"], 16 * TT)
            sp.wait_ge(S["h2T_mm"], KD)
            for s in (8, 9):
                load(0, s)
            sp.wait_ge(S["bd_mm"], TT)
            sp.wait_ge(S["tables"], 2)
            for s in (6, 7, 10, 11):
                load(0, s)
            with sp.Fori(1, NE) as e:
                prev = sp.value_load(blk[0:1, bass.ds(e + (BW - 1), 1)], min_val=0, max_val=BLOCKS - 1)
                for s in range(RING):
                    if s == KD - 1:
                        sp.wait_ge(S["gu_mm"], prev * 4 + 4)
                    elif s == RING - 1:
                        sp.wait_ge(S["down_mm"], prev + 1)
                    else:
                        sp.wait_ge(S["free_ring"], prev * (RING - 2) + (s + 1 if s < KD else s))
                    load(e, s)

        @block.tensor
        def _(pe):
            mm, tr = nc.tensor.matmul, nc.tensor.transpose
            pe.wait_ge(S["filter_in"], 80)
            mm(bank[0][0:64, :], w1, zin, start=True, stop=True).then_inc(S["fnet_mm"], 1)
            for i in range(2):
                pe.wait_ge(S["fnet_sin"], i + 1)
                mm(bank[0][0:64, :], w23[:, i, :], fh[i], start=True, stop=True).then_inc(S["fnet_mm"], 1)
            pe.wait_ge(S["fnet_sin"], 3)
            for t in range(TT):
                if t >= 2:
                    pe.wait_ge(S["filt_pair"], t - 1)
                for h in range(2):
                    last = mm(bank[1 + 2 * (t % 2) + h][:, :], fh[0][:, t * P:(t + 1) * P],
                              w4[:, h * HW:(h + 1) * HW], start=True, stop=True)
                last.then_inc(S["filt_mm"], 1)
            pe.wait_ge(S["filt_tile"], TT)
            pe.wait_ge(S["dft_in"], 16)
            for f in range(9):
                src = fa if f < 4 or f == 8 else fb
                if f >= 3:
                    pe.wait_ge(S["fspec_out"], f - 2)
                dst = bank[5 + f % 3]
                for t in range(TT):
                    if f < 8:
                        last = mm(dst[:, :], dft[:, t, f * P:(f + 1) * P], src[:, t, :], start=t == 0, stop=t == TT - 1)
                    else:
                        last = mm(dst[0:1, :], dft[:, t, L:L + 1], src[:, t, :], start=t == 0, stop=t == TT - 1)
                last.then_inc(S["fspec_mm"], 1)
            pe.wait_ge(S["filt_sq"], 2 * TT)
            pe.wait_ge(S["ones_ok"], 1)
            for n in range(2 * TT):
                g = 32 * (n % 4)
                last = mm(bank[1][g:g + 32, :], ones[:, 0:32], sq[:, n, :], start=n < 4, stop=n >= 4)
            last.then_inc(S["nsum_mm"], 1)
            pe.wait_ge(S["silu"], 1)
            for k in range(8):
                piece_ready(pe, "A", k)
                for j in range(4):
                    last = mm(bank[0][32 * j:32 * j + 32, :], cs[:, k, :], piece("A", k)[:, j * 512:(j + 1) * 512],
                              start=k == 0, stop=k == 7)
                last.then_inc(S["piece_used"], 1)
            pe.wait_ge(S["nrow_ok"], 1)
            for c in range(HC):
                last = mm(bank[1][:, c:c + 1], nrow[:, c * P:(c + 1) * P], konst[:, K_Q4:K_Q4 + 1], start=True, stop=True)
            last.then_inc(S["nsum_mm"], 1)
            pe.wait_ge(S["mrow_ok"], 1)
            for q in range(4):
                last = tr(bank[0][:, q * P:(q + 1) * P], mrow_a[:, q * P:(q + 1) * P], ident)
            last.then_inc(S["mcol_mm"], 1)
            pe.wait_ge(S["xn_ok"], TT)
            pe.wait_ge(S["fspec_out"], 9)
            pe.wait_ge(S["filt_pair"], TT)
            for k in range(KD):
                if k >= 4:
                    pe.wait_ge(S["hT_ok"], k - 3)
                for t in range(TT):
                    last = tr(bank[2 + k % 4][:, t * P:(t + 1) * P], xn[:, t, k * P:(k + 1) * P], ident)
                last.then_inc(S["hT_mm"], 1)
            pe.wait_ge(S["cn_ok"], CT)
            for k in range(KD):
                if k >= 2:
                    pe.wait_ge(S["hcT_ok"], k - 1)
                for t in range(CT):
                    last = tr(bank[6 + k % 2][:, t * P:(t + 1) * P], cn[:, t, k * P:(k + 1) * P], ident)
                last.then_inc(S["hcT_mm"], 1)
            pe.wait_ge(S["hT_ok"], KD)
            pe.wait_ge(S["hcT_ok"], KD)
            pe.wait_ge(S["moda_out"], 1)
            pe.wait_ge(S["nsum_out"], 1)
            for n, (i, kind, c) in enumerate(UNITS):
                if n >= 4:
                    pe.wait_ge(S["unit_out"], n - 3)
                if n == 0 or UNITS[n - 1][0] != i:
                    piece_ready(pe, "W", i)
                w = piece("W", i).rearrange("p (k n) -> p k n", k=KD)
                for k in range(KD):
                    a, z0 = k == 0, k == KD - 1
                    if kind == "u":
                        last = mm(bank[n % 4][:, :], w[:, k, c * P:(c + 1) * P], hT[:, k, :], start=a, stop=z0)
                    elif kind == "q":
                        last = mm(bank[n % 4][:, 0:256], hT[:, k, c * P:(c + 1) * P], w[:, k, :], start=a, stop=z0)
                    else:
                        last = mm(bank[n % 4][:, 0:256], hcT[:, k, c * P:(c + 1) * P], w[:, k, :], start=a, stop=z0)
                last.then_inc(S["unit_mm"], 1)
                n_w = WS.index(i)
                if n_w < 8 and UNITS[n + 1][0] != i:
                    for m in (2 * n_w, 2 * n_w + 1):
                        k, h = m // 2, m % 2
                        piece_ready(pe, "B", m)
                        for j in range(4):
                            last = mm(bank[6 + h][32 * j:32 * j + 32, :], cs[:, k, :], piece("B", m)[:, j * 512:(j + 1) * 512],
                                      start=k == 0, stop=k == 7)
                        last.then_inc(S["piece_used"], 1)
            pe.wait_ge(S["mrow_ok"], 3)
            for t in range(TT):
                if t == 0:
                    pe.wait_ge(S["z_ok"], HC)
                for c in range(HC):
                    last = tr(bank[4 + t][:, c * P:(c + 1) * P], z[:, c, t * P:(t + 1) * P], ident)
                last.then_inc(S["zT_mm"], 1)
            pe.wait_ge(S["zT_ok"], TT)
            pe.wait_ge(S["unit_out"], len(UNITS))
            for n in range(8):
                f = n // 2 + 4 * (n % 2)
                if n >= 4:
                    pe.wait_ge(S["uspec_out"], n - 3)
                for t in range(TT):
                    last = mm(bank[n % 4][:, :], dft[:, t, f * P:(f + 1) * P], ztok[:, t, :], start=t == 0, stop=t == TT - 1)
                last.then_inc(S["uspec_mm"], 1)
            for h in range(2):
                for q in range(4):
                    last = tr(bank[4 + h][:, q * P:(q + 1) * P], mrow_b[h][:, q * P:(q + 1) * P], ident)
            pe.wait_ge(S["uspec_out"], 8)
            pe.wait_ge(S["sel_ok"], 1)
            for n, (h, j) in enumerate(((0, 0), (0, 1), (1, 2), (1, 3))):
                last = mm(bank[(6, 7, 0, 1)[n]][:, :], sel[:, j, :], mrow_b[h], start=True, stop=True)
            last.then_inc(S["modb_mm"], 1)
            pe.wait_ge(S["yspec"], 4)
            pe.wait_ge(S["idft_in"], 16)
            for c in range(HC):
                if c >= 2:
                    pe.wait_ge(S["y_ok"], c - 1)
                for f in range(8):
                    last = mm(bank[2 + c % 2][:, :], uspec[:, f, c * P:(c + 1) * P], idft[:, f, :], start=f == 0, stop=f == 7)
                last.then_inc(S["inv_mm"], 1)
            pe.wait_ge(S["ysq"], HC)
            for c in range(HC):
                last = mm(bank[7][:, :], ones[:, :], ztok[:, c, :], start=c == 0, stop=c == HC - 1)
            last.then_inc(S["ysum_mm"], 1)
            pe.wait_ge(S["qk_ok"], 1)
            pe.wait_ge(S["modb_out"], 1)
            n = 0
            for j in range(8):
                if j >= 4:
                    pe.wait_ge(S["qkT_ok"], j - 3)
                dst = bank[j % 4]
                if j < 4:
                    for t in range(TT):
                        last = tr(dst[:, t * P:(t + 1) * P], qkv[:, t, j * P:(j + 1) * P], ident)
                else:
                    kv, part = (j - 4) // 2, (j - 4) % 2
                    for t in range(TT if part == 0 else CT):
                        last = tr(dst[:, t * P:(t + 1) * P], kd[:, t + TT * part, kv].rearrange("p r d -> p (r d)"), ident)
                last.then_inc(S["qkT_mm"], 1)
            pe.wait_ge(S["qkT_ok"], 8)
            pe.wait_ge(S["y_ok"], HC)
            pe.wait_ge(S["ysum_out"], 1)

            pe.wait_ge(S["kz_ok"], 2)

            def scores(u):
                qb, h = ATT[u]
                lo, hi = local_keys(qb)
                if u >= 2:
                    pe.wait_ge(S["p_exp"], u - 1)
                q, k = qT[:, h // 2, qb * P:(qb + 1) * P], kz[h % 2]
                mm(bank[2 * (u % 2)][:, 0:hi - lo], q, k[:, h // 4, lo:hi], start=True, stop=True)
                mm(bank[2 * (u % 2) + 1][:, 0:LC], q, k[:, h // 4, L:L + LC], start=True, stop=True)\
                    .then_inc(S["s_mm"], 1)

            def weights_T(u):
                qb, h = ATT[u]
                lo, hi = local_keys(qb)
                pe.wait_ge(S["p_ok"], u + 1)
                if u >= 1:
                    pe.wait_ge(S["pT_ok"], u)
                for j in range((hi - lo + LC) // P):
                    dst = bank[4][:, j * P:(j + 1) * P] if j < 4 else bank[5][:, 0:P]
                    last = tr(dst, pbuf(u)[:, 1 + j * P:1 + (j + 1) * P], ident)
                last.then_inc(S["pT_mm"], 1)

            def values(qb):
                lo, hi = local_keys(qb)
                pe.wait_ge(S["pT_ok"], NQ * qb + NQ)
                if qb >= 2:
                    pe.wait_ge(S["a_ok"], qb - 1)
                n = (hi - lo) // P
                for j in range(n + CT):
                    for kv in range(NKV):
                        v = (qkv[:, lo // P + j, AW + KVW + kv * HD:AW + KVW + (kv + 1) * HD] if j < n
                             else kvc[:, j - n, KVW + kv * HD:KVW + (kv + 1) * HD])
                        last = mm(bank[6 + qb % 2][64 * kv:64 * kv + 64, :], v, pt[kv][:, j, :],
                                  start=j == 0, stop=j == n + CT - 1)
                last.then_inc(S["pv_mm"], 1)

            scores(0)
            for u in range(len(ATT) + 1):
                if u + 1 < len(ATT):
                    scores(u + 1)
                if u >= 1:
                    weights_T(u - 1)
                if u > NQ and u % NQ == 1:
                    values(u // NQ - 1)
            values(TT - 1)
            pe.wait_ge(S["asq"], 4)
            for c in range(4):
                last = mm(bank[0][:, :], ones[:, :], asq[:, c, :], start=c == 0, stop=c == 3)
            last.then_inc(S["asum_mm"], 1)
            pe.wait_ge(S["yT_ok"], HC)
            for i in range(4):
                piece_ready(pe, "O", i)
            for part in range(2):
                for t in range(TT):
                    if part == 0 and t == 3:
                        pe.wait_ge(S["asum_out"], 1)
                    if part == 1 and t == 0:
                        pe.wait_ge(S["aT_ok"], 4)
                    for n in range(2):
                        for c in range(4):
                            w = piece("O", 2 * (1 - part) + c // 2)[:, (c % 2) * D + n * 512:(c % 2) * D + (n + 1) * 512]
                            src = (v2, aT)[part][:, c, t * P:(t + 1) * P]
                            last = mm(bank[(2 * t + 2 + n) % 8][:, :], src, w, start=part == 0 and c == 0, stop=part == 1 and c == 3)
                    if part == 1:
                        last.then_inc(S["wo_mm"], 1)
            pe.wait_ge(S["hn_ok"], TT)
            for k in range(KD):
                if k >= 4:
                    pe.wait_ge(S["h2T_ok"], k - 3)
                for t in range(TT):
                    last = tr(bank[k % 4][:, t * P:(t + 1) * P], hn[:, t, k * P:(k + 1) * P], ident)
                last.then_inc(S["h2T_mm"], 1)
            pe.wait_ge(S["h2T_ok"], KD)
            pe.wait_ge(S["late_in"], 48)
            for t in range(TT):
                for k in range(KD):
                    last = mm(bank[4][:, t * NE:(t + 1) * NE], hT[:, k, t * P:(t + 1) * P], wr[:, k, :], start=k == 0, stop=k == KD - 1)
            last.then_inc(S["lg_mm"], 1)
            pe.wait_ge(S["onehot"], 1)
            for t in range(TT):
                last = mm(bank[5][0:NE, 0:1], R.M[:, t, :], ones[:, 0:1], start=t == 0, stop=t == TT - 1)
            last.then_inc(S["cntc_mm"], 1)
            for t in range(TT):
                for s in range(t + 1):
                    last = mm(bank[6][:, t * NE:(t + 1) * NE], ones[:, :] if s < t else konst[:, K_TRI:K_TRI + P],
                              R.M[:, s, :], start=s == 0, stop=s == t)
            last.then_inc(S["pos_mm"], 1)
            pe.wait_ge(S["nbrep"], 1)
            mm(bank[7][:, 0:2 * NE], R.nbrep, konst[0:NE, K_TRE:K_TRE + 2 * NE], start=True, stop=True).then_inc(S["bs_mm"], 1)
            pe.wait_ge(S["gmat"], 1)
            for t in range(TT):
                last = tr(bank[0][0:NE, t * P:(t + 1) * P], R.G[:, t, :], ident)
            last.then_inc(S["gT_mm"], 1)
            pe.wait_ge(S["onehot"], 2)
            for i in range(TT * TOPK):
                last = mm(bank[5][:, 0:2 * BW], R.S1[:, i, :], R.B2[:, i, :], start=i == 0, stop=i == TT * TOPK - 1)
            last.then_inc(S["tab_mm"], 1)
            pe.wait_ge(S["gT_ok"], 1)
            for t in range(TT):
                if t >= 1:
                    pe.wait_ge(S["acc_ok"], t)
                for n in range(2):
                    last = mm(bank[1 + n][:, :], R.GT[:, t * P:(t + 1) * P], R.bd[:, n * 512:(n + 1) * 512], start=True, stop=True)
                last.then_inc(S["bd_mm"], 1)
            def slots_T():
                for k in range(KD):
                    last = tr(bank[6 + k // 4][:, (k % 4) * P:(k % 4 + 1) * P], xs[:, k * P:(k + 1) * P], ident)
                last.then_inc(S["xsT_mm"], 1)

            pe.wait_ge(S["tables"], 2)
            pe.wait_ge(S["gathered"], 16)
            slots_T()
            nblk = pe.value_load(blk[0:1, BW + NE - 1:BW + NE], min_val=0, max_val=BLOCKS - 1) + 1
            with pe.Fori(0, BLOCKS) as b:
                with pe.If(b < nblk):
                    e = pe.value_load(blk[0:1, bass.ds(b, 1)], min_val=0, max_val=NE - 1)
                    many = pe.value_load(more[HALF:HALF + 1, bass.ds(b, 1)], min_val=0, max_val=1)
                    pe.wait_ge(S["xsT_ok"], 2 * b + 2)
                    with pe.If(many > 0):
                        for k in range(KD):
                            pe.wait_ge(full[k], 16 * e + 16)
                            for i in range(4):
                                if k == 0:
                                    pe.wait_ge(S["gate_ready"], 4 * b + i + 1)
                                for q in range(4):
                                    f = (q % 2) * FF + (2 * i + q // 2) * P
                                    last = mm(bank[i][:, q * P:(q + 1) * P], ring[:, k, f:f + P], xsT[:, k, :],
                                              start=k == 0 and q == 0, stop=k == KD - 1, skip_group_check=True)
                                if k == KD - 1:
                                    last.then_inc(S["gu_mm"], 1)
                            if k < KD - 1:
                                last.then_inc(S["free_ring"], 1)
                        pe.sem_inc(S["gu_T"], 4)
                        pe.wait_ge(S["gathered"], 16 * b + 32)
                        slots_T()
                        pe.wait_ge(S["y_out"], b)
                        for s in range(4):
                            pe.wait_ge(S["h_ok"], 4 * b + s + 1)
                            pe.wait_ge(full[KD + s], 16 * e + 16)
                            for c in range(2):
                                for n in range(2):
                                    last = mm(bank[4 + n][:, :], gh[:, 2 * s + c, :],
                                              ring[:, KD + s, c * D + n * 512:c * D + (n + 1) * 512],
                                              start=s + c == 0, stop=s + c == 4)
                            last.then_inc(S["free_ring" if s < 3 else "down_mm"], 1)
                    with pe.Else():
                        for k in range(KD):
                            pe.wait_ge(full[k], 16 * e + 16)
                            for g in range(2):
                                if k == 0:
                                    pe.wait_ge(S["gate_ready"], 4 * b + g + 1)
                                for n in range(2):
                                    last = mm(bank[g][HALF * n:HALF * (n + 1), :], xsT[:, k, 0:HALF],
                                              ring[:, k, g * FF + n * 512:g * FF + (n + 1) * 512],
                                              start=k == 0, stop=k == KD - 1)
                                if k == KD - 1:
                                    last.then_inc(S["gu_mm"], 2)
                            if k < KD - 1:
                                last.then_inc(S["free_ring"], 1)
                        pe.wait_ge(S["gathered"], 16 * b + 32)
                        slots_T()
                        for i in range(2):
                            pe.wait_ge(S["gate_ready"], 4 * b + 3 + i)
                            pe.wait_ge(S["gu_sb"], 2 * b + 2)
                            for q in range(4):
                                last = tr(bank[2 + i][:, q * P:(q + 1) * P],
                                          gusb[:, q % 2, (2 * i + q // 2) * P:(2 * i + q // 2 + 1) * P], ident)
                            last.then_inc(S["gu_T"], 2)
                        pe.wait_ge(S["y_out"], b)
                        for s in range(4):
                            pe.wait_ge(S["h_ok"], 4 * b + (2 if s == 0 else 4))
                            pe.wait_ge(full[KD + s], 16 * e + 16)
                            for c in range(2):
                                f = 2 * s + c
                                for n in range(2):
                                    last = mm(bank[4][HALF * n:HALF * (n + 1), :], gh[:, f % 4, HALF * (f // 4):HALF * (f // 4 + 1)],
                                              ring[:, KD + s, c * D + n * 512:c * D + (n + 1) * 512],
                                              start=f == 0, stop=f == KF - 1)
                            last.then_inc(S["free_ring" if s < 3 else "down_mm"], 1)
                    pe.wait_ge(S["down_mm"], b + 1)

        @block.vector
        def _(v):
            dve = nc.vector
            steps = [0]

            def link(ins):
                steps[0] += 1
                ins.then_inc(S["chain_v"], 1)
                v.wait_ge(S["chain_v"], steps[0])

            v.wait_ge(S["filter_in"], 80)
            for i in range(3):
                v.wait_ge(S["fnet_mm"], i + 1)
                a, n = ftmp
                link(dve.tensor_scalar(a, bank[0][0:64, :], fcol[:, i:i + 1], fcol[:, 3:4], ALU.add, ALU.mult))
                link(dve.tensor_scalar(n, a, 1.0 / (TWO_PI_HI + TWO_PI_LO), ROUND, ALU.mult, ALU.add))
                link(dve.tensor_scalar(n, n, -ROUND, None, ALU.add))
                link(dve.scalar_tensor_tensor(a, n, -TWO_PI_HI, a, ALU.mult, ALU.add))
                link(dve.scalar_tensor_tensor(a, n, -TWO_PI_LO, a, ALU.mult, ALU.add))
                dve.tensor_scalar(a, a, PI_BOUND, -PI_BOUND, ALU.min, ALU.max).then_inc(S["fnet_lin"], 1)
            v.wait_ge(S["small_in"], 64)
            v.wait_ge(S["silu_s"], 1)
            link(dve.memset(cs, 0.0))
            dve.tensor_tensor(cs[:, :, 0:2], cc[:, :, :], sig_c[:, :, :], ALU.mult).then_inc(S["silu"], 1)
            for j in range(4):
                last = dve.tensor_copy(sel[:, j], konst[:, K_ID + 32 * j:K_ID + 32 * j + 1].to_broadcast([P, P]))
            last.then_inc(S["sel_ok"], 1)
            v.wait_ge(S["xs_sq"], 1)
            dve.tensor_scalar(st[:, 0:6], st[:, 0:6], 1.0 / D, EPS, ALU.mult, ALU.add).then_inc(S["x_lin"], 1)
            v.wait_ge(S["decay_in"], 16)
            for t in range(TT):
                v.wait_ge(S["filt_mm"], t + 1)
                dve.tensor_tensor(fpair[:, 0], bank[1 + 2 * (t % 2)][:, :], decay[:, t], ALU.mult)
                dve.tensor_tensor(fpair[:, 1], bank[2 + 2 * (t % 2)][:, :], decay[:, t], ALU.mult).then_inc(S["filt_pair"], 1)
                v.wait_ge(S["filt_pair"], t + 1)
                if t == 0:
                    link(dve.memset(fpair[0:1, 1, :], 0.0))
                link(dve.tensor_tensor(fa[:, t], fpair[:, 0], fpair[:, 1], ALU.add))
                dve.tensor_tensor(fb[:, t], fpair[:, 0], fpair[:, 1], ALU.subtract).then_inc(S["filt_tile"], 1)
                v.wait_ge(S["filt_tile"], t + 1)
            v.wait_ge(S["x_sqrt"], 1)
            link(dve.reciprocal(st[:, 8:14], st[:, 0:6]))
            for t in range(TT):
                dve.tensor_scalar(xn[:, t], xt[:, t], st[:, 8 + t:9 + t], None, ALU.mult).then_inc(S["xn_ok"], 1)
            for t in range(CT):
                dve.tensor_scalar(cn[:, t], ctxt[:, t], st[:, 12 + t:13 + t], None, ALU.mult).then_inc(S["cn_ok"], 1)
            v.wait_ge(S["nsum_mm"], 2)
            dve.tensor_scalar(st[:, 16:20], bank[1][:, 0:HC], 0.5, EPS, ALU.mult, ALU.add).then_inc(S["ns_lin"], 1)
            v.wait_ge(S["ns_sqrt"], 1)
            dve.reciprocal(st[:, 20:24], st[:, 16:20]).then_inc(S["nsum_out"], 1)
            v.wait_ge(S["mcol_mm"], 1)
            def by_chunk(ap, j):
                return ap.rearrange("p (q j m) -> p j q m", q=4, j=4)[:, j:j + 2, :, 0:2] if j is not None else \
                    ap.rearrange("p (q j m) -> p j q m", q=4, j=4)[:, :, :, 0:2]

            def chunks(ap, n):
                return ap.rearrange("p (j q) -> p j q", q=4).unsqueeze(3).to_broadcast([P, n, 4, 2])

            link(dve.tensor_tensor(modc[:, 0:16, :].rearrange("p (j q) m -> p j q m", q=4), by_chunk(bank[0][:, :], None),
                                   chunks(cols[:, C_BMOD:C_BMOD + 16], 4), ALU.add))
            link(dve.tensor_scalar(modc[:, 8:16, :], modc[:, 8:16, :], 1.0, None, ALU.add))
            dve.tensor_tensor(modc[:, 8:16, :], modc[:, 8:16, :],
                              cols[:, C_N1:C_N1 + 8].unsqueeze(2).to_broadcast([P, 8, 2]), ALU.mult).then_inc(S["moda_out"], 1)
            v.wait_ge(S["moda_out"], 1)
            for k in range(KD):
                v.wait_ge(S["hT_mm"], k + 1)
                dve.tensor_scalar(hT[:, k, :], bank[2 + k % 4][:, :], modc[:, 8 + k, 0:1], modc[:, k, 0:1],
                                  ALU.mult, ALU.add).then_inc(S["hT_ok"], 1)
            uflat = uT[:, :, :, :].rearrange("p a c n -> p (a c) n")
            for n in range(3 * HC):
                v.wait_ge(S["unit_mm"], n + 1)
                src, dst = bank[n % 4], uflat[:, n]
                tap = [cols[:, C_CW + 12 * i + n:C_CW + 12 * i + n + 1] for i in range(3)]
                link(dve.tensor_scalar(dst, src[:, :], tap[1], cols[:, C_CB + n:C_CB + n + 1], ALU.mult, ALU.add))
                link(dve.scalar_tensor_tensor(dst[:, 1:L], src[:, 0:L - 1], tap[0], dst[:, 1:L], ALU.mult, ALU.add))
                dve.scalar_tensor_tensor(dst[:, 0:L - 1], src[:, 1:L], tap[2], dst[:, 0:L - 1], ALU.mult, ALU.add)\
                   .then_inc(S["unit_out"], 1)
                v.wait_ge(S["unit_out"], n + 1)
            for c in range(HC):
                dve.tensor_tensor(z[:, c], z[:, c], v2[:, c], ALU.mult).then_inc(S["z_ok"], 1)
            v.wait_ge(S["unit_out"], len(UNITS))
            qk = qkv[:, :, 0:AW + KVW]
            qk4 = qk.rearrange("p t (h d) -> p t h d", d=HD)
            kc = kvc[:, :, 0:KVW]
            kc4 = kc.rearrange("p t (h d) -> p t h d", d=HD)
            kc_sq = rot[1][:, 0:CT, 0:KVW]
            dve.tensor_tensor(rot[0], qk, qk, ALU.mult)
            link(dve.tensor_tensor(kc_sq, kc, kc, ALU.mult))
            dve.tensor_reduce(st[:, 32:72].rearrange("p (t h) -> p t h", t=TT), rot[0].rearrange("p t (h d) -> p t h d", d=HD), X, ALU.add)
            link(dve.tensor_reduce(st[:, 72:76].rearrange("p (t h) -> p t h", t=CT), kc_sq.rearrange("p t (h d) -> p t h d", d=HD), X, ALU.add))
            dve.tensor_scalar(st[:, 32:76], st[:, 32:76], 1.0 / HD, EPS, ALU.mult, ALU.add).then_inc(S["qk_lin"], 1)
            v.wait_ge(S["qk_sqrt"], 1)
            dve.reciprocal(st[:, 80:124], st[:, 32:76]).then_inc(S["qk_factor"], 1)
            v.wait_ge(S["fspec_out"], 9)
            t1, t2, keep = v2[:, 0], v2[:, 1], v2[0:1, 2]
            for f in range(4):
                v.wait_ge(S["uspec_out"], 2 * f + 2)
                ur, ui, kr, ki = uspec[:, f], uspec[:, 4 + f], kspec[:, f], kspec[:, 4 + f]
                dve.tensor_tensor(t1, ui, ki, ALU.mult)
                link(dve.tensor_tensor(t2, ur, ki, ALU.mult))
                if f == 0:
                    link(dve.tensor_copy(keep, t1[0:1, :]))
                    link(dve.memset(t1[0:1, :], 0.0))
                dve.tensor_tensor(ur, ur, kr, ALU.mult)
                link(dve.tensor_tensor(ui, ui, kr, ALU.mult))
                dve.tensor_tensor(ur, ur, t1, ALU.subtract)
                if f == 0:
                    link(dve.tensor_tensor(ui, ui, t2, ALU.add))
                    dve.tensor_copy(ui[0:1, :], keep).then_inc(S["yspec"], 1)
                else:
                    dve.tensor_tensor(ui, ui, t2, ALU.add).then_inc(S["yspec"], 1)
                v.wait_ge(S["yspec"], f + 1)
            v.wait_ge(S["modb_mm"], 1)
            v.wait_ge(S["brow_in"], 16)
            for h in range(2):
                for n in range(2):
                    g = gB[:, h, n * 512:(n + 1) * 512]
                    dve.tensor_tensor(g, g, bank[(6, 7, 0, 1)[2 * h + n]][:, :], ALU.add)
            for h in range(2):
                dst = modc[:, 16 + 8 * h:24 + 8 * h, :].rearrange("p (j q) m -> p j q m", q=4)
                last = dve.tensor_tensor(dst, by_chunk(bank[4 + h][:, :], 2 - 2 * h),
                                         chunks(cols[:, C_BMOD + 24 + 8 * h:C_BMOD + 32 + 8 * h], 2), ALU.add)
            link(last)
            link(dve.tensor_scalar(modc[:, 24:32, :], modc[:, 24:32, :], 1.0, None, ALU.add))
            dve.tensor_tensor(modc[:, 24:32, :], modc[:, 24:32, :],
                              cols[:, C_N2:C_N2 + 8].unsqueeze(2).to_broadcast([P, 8, 2]), ALU.mult).then_inc(S["modb_out"], 1)
            for c in range(HC):
                link(dve.tensor_scalar(z[:, c], z[:, c], cols[:, C_FB + c:C_FB + c + 1], None, ALU.mult))
                v.wait_ge(S["inv_mm"], c + 1)
                dve.scalar_tensor_tensor(v2[:, c], bank[2 + c % 2][:, :], st[:, 20 + c:21 + c], z[:, c], ALU.mult, ALU.add).then_inc(S["y_ok"], 1)
                v.wait_ge(S["y_ok"], c + 1)
                dve.tensor_tensor(v2[:, c], v2[:, c], x0[:, c], ALU.mult).then_inc(S["y_mul"], 1)
            yr = half[:, 0:512]
            v.wait_ge(S["ysum_mm"], 1)
            dve.tensor_scalar(yr, bank[7][:, :], 1.0 / HW, EPS, ALU.mult, ALU.add).then_inc(S["ysum_out"], 1)
            v.wait_ge(S["yr_sqrt"], 1)
            link(dve.reciprocal(yr, yr))
            for c in range(HC):
                dve.scalar_tensor_tensor(v2[:, c], v2[:, c], cols[:, C_HG + c:C_HG + c + 1], yr, ALU.mult, ALU.mult).then_inc(S["yT_ok"], 1)
            sink8 = st[:, 124:132]
            link(dve.tensor_scalar(sink8, rows[:, R_SINK:R_SINK + NQ], 1.0 / ATTN_SCALE, None, ALU.mult))
            top, top2, neg = att_m, att_m2, att_neg

            def maxima(u):
                qb, h = ATT[u]
                lo, hi = local_keys(qb)
                v.wait_ge(S["s_mm"], u + 1)
                if u >= 2:
                    v.wait_ge(S["pT_mm"], u - 1)
                m0 = K_MASK + (P if qb == 0 else 0)
                dve.tensor_copy(pbuf(u)[:, 0:1], sink8[:, h:h + 1])
                dve.tensor_tensor_reduce(out=pbuf(u)[:, 1:1 + hi - lo], in0=bank[2 * (u % 2)][:, 0:hi - lo],
                                         in1=konst[:, m0:m0 + hi - lo], scale=1.0, scalar=sink8[:, h:h + 1],
                                         op0=ALU.add, op1=ALU.max, accum_out=top[:, u:u + 1])
                link(dve.tensor_reduce(top2[:, u:u + 1], bank[2 * (u % 2) + 1][:, 0:LC], X, ALU.max))
                dve.tensor_scalar(neg[:, u:u + 1], top[:, u:u + 1], top2[:, u:u + 1], -ATTN_SCALE, ALU.max, ALU.mult)\
                   .then_inc(S["s_max"], 1)

            def factor(u):
                v.wait_ge(S["p_exp"], u + 1)
                link(dve.tensor_tensor(att_l[:, 2, u:u + 1], att_l[:, 0, u:u + 1], att_l[:, 1, u:u + 1], ALU.add))
                dve.reciprocal(att_l[:, 2, u:u + 1], att_l[:, 2, u:u + 1]).then_inc(S["rl_ok"], 1)

            def copy_T(u):
                qb, h = ATT[u]
                lo, hi = local_keys(qb)
                v.wait_ge(S["pT_mm"], u + 1)
                if qb >= 1 and h == 0:
                    v.wait_ge(S["pv_mm"], qb)
                dst, at = pt[h // 4], (h % 4) * P
                last = dve.tensor_copy(dst[:, 0:4, at:at + P], bank[4][:, :].rearrange("p (j q) -> p j q", j=4))
                if (hi - lo + LC) // P > 4:
                    last = dve.tensor_copy(dst[:, 4, at:at + P], bank[5][:, 0:P])
                last.then_inc(S["pT_ok"], 1)

            for u in range(len(ATT) + 2):
                if u < len(ATT):
                    maxima(u)
                if 1 <= u <= len(ATT):
                    factor(u - 1)
                if u >= 2:
                    copy_T(u - 2)
            v.wait_ge(S["asum_mm"], 1)
            dve.tensor_scalar(ar, bank[0][:, :], 1.0 / AW, EPS, ALU.mult, ALU.add).then_inc(S["asum_out"], 1)
            v.wait_ge(S["ar_sqrt"], 1)
            link(dve.reciprocal(ar, ar))
            for c in range(4):
                dve.scalar_tensor_tensor(aT[:, c], aT[:, c], cols[:, C_AG + c:C_AG + c + 1], ar, ALU.mult, ALU.mult).then_inc(S["aT_ok"], 1)
            for t in range(TT):
                v.wait_ge(S["wo_mm"], t + 1)
                for n in range(2):
                    last = dve.tensor_tensor(wtmp[:, n], bank[(2 * t + 2 + n) % 8][:, :], gB[:, 0, n * 512:(n + 1) * 512], ALU.mult)
                link(last)
                dve.tensor_tensor(xt[:, t], xt[:, t], wtmp.rearrange("p a n -> p (a n)"), ALU.add).then_inc(S["xnew"], 1)
                v.wait_ge(S["xnew"], t + 1)
            v.wait_ge(S["n2_sq"], 1)
            dve.tensor_scalar(st[:, 0:4], st[:, 0:4], 1.0 / D, EPS, ALU.mult, ALU.add).then_inc(S["n2_lin"], 1)
            v.wait_ge(S["n2_sqrt"], 1)
            link(dve.reciprocal(st[:, 8:12], st[:, 0:4]))
            for t in range(TT):
                dve.tensor_scalar(hn[:, t], xt[:, t], st[:, 8 + t:9 + t], None, ALU.mult).then_inc(S["hn_ok"], 1)
            for k in range(KD):
                v.wait_ge(S["h2T_mm"], k + 1)
                dve.tensor_scalar(hT[:, k, :], bank[k % 4][:, :], modc[:, 24 + k, 0:1], modc[:, 16 + k, 0:1],
                                  ALU.mult, ALU.add).then_inc(S["h2T_ok"], 1)
            v.wait_ge(S["lg_mm"], 1)
            link(dve.tensor_tensor(R.lg, bank[4][:, 0:TT * NE].rearrange("p (t e) -> p t e", t=TT),
                                   rows[:, R_BR:R_BR + NE].unsqueeze(1).to_broadcast([P, TT, NE]), ALU.add))
            for t in range(TT):
                last = dve.max(R.v8[:, t], R.lg[:, t])
            link(last)
            for t in range(TT):
                last = dve.max_index(R.i8[:, t], R.v8[:, t], R.lg[:, t])
            link(last)
            dve.tensor_tensor(R.ex, R.v8[:, :, 0:TOPK], R.v8[:, :, 0:1].to_broadcast([P, TT, TOPK]), ALU.subtract).then_inc(S["route_shift"], 1)
            link(dve.tensor_copy(R.i8f, R.i8))
            link(dve.tensor_tensor(R.OH, R.i8f[:, :, 0:TOPK].unsqueeze(3).to_broadcast([P, TT, TOPK, NE]),
                                   konst[:, K_SLOT:K_SLOT + NE].unsqueeze(1).unsqueeze(1).to_broadcast([P, TT, TOPK, NE]), ALU.is_equal))
            dve.tensor_reduce(R.M, R.OH.rearrange("p t k e -> p t e k"), X, ALU.add).then_inc(S["onehot"], 1)
            v.wait_ge(S["cntc_mm"], 1)
            link(dve.tensor_tensor(R.nb4, bank[5][0:NE, 0:1].to_broadcast([NE, 4]), konst[0:NE, K_JN:K_JN + 4], ALU.is_gt))
            link(dve.tensor_reduce(R.nb, R.nb4, X, ALU.add))
            dve.tensor_copy(R.nbrep, R.nb.to_broadcast([NE, P])).then_inc(S["nbrep"], 1)
            v.wait_ge(S["route_exp"], 1)
            link(dve.tensor_reduce(R.sums[:, 0:4], R.ex, X, ALU.add))
            link(dve.reciprocal(R.sums[:, 4:8], R.sums[:, 0:4]))
            link(dve.tensor_tensor(R.gate, R.ex, R.sums[:, 4:8].unsqueeze(2).to_broadcast([P, TT, TOPK]), ALU.mult))
            link(dve.tensor_tensor(R.OHS, R.OH, R.gate.unsqueeze(3).to_broadcast([P, TT, TOPK, NE]), ALU.mult))
            dve.tensor_reduce(R.G, R.OHS.rearrange("p t k e -> p t e k"), X, ALU.add).then_inc(S["gmat"], 1)
            v.wait_ge(S["gmat"], 1)
            v.wait_ge(S["bs_mm"], 1)
            link(dve.tensor_copy(R.bs, bank[7][:, 0:2 * NE]))
            link(dve.scalar_tensor_tensor(R.slot_of, R.bs[:, 0:NE].unsqueeze(1).to_broadcast([P, TT, NE]), float(SLOTS),
                                          bank[6][:, 0:TT * NE].rearrange("p (t e) -> p t e", t=TT), ALU.mult, ALU.add))
            link(dve.tensor_tensor(R.OHS, R.OH, R.slot_of.unsqueeze(2).to_broadcast([P, TT, TOPK, NE]), ALU.mult))
            link(dve.tensor_reduce(R.slot, R.OHS.rearrange("p t k e -> p (t k) e"), X, ALU.add))
            link(dve.tensor_tensor(R.GE, R.slot.unsqueeze(2).to_broadcast([P, 16, BW + 1]),
                                   konst[:, K_BN:K_BN + BW + 1].unsqueeze(1).to_broadcast([P, 16, BW + 1]), ALU.is_ge))
            link(dve.tensor_reduce(R.within, R.GE, X, ALU.add))
            link(dve.tensor_scalar(R.within, R.within, -float(SLOTS), float(SLOTS), ALU.mult, ALU.add))
            link(dve.tensor_tensor(R.within, R.within, R.slot, ALU.add))
            link(dve.tensor_tensor(R.S1, R.within.unsqueeze(2).to_broadcast([P, 16, SLOTS]),
                                   konst[:, K_SLOT:K_SLOT + SLOTS].unsqueeze(1).to_broadcast([P, 16, SLOTS]), ALU.is_equal))
            link(dve.tensor_tensor(R.B2[:, :, 0:BW], R.GE[:, :, 0:BW], R.GE[:, :, 1:BW + 1], ALU.subtract))
            link(dve.tensor_tensor(R.B2[:, :, BW:2 * BW], R.B2[:, :, 0:BW],
                                   R.gate.rearrange("p t k -> p (t k)").unsqueeze(2).to_broadcast([P, 16, BW]), ALU.mult))
            B4 = R.B2[:, :, 0:BW].rearrange("p (t k) b -> p t k b", t=TT)
            dve.tensor_tensor(B4, B4, konst[:, K_VAL:K_VAL + TT].unsqueeze(2).unsqueeze(3).to_broadcast([P, TT, TOPK, BW]),
                              ALU.mult).then_inc(S["onehot"], 1)
            link(dve.tensor_tensor(R.blkcmp, R.bs[0:1, NE:2 * NE].unsqueeze(1).to_broadcast([1, BW, NE]),
                                   konst[0:1, K_SLOT:K_SLOT + BW].unsqueeze(2).to_broadcast([1, BW, NE]), ALU.is_le))
            link(dve.tensor_reduce(R.blkf[:, 0:BW], R.blkcmp, X, ALU.add))
            link(dve.tensor_scalar(R.blkf[:, 0:BW], R.blkf[:, 0:BW], float(NE - 1), None, ALU.min))
            dve.tensor_copy(blk[:, 0:BW], R.blkf[:, 0:BW])
            dve.tensor_scalar(blk[:, BW:BW + NE], R.bs[0:1, NE:2 * NE], -1.0, None, ALU.add).then_inc(S["tables"], 1)
            v.wait_ge(S["tab_mm"], 1)
            link(dve.tensor_scalar(R.tok, bank[5][:, 0:BW], float(2 * L), None, ALU.add))
            dve.tensor_scalar(idx[:, 0], R.tok, float(L - 1), None, ALU.min)
            dve.tensor_scalar(idx[:, 1], R.tok, konst[:, K_ROW:K_ROW + 1], None, ALU.min)
            dve.tensor_scalar(more[HALF:HALF + 1, :], R.tok[HALF:HALF + 1, :], float(L), None, ALU.is_lt)
            dve.tensor_copy(tabs[:, :], bank[5][:, BW:2 * BW]).then_inc(S["tables"], 1)
            v.wait_ge(S["gT_mm"], 1)
            dve.tensor_copy(R.GT, bank[0][0:NE, :]).then_inc(S["gT_ok"], 1)
            for t in range(TT):
                v.wait_ge(S["bd_mm"], t + 1)
                for n in range(2):
                    last = dve.tensor_tensor(wtmp[:, n], bank[1 + n][:, :], gB[:, 1, n * 512:(n + 1) * 512], ALU.mult)
                link(last)
                dve.tensor_tensor(xt[:, t], xt[:, t], wtmp.rearrange("p a n -> p (a n)"), ALU.add).then_inc(S["acc_ok"], 1)
                v.wait_ge(S["acc_ok"], t + 1)

            v.sem_inc(S["gate_ready"], 4)
            v.wait_ge(S["tables"], 2)
            nblk = v.value_load(blk[0:1, BW + NE - 1:BW + NE], min_val=0, max_val=BLOCKS - 1) + 1
            base = steps[0]
            PER = 10
            with v.Fori(0, BLOCKS) as b:
                with v.If(b < nblk):
                    n = [0]

                    def step(ins):
                        n[0] += 1
                        ins.then_inc(S["chain_v"], 1)
                        v.wait_ge(S["chain_v"], b * PER + (base + n[0]))

                    def bounds(i, src, bias, by):
                        s = gu[:, i % 2]
                        if i >= 2:
                            v.wait_ge(S["h_ok"], 4 * b + i - 1)
                        shape = "p (q h s) -> p q h s"
                        dve.tensor_tensor(s.rearrange("p q (h s) -> p q h s", s=HALF), src[:, :].rearrange(shape, q=4, s=HALF),
                                          bias, ALU.add).then_inc(S["gate_ready"], by)
                        v.wait_ge(S["gate_ready"], 4 * b + by * (i + 1) + 4)
                        g = s.rearrange("p (c r) s -> p c r s", r=2)
                        dve.tensor_scalar(g[:, :, 0], g[:, :, 0], LIMIT, None, ALU.min).then_inc(S["glu_p"], by)
                        step(dve.tensor_scalar(g[:, :, 1], g[:, :, 1], LIMIT, -LIMIT, ALU.min, ALU.max))

                    def gates(i, by):
                        g = gu[:, i % 2].rearrange("p (c r) s -> p c r s", r=2)
                        v.wait_ge(S["sig"], 4 * b + by * (i + 1))
                        step(dve.tensor_tensor(g[:, :, 0], g[:, :, 0], sg[:, i % 2], ALU.mult))
                        dve.scalar_tensor_tensor(gh[:, 2 * i:2 * i + 2, :], g[:, :, 1], 1.0, g[:, :, 0], ALU.add, ALU.mult)\
                           .then_inc(S["h_ok"], by)

                    e = v.value_load(blk[0:1, bass.ds(b, 1)], min_val=0, max_val=NE - 1)
                    many = v.value_load(more[HALF:HALF + 1, bass.ds(b, 1)], min_val=0, max_val=1)
                    dve.tensor_copy(gcur, tabs[:, bass.ds(b, 1)])
                    step(dve.tensor_copy(bcur, bgu[:, bass.ds(e, 1), :].rearrange("p o j -> p (o j)")))
                    v.sem_inc(S["dve_step"], 1)
                    n0 = n[0]
                    with v.If(many > 0):
                        for i in range(4):
                            v.wait_ge(S["gu_mm"], 4 * b + i + 1)
                            bounds(i, bank[i], bcur[:, 4 * i:4 * i + 4].unsqueeze(2).unsqueeze(3).to_broadcast([P, 4, 2, HALF]), 1)
                            if i >= 1:
                                gates(i - 1, 1)
                        gates(3, 1)
                        v.wait_ge(S["down_mm"], b + 1)
                        v.wait_ge(S["scattered"], 16 * b)
                        dve.scalar_tensor_tensor(yb[:, 0:512], bank[4][:, :], gcur, gB[:, 1, 0:512], ALU.mult, ALU.mult)
                        dve.scalar_tensor_tensor(yb[:, 512:D], bank[5][:, :], gcur, gB[:, 1, 512:D], ALU.mult, ALU.mult)\
                           .then_inc(S["y_out"], 1)
                        v.wait_ge(S["y_out"], b + 1)
                        for _ in range(PER - n[0]):
                            v.sem_inc(S["chain_v"], 1)
                    with v.Else():
                        n[0] = n0
                        halves = bcur.rearrange("p (h j) -> p j h", h=2)
                        step(dve.tensor_copy(gcur2[HALF:P], gcur[0:HALF]))
                        for i in range(2):
                            v.wait_ge(S["gu_T"], 4 * b + 2 * i + 2)
                            bounds(i, bank[2 + i], halves[:, 4 * i:4 * i + 4].unsqueeze(3).to_broadcast([P, 4, 2, HALF]), 2)
                            if i >= 1:
                                gates(i - 1, 2)
                        gates(1, 2)
                        v.wait_ge(S["down_mm"], b + 1)
                        v.wait_ge(S["scattered"], 16 * b)
                        dve.scalar_tensor_tensor(yb[0:HALF, 0:512], bank[4][0:HALF, :], gcur[0:HALF], gB[0:HALF, 1, 0:512], ALU.mult, ALU.mult)
                        dve.scalar_tensor_tensor(yb[0:HALF, 512:D], bank[4][HALF:P, :], gcur2[HALF:P], gB[HALF:P, 1, 512:D], ALU.mult, ALU.mult)\
                           .then_inc(S["y_out"], 1)
                        v.wait_ge(S["y_out"], b + 1)
                        for _ in range(PER - n[0]):
                            v.sem_inc(S["chain_v"], 1)

        @block.scalar
        def _(act):
            f = nc.scalar.activation
            steps = [0]

            def link(ins):
                steps[0] += 1
                ins.then_inc(S["chain_a"], 1)
                act.wait_ge(S["chain_a"], steps[0])

            act.dma_start(zin, t_z).then_inc(S["filter_in"], 16)
            act.dma_start(w1, t_w1).then_inc(S["filter_in"], 16)
            act.dma_start(w23, t_w23).then_inc(S["filter_in"], 16)
            act.dma_start(fcol, t_fcol).then_inc(S["filter_in"], 16)
            act.dma_start(w4, t_w4).then_inc(S["filter_in"], 16)
            act.dma_start(konst[:, :], t_konst).then_inc(S["small_in"], 16)
            act.dma_start(cc[:, :, :], t_cc).then_inc(S["small_in"], 16)
            act.dma_start(cols[:, :], t_cols).then_inc(S["small_in"], 16)
            act.dma_start(rows[:, :], t_rows.to_broadcast([P, NR])).then_inc(S["small_in"], 16)
            act.dma_start(ctxt[:, :, :], t_ctx.rearrange("(t p) d -> p t d", p=P)).then_inc(S["ctx_in"], 16)
            act.wait_ge(S["small_in"], 64)
            f(sig_c[:, :, :], cc[:, :, :], ACT.Sigmoid).then_inc(S["silu_s"], 1)
            for i in range(3):
                act.wait_ge(S["fnet_lin"], i + 1)
                f(fh[i % 2], ftmp[0], ACT.Sin).then_inc(S["fnet_sin"], 1)
            act.wait_ge(S["x_in"], 16)
            act.wait_ge(S["ctx_in"], 16)
            for t in range(TT + CT):
                src = xt[:, t] if t < TT else ctxt[:, t - TT]
                last = f(square, src, ACT.Square, accum_out=st[:, t:t + 1])
                if t < TT + CT - 1:
                    link(last)
            last.then_inc(S["xs_sq"], 1)
            act.wait_ge(S["x_lin"], 1)
            f(st[:, 0:6], st[:, 0:6], ACT.Sqrt).then_inc(S["x_sqrt"], 1)
            for n in range(9):
                act.wait_ge(S["fspec_mm"], n + 1)
                if n < 8:
                    f(kspec[:, n], bank[5 + n % 3][:, :], ACT.Copy).then_inc(S["fspec_out"], 1)
                else:
                    act.wait_ge(S["fspec_out"], 8)
                    f(kspec[0:1, 4], bank[5 + n % 3][0:1, :], ACT.Copy).then_inc(S["fspec_out"], 1)
            act.wait_ge(S["nsum_mm"], 1)
            f(nrow, bank[1][:, :], ACT.Copy).then_inc(S["nrow_ok"], 1)
            act.wait_ge(S["piece_used"], 8)
            f(mrow_a, bank[0][:, :], ACT.Copy).then_inc(S["mrow_ok"], 1)
            act.wait_ge(S["ns_lin"], 1)
            f(st[:, 16:20], st[:, 16:20], ACT.Sqrt).then_inc(S["ns_sqrt"], 1)
            act.wait_ge(S["moda_out"], 1)
            for k in range(KD):
                act.wait_ge(S["hcT_mm"], k + 1)
                f(hcT[:, k, :], bank[6 + k % 2][:, 0:LC], ACT.Identity, bias=modc[:, k, 1:2], scale=modc[:, 8 + k, 1:2])\
                    .then_inc(S["hcT_ok"], 1)
            act.wait_ge(S["unit_out"], 3 * HC)
            for n in range(3 * HC, len(UNITS)):
                i, kind, t = UNITS[n]
                act.wait_ge(S["unit_mm"], n + 1)
                dst = kvc[:, t] if kind == "c" else qkv[:, t, i * 256:(i + 1) * 256]
                f(dst, bank[n % 4][:, 0:256], ACT.Copy).then_inc(S["unit_out"], 1)
            act.wait_ge(S["piece_used"], 24)
            for h in range(2):
                f(mrow_b[h], bank[6 + h][:, :], ACT.Copy).then_inc(S["mrow_ok"], 1)
            act.wait_ge(S["qk_lin"], 1)
            f(st[:, 32:76], st[:, 32:76], ACT.Sqrt).then_inc(S["qk_sqrt"], 1)
            for t in range(TT):
                act.wait_ge(S["zT_mm"], t + 1)
                f(ztok[:, t], bank[4 + t][:, :], ACT.Copy).then_inc(S["zT_ok"], 1)
            for n in range(8):
                act.wait_ge(S["uspec_mm"], n + 1)
                f(uspec[:, n // 2 + 4 * (n % 2)], bank[n % 4][:, :], ACT.Copy).then_inc(S["uspec_out"], 1)
            for c in range(HC):
                act.wait_ge(S["y_mul"], c + 1)
                f(ztok[:, c], v2[:, c], ACT.Square).then_inc(S["ysq"], 1)
            act.wait_ge(S["ysum_out"], 1)
            f(half[:, 0:512], half[:, 0:512], ACT.Sqrt).then_inc(S["yr_sqrt"], 1)
            for j in range(8):
                act.wait_ge(S["qkT_mm"], j + 1)
                if j < 4:
                    f(qT[:, j], bank[j % 4][:, :], ACT.Copy).then_inc(S["qkT_ok"], 1)
                else:
                    kv, part = (j - 4) // 2, (j - 4) % 2
                    keys = slice(0, L) if part == 0 else slice(L, L + LC)
                    n = keys.stop - keys.start
                    f(kz[0][0:64, kv, keys], bank[j % 4][0:64, 0:n], ACT.Copy)
                    f(kz[1][64:P, kv, keys], bank[j % 4][64:P, 0:n], ACT.Copy).then_inc(S["qkT_ok"], 1)

            def out_T(qb):
                act.wait_ge(S["pv_mm"], qb + 1)
                f(aT[:, :, qb * P:(qb + 1) * P], bank[6 + qb % 2][:, :].rearrange("p (h q) -> p h q", h=4), ACT.Copy)\
                    .then_inc(S["a_ok"], 1)

            for u in range(len(ATT)):
                qb, h = ATT[u]
                lo, hi = local_keys(qb)
                w = 1 + hi - lo
                act.wait_ge(S["s_max"], u + 1)
                f(pbuf(u)[:, 0:w], pbuf(u)[:, 0:w], ACT.Exp, bias=att_neg[:, u:u + 1], scale=ATTN_SCALE, accum_out=att_l[:, 0, u:u + 1])
                f(pbuf(u)[:, w:w + LC], bank[2 * (u % 2) + 1][:, 0:LC], ACT.Exp, bias=att_neg[:, u:u + 1], scale=ATTN_SCALE,
                  accum_out=att_l[:, 1, u:u + 1]).then_inc(S["p_exp"], 1)
                if qb >= 1 and h == 3:
                    out_T(qb - 1)
            out_T(TT - 1)
            act.wait_ge(S["a_ok"], TT)
            for c in range(4):
                f(asq[:, c], aT[:, c], ACT.Square).then_inc(S["asq"], 1)
            act.wait_ge(S["asum_out"], 1)
            f(ar, ar, ACT.Sqrt).then_inc(S["ar_sqrt"], 1)
            for t in range(TT):
                act.wait_ge(S["xnew"], t + 1)
                last = f(slab[:, 0:D], xt[:, t], ACT.Square, accum_out=st[:, t:t + 1])
                if t < TT - 1:
                    link(last)
            last.then_inc(S["n2_sq"], 1)
            act.wait_ge(S["n2_lin"], 1)
            f(st[:, 0:4], st[:, 0:4], ACT.Sqrt).then_inc(S["n2_sqrt"], 1)
            for t in range(TT):
                act.wait_ge(S["hn_ok"], t + 1)
                act.dma_start(d_hn[t * P:(t + 1) * P, :], hn[:, t]).then_inc(S["hn_stored"], 16)
            act.wait_ge(S["route_shift"], 1)
            f(R.ex, R.ex, ACT.Exp).then_inc(S["route_exp"], 1)
            for t in range(TT):
                act.wait_ge(S["acc_ok"], t + 1)
                act.dma_start(d_acc[t * P:(t + 1) * P, :], xt[:, t]).then_inc(S["acc_in"], 16)
            act.dma_start(d_acc[L:L + SLOTS, :], xt[:, 0]).then_inc(S["acc_in"], 16)

            def modulate(at):
                act.wait_ge(S["xsT_mm"], at)
                for k in range(KD):
                    last = f(xsT[:, k], bank[6 + k // 4][:, (k % 4) * P:(k % 4 + 1) * P], ACT.Identity,
                             bias=modc[:, 16 + k, 0:1], scale=modc[:, 24 + k, 0:1])
                    if k % 4 == 3:
                        last.then_inc(S["xsT_ok"], 1)

            modulate(1)
            act.wait_ge(S["tables"], 2)
            nblk = act.value_load(blk[0:1, BW + NE - 1:BW + NE], min_val=0, max_val=BLOCKS - 1) + 1
            with act.Fori(0, BLOCKS) as b:
                with act.If(b < nblk):
                    many = act.value_load(more[HALF:HALF + 1, bass.ds(b, 1)], min_val=0, max_val=1)

                    def sigmoid(i, by):
                        g = gu[:, i % 2].rearrange("p (c r) s -> p c r s", r=2)
                        act.wait_ge(S["glu_p"], 4 * b + by * (i + 1))
                        f(sg[:, i % 2], g[:, :, 0], ACT.Sigmoid, scale=ALPHA).then_inc(S["sig"], by)

                    with act.If(many > 0):
                        act.sem_inc(S["gu_sb"], 2)
                        for i in range(4):
                            sigmoid(i, 1)
                    with act.Else():
                        for g in range(2):
                            act.wait_ge(S["gu_mm"], 4 * b + 2 * g + 2)
                            f(gusb[:, g], bank[g][:, :], ACT.Copy).then_inc(S["gu_sb"], 1)
                        for i in range(2):
                            sigmoid(i, 2)
                    modulate(b + 2)
            act.wait_ge(S["scattered"], 16)

        @block.gpsimd
        def _(pool):
            nc.gpsimd.memset(ones[:, :], 1.0).then_inc(S["ones_ok"], 1)
            for t in range(TT):
                pool.wait_ge(S["filt_tile"], t + 1)
                nc.gpsimd.tensor_tensor(sq[:, t], fa[:, t], fa[:, t], ALU.mult).then_inc(S["filt_sq"], 1)
                nc.gpsimd.tensor_tensor(sq[:, TT + t], fb[:, t], fb[:, t], ALU.mult).then_inc(S["filt_sq"], 1)

            pool_ = nc.gpsimd
            steps = [0]

            def link(ins):
                steps[0] += 1
                ins.then_inc(S["chain_p"], 1)
                pool.wait_ge(S["chain_p"], steps[0])

            pool.wait_ge(S["qk_factor"], 1)
            qk = qkv[:, :, 0:AW + KVW]
            qk4 = qk.rearrange("p t (h d) -> p t h d", d=HD)
            kc4 = kvc[:, :, 0:KVW].rearrange("p t (h d) -> p t h d", d=HD)
            pool_.tensor_tensor(qk4, qk4, st[:, 80:120].rearrange("p (t h) -> p t h", t=TT).unsqueeze(3).to_broadcast([P, TT, NQ + NKV, HD]), ALU.mult)
            link(pool_.tensor_tensor(kc4, kc4, st[:, 120:124].rearrange("p (t h) -> p t h", t=CT).unsqueeze(3).to_broadcast([P, CT, NKV, HD]), ALU.mult))

            def gain(at, t, h):
                return rows[:, at:at + HD].unsqueeze(1).unsqueeze(1).to_broadcast([P, t, h, HD])

            pool_.tensor_tensor(qk4[:, :, 0:NQ], qk4[:, :, 0:NQ], gain(R_QN, TT, NQ), ALU.mult)
            pool_.tensor_tensor(qk4[:, :, NQ:], qk4[:, :, NQ:], gain(R_KN, TT, NKV), ALU.mult)
            link(pool_.tensor_tensor(kc4, kc4, gain(R_KN, CT, NKV), ALU.mult))
            pairs = qk.rearrange("p t (g j i) -> p t g j i", j=2, i=HD // 4)
            swapped = rot[0].rearrange("p t (g j i) -> p t g j i", j=2, i=HD // 4)
            pool_.tensor_copy(swapped[:, :, :, 0], pairs[:, :, :, 1])
            link(pool_.tensor_copy(swapped[:, :, :, 1], pairs[:, :, :, 0]))

            def turn(at):
                return konst[:, at:at + TT * HD].rearrange("p (t d) -> p t d", t=TT).unsqueeze(2).to_broadcast([P, TT, NQ + NKV, HD])

            rot4 = [r.rearrange("p t (h d) -> p t h d", d=HD) for r in rot]
            pool_.tensor_tensor(rot4[0], rot4[0], turn(K_RS), ALU.mult)
            link(pool_.tensor_tensor(rot4[1], qk4, turn(K_RC), ALU.mult))
            link(pool_.tensor_tensor(qk4, rot4[0], rot4[1], ALU.add))
            for r in range(2):
                pool_.tensor_copy(kd[:, 0:TT, :, r], qk4[:, :, NQ:])
                last = pool_.tensor_copy(kd[:, TT:, :, r], kc4)
            last.then_inc(S["qk_ok"], 1)
            pool.wait_ge(S["qk_ok"], 1)
            pool.wait_ge(S["modb_out"], 1)
            nc.gpsimd.memset(kz[0][64:P, :, :], 0.0).then_inc(S["kz_ok"], 1)
            pool.wait_ge(S["kz_ok"], 1)
            pool.wait_ge(S["ysum_mm"], 1)
            nc.gpsimd.memset(kz[1][0:64, :, :], 0.0).then_inc(S["kz_ok"], 1)
            pool.wait_ge(S["kz_ok"], 2)
            for u in range(len(ATT)):
                lo, hi = local_keys(ATT[u][0])
                pool.wait_ge(S["rl_ok"], u + 1)
                w = pbuf(u)[:, 1:1 + hi - lo + LC]
                nc.gpsimd.tensor_scalar(w, w, att_l[:, 2, u:u + 1], 1.0, ALU.mult, ALU.mult).then_inc(S["p_ok"], 1)

            def gather(n):
                pool.indirect_dma_start(out=xs[0:n], out_offset=None, in_=d_hn,
                                        in_offset=bass.IndirectOffsetOnAxis(ap=icur[0:n, 0:1].bitcast(u32), axis=0)).then_inc(S["gathered"], 16)

            def add_rows(n):
                pool.indirect_dma_start(out=d_acc, out_offset=bass.IndirectOffsetOnAxis(ap=icur[0:n, 1:2].bitcast(u32), axis=0),
                                        in_=yb[0:n], in_offset=None, compute_op=ALU.add).then_inc(S["scattered"], 16)

            pool.wait_ge(S["wo_mm"], TT)
            nc.gpsimd.memset(xs, 0.0).then_inc(S["chain_p"], 1)
            done = steps[0]
            pool.wait_ge(S["tables"], 2)
            pool.wait_ge(S["hn_stored"], 16 * TT)
            nc.gpsimd.tensor_copy(icur[:, 0:1], idx[:, 0, 0:1]).then_inc(S["chain_p"], 1)
            pool.wait_ge(S["chain_p"], done + 2)
            gather(SLOTS)
            pool.wait_ge(S["acc_in"], 16 * (TT + 1))
            nblk = pool.value_load(blk[0:1, BW + NE - 1:BW + NE], min_val=0, max_val=BLOCKS - 1) + 1
            with pool.Fori(0, BLOCKS) as b:
                with pool.If(b < nblk):
                    next_many = pool.value_load(more[HALF:HALF + 1, bass.ds(b + 1, 1)], min_val=0, max_val=1)
                    many = pool.value_load(more[HALF:HALF + 1, bass.ds(b, 1)], min_val=0, max_val=1)
                    pool.wait_ge(S["xsT_mm"], b + 1)
                    pool.sem_inc(S["pool_step"], 1)
                    nc.gpsimd.tensor_copy(icur[:, 0:1], idx[:, 0, bass.ds(b + 1, 1)]).then_inc(S["chain_p"], 1)
                    pool.wait_ge(S["chain_p"], 2 * b + (done + 3))
                    pool.sem_inc(S["pool_step"], 1)
                    with pool.If(next_many > 0):
                        gather(SLOTS)
                    with pool.Else():
                        gather(HALF)
                    pool.wait_ge(S["scattered"], 16 * b)
                    pool.sem_inc(S["pool_step"], 1)
                    nc.gpsimd.tensor_copy(icur[:, 1:2], idx[:, 1, bass.ds(b, 1)]).then_inc(S["chain_p"], 1)
                    pool.wait_ge(S["chain_p"], 2 * b + (done + 4))
                    pool.wait_ge(S["y_out"], b + 1)
                    pool.sem_inc(S["pool_step"], 1)
                    with pool.If(many > 0):
                        add_rows(SLOTS)
                    with pool.Else():
                        add_rows(HALF)
                    pool.sem_inc(S["pool_step"], 1)
            pool.wait_ge(S["scattered"], nblk * 16)
            pool.sem_inc(S["pool_step"], 1)
            pool.dma_start(t_out, d_acc[0:L, :]).then_inc(S["out_done"], 16)
            pool.wait_ge(S["out_done"], 16)


def _constants():
    import numpy as np
    f32 = np.float32
    n = 2 * L
    t = np.arange(L)
    ang = 2.0 * np.pi * ((t[:, None] * np.arange(L)[None, :]) % n) / n
    nyq = np.where(t % 2 == 0, 1.0, -1.0)
    cos, sin = np.cos(ang), -np.sin(ang)
    sin[:, 0] = nyq
    dft = np.concatenate([cos, sin], axis=1)
    scale = np.full((n, 1), 2.0 / n)
    scale[0] = scale[L] = 1.0 / n
    idft = dft.T * scale
    konst = np.zeros((P, NK), f32)
    i = np.arange(P)
    konst[:, K_ID:K_ID + P] = np.eye(P)
    konst[:, K_TRI:K_TRI + P] = i[:, None] < i[None, :]
    konst[:, K_MASK:K_MASK + P] = np.where(i[None, :] >= i[:, None], 0.0, -1e30)
    konst[:, K_MASK + 2 * P:K_MASK + 3 * P] = np.where(i[None, :] <= i[:, None], 0.0, -1e30)
    nf = HD // 4
    inv = (f32(10000.0) ** (-np.arange(nf, dtype=f32) / f32(nf))).astype(f32)
    for tile in range(TT):
        pos = tile * P + i
        for j, p in enumerate((pos // 64, pos % 64)):
            a = (p[:, None].astype(f32) * inv[None, :]).astype(f32)
            at = tile * HD + j * 2 * nf
            for r in range(2):
                konst[:, K_RC + at + r * nf:K_RC + at + (r + 1) * nf] = np.cos(a)
                konst[:, K_RS + at + r * nf:K_RS + at + (r + 1) * nf] = (-1.0, 1.0)[r] * np.sin(a)
    konst[:, K_SLOT:K_SLOT + SLOTS] = np.arange(SLOTS)
    konst[:, K_BN:K_BN + 64] = SLOTS * np.arange(64)
    konst[:, K_VAL:K_VAL + TT] = np.arange(TT)[None, :] * P + i[:, None] - 2 * L
    konst[:, K_ROW] = L + i
    e = np.arange(NE)
    konst[0:NE, K_TRE:K_TRE + NE] = e[:, None] < e[None, :]
    konst[0:NE, K_TRE + NE:K_TRE + 2 * NE] = e[:, None] <= e[None, :]
    konst[:, K_JN:K_JN + 4] = SLOTS * np.arange(4)
    konst[:, K_JN] = -1.0
    konst[0:P:32, K_Q4] = 1.0
    tl = np.linspace(0.0, 1.0, L, dtype=f32)[:, None]
    w = (f32(2.0 * np.pi) * np.arange(L, dtype=f32)[:, None] / f32(L)).astype(f32)
    bands = np.linspace(1e-4, 15, 16, dtype=f32)[None, :]
    zf = np.concatenate([tl, np.cos(bands * w), -np.sin(bands * w)], axis=1).astype(f32)
    lo, hi = -np.log(1e-2) / 1.5, -np.log(1e-2) / 0.3
    deltas = np.linspace(lo, hi, HW, dtype=f32)
    decay = np.exp(-tl * deltas[None, :]).astype(f32)
    return konst, zf.T.copy(), decay, dft.astype(f32), idft.astype(f32)


def kernel(**inputs):
    import numpy as np
    import concourse.bacc as bacc
    from concourse.bass_utils import run_bass_kernel_spmd

    g = {k: np.asarray(v) for k, v in inputs.items()}
    konst, zf, decay, dft, idft = _constants()

    def columns(a):
        return a.reshape(-1, P).T

    def by_head(a):
        return a.reshape(NKV, NQ // NKV, HD, -1).transpose(1, 0, 2, 3).reshape(AW, -1)

    g["attn_out_norm"] = by_head(g["attn_out_norm"][0])
    g["w_out"] = np.concatenate([by_head(g["w_out"][0, :AW]), g["w_out"][0, AW:]], axis=0)[None]
    cols = np.concatenate([columns(g[k]) for k in ("b_mod", "norm1", "norm2", "conv_w", "conv_b", "filt_bias",
                                                    "attn_out_norm", "hyena_out_norm")], axis=1)
    rows = np.concatenate([g[k].reshape(1, -1) for k in ("q_norm", "k_norm", "sink", "b_router")], axis=1)
    cc = np.stack([g["c"].reshape(KD, P), g["c_ctx"].reshape(KD, P)], axis=-1).transpose(1, 0, 2)
    bgu = g["b_gu"].reshape(NE, 2, KF, P).transpose(3, 0, 2, 1).reshape(P, NE, 2 * KF)
    arrays = {
        "x": g["x"].reshape(L, D), "ctx": g["ctx"].reshape(LC, D), "cc": cc, "cols": cols, "rows": rows,
        "konst": konst, "z": zf, "w1": g["filt_w1"][0], "w23": np.stack([g["filt_w2"][0], g["filt_w3"][0]], axis=1),
        "fcol": np.stack([g[k][0] for k in ("filt_b1", "filt_b2", "filt_b3", "filt_freq")], axis=1),
        "w4": g["filt_w4"][0], "decay": decay, "dft": dft, "idft": idft, "wmod": g["w_mod"][0],
        "brows": np.concatenate([g["b_mod"][:, 2 * D:3 * D], g["b_mod"][:, 5 * D:6 * D]], axis=1),
        "win": g["w_in"][0], "wout": g["w_out"][0], "wr": g["w_router"][0], "bgu": bgu,
        "wgu": g["w_gu"].reshape(NE * KD, P, 2 * FF), "wdown": g["w_down"].reshape(NE * 4, 2, P, D),
        "bdown": g["b_down"][0],
    }
    nc = bacc.Bacc("TRN2", target_bir_lowering=False, num_devices=1)
    arrays = {f"in_{k}": np.ascontiguousarray(a) for k, a in arrays.items()}
    args = [nc.dram_tensor(k, a.shape, mybir.dt.from_np(a.dtype), kind="ExternalInput").ap() for k, a in arrays.items()]
    args.append(nc.dram_tensor("out", (L, D), mybir.dt.float32, kind="ExternalOutput").ap())
    layer_kernel(nc, *args)
    r = run_bass_kernel_spmd(nc, [arrays], core_ids=[0])
    return r.results[0]["out"].reshape(1, L, D)
```

```python
from contextlib import ExitStack, contextmanager

import concourse.bass as bass
from concourse import mybir

P = 128
D = 1024
L = 512
LC = 256
TT = L // P
CT = LC // P
KD = D // P
HD = 64
NQ = 8
NKV = 2
AW = NQ * HD
KVW = NKV * HD
HW = D - AW
HC = HW // P
QKV = AW + 2 * KVW
NE = 32
TOPK = 4
FF = 1024
KF = FF // P
SLOTS = P
BLOCKS = (L * TOPK + NE * (SLOTS - 1)) // SLOTS
GROUP = 6
GROUPS = -(-BLOCKS // GROUP)
BW = GROUPS * GROUP + 2
EPS = 1e-6
ATTN_SCALE = HD ** -0.5
LIMIT = 7.0
ALPHA = 1.702
HALF = SLOTS // 2
QUART = SLOTS // 4
PIECE = 2048
RING = 12
FRONT_RING = 4
TWO_PI_HI = 6.28125
TWO_PI_LO = 6.283185307179586 - TWO_PI_HI
ROUND = 12582912.0
PI_BOUND = 3.1415925

C_BMOD, C_N1, C_N2, C_CW, C_CB, C_FB, C_AG, C_HG = 0, 48, 56, 64, 100, 112, 116, 120
NCOLS = 124
K_ID, K_TRI, K_MASK, K_RC, K_RS = 0, 128, 256, 640, 896
K_SLOT, K_BN, K_VAL, K_ROW, K_TRE, K_JN, K_Q4, K_S4 = 1152, 1280, 1344, 1348, 1349, 1413, 1417, 1418
NK = 1450
R_QN, R_KN, R_SINK, R_BR = 0, 64, 128, 136
NR = 168


def layer_kernel(nc, t_x, t_ctx, t_cc, t_cols, t_rows, t_konst, t_z, t_w1, t_w23, t_fcol, t_w4,
                 t_decay, t_dft, t_idft, t_wmod, t_brows, t_win, t_wout, t_wr, t_bgu, t_wgu,
                 t_wdown, t_bdown, t_out):
    f32, i32, u32 = mybir.dt.float32, mybir.dt.int32, mybir.dt.uint32
    ALU = mybir.AluOpType
    ACT = mybir.ActivationFunctionType
    X = mybir.AxisListType.X

    d_hn = nc.dram_tensor("normed_rows", [L, D], f32, kind="Internal").ap()

    with ExitStack() as ctx:
        def sb(name, shape, dt=f32):
            return ctx.enter_context(nc.sbuf_tensor(name, shape, dt))

        def sem(name):
            return ctx.enter_context(nc.semaphore(name))

        ring = sb("ring", [P, RING, PIECE])
        xt = sb("xt", [P, TT, D])
        big = sb("big", [P, 4096])
        half = sb("half", [P, 2048])
        uT = sb("uT", [P, 3, HC, L])
        qkv = sb("qkv", [P, TT, QKV])
        kvc = sb("kvc", [P, CT, 2 * KVW])
        kT = sb("kT", [P, NKV, L + LC])
        work = sb("work", [P, 2560])
        gB = sb("gB", [P, 2, D])
        cols = sb("cols", [P, NCOLS])
        rows = sb("rows", [P, NR])
        konst = sb("konst", [P, NK])
        ones = sb("ones", [P, P])
        cc = sb("cc", [P, KD, 2])
        sig_c = sb("sig_c", [P, KD, 2])
        modc = sb("modc", [P, 32, 2])
        st = sb("st", [P, 192])
        tabs = sb("tabs", [P, BW])
        idx = sb("idx", [P, 2, BW], i32)
        blk = sb("blk", [1, BW + NE], i32)
        more = sb("more", [P, BW], i32)
        icur = sb("icur", [P, 2], i32)
        att_m = tabs[:, 0:32]
        att_m2 = st[:, 132:164]
        att_neg = sb("att_neg", [P, 32])
        att_l = idx[:, :, :].rearrange("p a b -> p (a b)")[:, 0:96].bitcast(f32).rearrange("p (a b) -> p a b", a=3)

        ident = konst[:, K_ID:K_ID + P]
        slab = ring[:, 4:6, :].rearrange("p a n -> p (a n)")
        dft = ring[:, 6:8, :].rearrange("p a n -> p (a n)").rearrange("p (t f) -> p t f", t=TT)
        idft = ring[:, 8:10, :].rearrange("p a n -> p (a n)").rearrange("p (f t) -> p f t", f=8)
        kspec = ring[:, 10:12, :].rearrange("p a n -> p (a n)").rearrange("p (f c) -> p f c", f=8)
        xn = ring[:, 8:10, :].rearrange("p a n -> p (a n)").rearrange("p (t d) -> p t d", t=TT)
        hT = big[:, :].rearrange("p (k t) -> p k t", k=KD)
        uspec = big[:, :].rearrange("p (f c) -> p f c", f=8)
        sq = big[:, :].rearrange("p (f c) -> p f c", f=8)
        hcT = half[:, :].rearrange("p (k t) -> p k t", k=KD)
        ztok = half[:, :].rearrange("p (t c) -> p t c", t=TT)
        decay, fa, fb = uT[:, 0], uT[:, 1], uT[:, 2]
        x0, z, v2 = uT[:, 0], uT[:, 1], uT[:, 2]
        cn = qkv[:, :, :].rearrange("p t n -> p (t n)")[:, 0:CT * D].rearrange("p (t d) -> p t d", t=CT)
        qT = slab[:, 0:2048].rearrange("p (j t) -> p j t", j=4)
        aT = slab[:, 2048:4096].rearrange("p (j t) -> p j t", j=4)
        w4 = work[0:64, 0:1024]
        zin = work[0:33, 1024:1536]
        fh = [work[0:64, 1536:2048], work[0:64, 2048:2560]]
        w1 = slab[0:33, 2048:2112]
        w23 = slab[0:64, 2112:2240].rearrange("p (a n) -> p a n", a=2)
        fcol = slab[0:64, 2240:2244]
        ftmp = [slab[0:64, 1024:1536], slab[0:64, 1536:2048]]
        fpair = slab[:, 0:1024].rearrange("p (a n) -> p a n", a=2)
        square = slab[:, 3072:4096]
        rot = [work[:, :].rearrange("p (t n) -> p t n", t=TT), slab[:, 0:2560].rearrange("p (t n) -> p t n", t=TT)]
        kd = slab[:, 2560:4096].rearrange("p (t k r d) -> p t k r d", t=TT + CT, k=NKV, r=2)
        ctxt = gB
        cs = slab[:, 2816:3072].rearrange("p (k m) -> p k m", k=KD)
        nrow = slab[:, 1024:1536]
        mrow_a = slab[:, 2304:2816]
        kflat = kT[:, :, :].rearrange("p a n -> p (a n)")
        sel = kflat[:, 0:512].rearrange("p (j m) -> p j m", j=4)
        mrow_b = [kflat[:, 512:1024], kflat[:, 1024:1536]]
        kz = [kT, half[:, 512:2048].rearrange("p (a n) -> p a n", a=NKV)]
        hn = xn
        bgu = work[:, 0:NE * 2 * KF].rearrange("p (e j) -> p e j", e=NE)
        wr = work[:, 512:768].rearrange("p (k e) -> p k e", k=KD)
        lgq = work[:, 2048:2560]
        wtmp = work[:, 1024:2048].rearrange("p (a n) -> p a n", a=2)
        moe = uT[:, :, :, :].rearrange("p a c n -> p (a c n)")
        xs = moe[:, 0:D]
        xsT = moe[:, 1024:2048].rearrange("p (k s) -> p k s", k=KD)
        gh = moe[:, 2048:3072].rearrange("p (k s) -> p k s", k=KF)
        yb = moe[:, 3072:4096]
        gu = moe[:, 4096:5120].rearrange("p (a q s) -> p a q s", a=2, q=4)
        sg = moe[:, 5120:5632].rearrange("p (a q s) -> p a q s", a=2, q=2)
        bd = half[0:NE, 0:D]
        ecur = half[0:NE, D:D + P]
        gq = moe[:, 2048:2304].rearrange("p (k s) -> p k s", k=4)
        gusb = qkv[:, :, :].rearrange("p t n -> p (t n)")[:, 0:1024].rearrange("p (g n) -> p g n", g=2)
        bcur = moe[:, 5632:5648]
        gcur = moe[:, 5648:5649]
        gcur2 = moe[:, 5649:5650]

        def pbuf(u):
            return ring[:, 8:10, :].rearrange("p a n -> p (a n)")[:, (u % 3) * 641:(u % 3 + 1) * 641]

        pt = [big[:, 0:2560].rearrange("p (j n) -> p j n", j=5), work[:, :].rearrange("p (j n) -> p j n", j=5)]
        asq = big[:, 0:2048].rearrange("p (j t) -> p j t", j=4)
        ar = big[:, 2048:2560]

        class R:
            a = big[:, :]
            b = uT[:, :, :, :].rearrange("p a c n -> p (a c n)")[:, 2048:6144]
            lg = a[:, 0:128].rearrange("p (t e) -> p t e", t=TT)
            v8 = a[:, 128:160].rearrange("p (t e) -> p t e", t=TT)
            i8 = a[:, 160:192].bitcast(u32).rearrange("p (t e) -> p t e", t=TT)
            i8f = a[:, 192:224].rearrange("p (t e) -> p t e", t=TT)
            ex = a[:, 224:240].rearrange("p (t k) -> p t k", t=TT)
            gate = a[:, 240:256].rearrange("p (t k) -> p t k", t=TT)
            OH = a[:, 256:768].rearrange("p (t k e) -> p t k e", t=TT, k=TOPK)
            M = a[:, 768:896].rearrange("p (t e) -> p t e", t=TT)
            OHS = a[:, 1024:1536].rearrange("p (t k e) -> p t k e", t=TT, k=TOPK)
            slot_of = a[:, 1536:1664].rearrange("p (t e) -> p t e", t=TT)
            slot = a[:, 1664:1680]
            GE = a[:, 1680:1680 + 16 * (BW + 1)].rearrange("p (i b) -> p i b", i=16)
            bs = a[:, 3400:3464]
            nb4 = a[0:NE, 2560:2564]
            nb = a[0:NE, 2564:2565]
            within = a[:, 2576:2592]
            sums = a[:, 3104:3120]
            tok = a[:, 3120:3120 + BW]
            S1 = b[:, 0:2048].rearrange("p (i s) -> p i s", i=16)
            B2 = b[:, 2048:2048 + 16 * 2 * BW].rearrange("p (i b) -> p i b", i=16)
            nbrep = b[0:NE, 3648:3776]
            blkcmp = qkv[0:1, :, :].rearrange("p t n -> p (t n)")[:, 0:BW * NE].rearrange("p (b e) -> p b e", b=BW)
            blkf = a[0:1, 3200:3200 + BW + 1]


        bank = [ctx.enter_context(nc.psum_tensor(f"bank{i}", [P, 512], f32)) for i in range(8)]

        names = """x_in cc_in small_in filter_in ctx_in dft_in idft_in decay_in chain_v chain_a chain_p ones_ok silu
            fnet_mm fnet_lin fnet_sin filt_mm filt_pair filt_tile filt_sq fspec_mm fspec_out nsum_mm nsum_out
            moda_out xn_ok cn_ok hT_mm hT_ok hcT_mm hcT_ok piece_used unit_mm unit_out modb_mm modb_out z_ok
            zT_mm zT_ok uspec_mm uspec_out yspec inv_mm y_ok ysq ysum_mm ysum_out yT_ok qk_ok qkT_mm qkT_ok s_mm
            s_max p_ok pT_mm pT_ok pv_mm a_ok aT_ok wo_mm xnew hn_ok hn_stored h2T_mm h2T_ok lg_mm route_exp
            route_shift cntc_mm nbrep bs_mm pos_mm onehot tab_mm acc_in lgq_mm lgq_ok tables ecur_ok pe_step
            free_ring gathered xsT_mm xsT_ok gu_mm sig gate_ready h_ok down_mm y_out scattered nrow_ok mrow_ok
            mcol_mm sel_ok kz_ok p_exp rl_ok asum_mm asum_out ar_sqrt asq qk_factor dve_step glu_p gu_sb gu_T
            late_in brow_in xs_sq y_mul yr_sqrt ns_lin ns_sqrt x_lin x_sqrt silu_s qk_lin qk_sqrt n2_sq n2_lin
            n2_sqrt pool_step""".split()
        S = {n: sem(n) for n in names}
        stream = [sem(f"stream{i}") for i in range(FRONT_RING)]
        full = [sem(f"full{i}") for i in range(RING)]

        block = ctx.enter_context(nc.Block())

        WS = (3, 4, 5, 6, 7, 8, 0, 1, 2)
        ORDER = [("A", k) for k in range(8)]
        for n, i in enumerate(WS):
            ORDER += [("W", i)] + ([("B", 2 * n), ("B", 2 * n + 1)] if n < 8 else [])
        ORDER += [("O", i) for i in range(4)]
        AT = {w: n for n, w in enumerate(ORDER)}

        def piece_src(what, i):
            if what == "A":
                return t_wmod[i * P:(i + 1) * P, 0:2048]
            if what == "W":
                return t_win.rearrange("(k p) n -> p k n", p=P)[:, :, i * 256:(i + 1) * 256]
            if what == "B":
                k, h = i // 2, i % 2
                return t_wmod[k * P:(k + 1) * P, 2048 + h * 2048:4096 + h * 2048]
            return t_wout[i * 256:(i + 1) * 256, :].rearrange("(c p) n -> p c n", p=P)

        def piece(what, i):
            return ring[:, AT[what, i] % FRONT_RING, :]

        def piece_ready(eng, what, i):
            n = AT[what, i]
            eng.wait_ge(stream[n % FRONT_RING], 16 * (n // FRONT_RING + 1))

        UNITS = ([(i, "u", c) for i in (3, 4, 5, 6, 7, 8) for c in range(2)]
                 + [(i, "q", t) for i in (0, 1) for t in range(TT)]
                 + [(2, "c", t) for t in range(CT)] + [(2, "q", t) for t in range(TT)])
        B_END = UNITS.index((1, "q", TT - 1))
        Z_AT = UNITS.index((2, "q", 0))
        def used(what, i):
            if what == "W":
                return S["unit_mm"], 1 + max(n for n, u in enumerate(UNITS) if u[0] == i)
            return S["piece_used"], i + 1 + (8 if what == "B" else 0)

        ATT = [(qb, h) for qb in range(TT) for h in range(NQ)]

        def local_keys(qb):
            return max(0, qb - 1) * P, min(TT, qb + 2) * P

        @contextmanager
        def blocks(eng, nblk):
            with eng.Fori(0, GROUPS) as g:
                with eng.If(g * GROUP < nblk):
                    with eng.Fori(0, GROUP) as i:
                        b = eng.snap(g * GROUP + i)
                        with eng.If(b < nblk):
                            yield b

        @block.sync
        def _(sp):
            sp.dma_start(zin, t_z).then_inc(S["filter_in"], 16)
            sp.dma_start(w1, t_w1).then_inc(S["filter_in"], 16)
            sp.dma_start(w23, t_w23).then_inc(S["filter_in"], 16)
            sp.dma_start(fcol, t_fcol).then_inc(S["filter_in"], 16)
            sp.dma_start(cc[:, :, :], t_cc).then_inc(S["cc_in"], 16)
            sp.dma_start(w4, t_w4).then_inc(S["filter_in"], 16)
            sp.dma_start(konst[:, :], t_konst).then_inc(S["small_in"], 16)
            sp.dma_start(cols[:, :], t_cols).then_inc(S["small_in"], 16)
            sp.dma_start(rows[:, :], t_rows.to_broadcast([P, NR])).then_inc(S["small_in"], 16)
            sp.dma_start(xt[:, :, :], t_x.rearrange("(t p) d -> p t d", p=P)).then_inc(S["x_in"], 16)
            sp.dma_start(ctxt[:, :, :], t_ctx.rearrange("(t p) d -> p t d", p=P)).then_inc(S["ctx_in"], 16)
            for n, w in enumerate(ORDER):
                if n == FRONT_RING:
                    sp.dma_start(decay, t_decay.rearrange("(t p) c -> p t c", p=P)).then_inc(S["decay_in"], 16)
                    sp.dma_start(dft[:, :, :], t_dft.rearrange("(t p) f -> p t f", p=P)).then_inc(S["dft_in"], 16)
                if n >= FRONT_RING:
                    sp.wait_ge(*used(*ORDER[n - FRONT_RING]))
                dst = ring[:, n % FRONT_RING, :]
                if w[0] == "W":
                    dst = dst.rearrange("p (k n) -> p k n", k=KD)
                if w[0] == "O":
                    dst = dst.rearrange("p (c n) -> p c n", c=2)
                sp.dma_start(dst, piece_src(*w)).then_inc(stream[n % FRONT_RING], 16)
                if w == ("W", 8):
                    sp.wait_ge(S["cn_ok"], CT)
                    sp.dma_start(gB[:, :, :].rearrange("p a n -> p (a n)"), t_brows.to_broadcast([P, 2 * D])).then_inc(S["brow_in"], 16)
                    sp.wait_ge(S["hT_mm"], KD)
                    sp.dma_start(idft[:, :, :], t_idft.rearrange("(f p) t -> p f t", p=P)).then_inc(S["idft_in"], 16)

            def load(e, s):
                if s < KD:
                    src = t_wgu[bass.ds(e * KD + s, 1), :, :].rearrange("o p n -> (o p) n")
                    sp.dma_start(ring[:, s, :], src).then_inc(full[s], 16)
                else:
                    src = t_wdown[bass.ds(e * 4 + s - KD, 1), :, :, :].rearrange("o c p n -> p (o c) n")
                    sp.dma_start(ring[:, s, :].rearrange("p (c n) -> p c n", c=2), src).then_inc(full[s], 16)

            sp.wait_ge(S["uspec_mm"], 8)
            for s in (6, 7):
                load(0, s)
            sp.wait_ge(S["yspec"], 4)
            for s in (10, 11):
                load(0, s)
            sp.wait_ge(S["a_ok"], TT)
            sp.dma_start(bgu, t_bgu).then_inc(S["late_in"], 16)
            sp.dma_start(wr, t_wr.rearrange("(k p) e -> p k e", p=P)).then_inc(S["late_in"], 16)
            sp.wait_ge(S["yT_ok"], HC)
            sp.dma_start(bd, t_bdown).then_inc(S["late_in"], 16)

            sp.wait_ge(S["wo_mm"], TT)
            sp.wait_ge(S["n2_sq"], 1)
            for s in range(6):
                load(0, s)
            sp.wait_ge(S["hn_stored"], 16 * TT)
            sp.wait_ge(S["h2T_mm"], KD)
            for s in (8, 9):
                load(0, s)
            sp.wait_ge(S["tables"], 2)
            with sp.Fori(1, NE) as e:
                prev = sp.value_load(blk[0:1, bass.ds(e + (BW - 1), 1)], min_val=0, max_val=BLOCKS - 1)
                for s in range(RING):
                    if s == KD - 1:
                        sp.wait_ge(S["gu_mm"], prev * 4 + 4)
                    elif s == RING - 1:
                        sp.wait_ge(S["down_mm"], prev + 1)
                    else:
                        sp.wait_ge(S["free_ring"], prev * (RING - 2) + (s + 1 if s < KD else s))
                    load(e, s)

        @block.tensor
        def _(pe):
            mm, tr = nc.tensor.matmul, nc.tensor.transpose
            pe.wait_ge(S["filter_in"], 80)
            mm(bank[7][0:64, :], w1, zin, start=True, stop=True).then_inc(S["fnet_mm"], 1)
            for i in range(2):
                pe.wait_ge(S["fnet_sin"], i + 1)
                mm(bank[7][0:64, :], w23[:, i, :], fh[i], start=True, stop=True).then_inc(S["fnet_mm"], 1)

            def modulation(ks):
                for k in ks:
                    piece_ready(pe, "A", k)
                    for j in range(4):
                        last = mm(bank[0][32 * j:32 * j + 32, :], cs[:, k, :], piece("A", k)[:, j * 512:(j + 1) * 512],
                                  start=k == 0, stop=k == 7)
                    last.then_inc(S["piece_used"], 1)

            pe.wait_ge(S["silu"], 1)
            modulation(range(4))
            pe.wait_ge(S["fnet_sin"], 3)
            for t in range(TT):
                if t >= 2:
                    pe.wait_ge(S["filt_pair"], t - 1)
                for h in range(2):
                    last = mm(bank[1 + 2 * (t % 2) + h][:, :], fh[0][:, t * P:(t + 1) * P],
                              w4[:, h * HW:(h + 1) * HW], start=True, stop=True)
                last.then_inc(S["filt_mm"], 1)
            modulation(range(4, 8))
            pe.wait_ge(S["filt_tile"], TT)
            pe.wait_ge(S["dft_in"], 16)
            for f in range(9):
                src = fa if f < 4 or f == 8 else fb
                if f >= 3:
                    pe.wait_ge(S["fspec_out"], f - 2)
                dst = bank[5 + f % 3]
                for t in range(TT):
                    if f < 8:
                        last = mm(dst[:, :], dft[:, t, f * P:(f + 1) * P], src[:, t, :], start=t == 0, stop=t == TT - 1)
                    else:
                        last = mm(dst[0:1, :], dft[:, t, L:L + 1], src[:, t, :], start=t == 0, stop=t == TT - 1)
                last.then_inc(S["fspec_mm"], 1)
            pe.wait_ge(S["filt_sq"], 2 * TT)
            pe.wait_ge(S["ones_ok"], 1)
            for n in range(2 * TT):
                g = 32 * (n % 4)
                last = mm(bank[1][g:g + 32, :], ones[:, 0:32], sq[:, n, :], start=n < 4, stop=n >= 4)
            last.then_inc(S["nsum_mm"], 1)
            pe.wait_ge(S["nrow_ok"], 1)
            for c in range(HC):
                last = mm(bank[1][:, c:c + 1], nrow[:, c * P:(c + 1) * P], konst[:, K_Q4:K_Q4 + 1], start=True, stop=True)
            last.then_inc(S["nsum_mm"], 1)
            pe.wait_ge(S["mrow_ok"], 1)
            for q in range(4):
                last = tr(bank[0][:, q * P:(q + 1) * P], mrow_a[:, q * P:(q + 1) * P], ident)
            last.then_inc(S["mcol_mm"], 1)
            pe.wait_ge(S["xn_ok"], TT)
            pe.wait_ge(S["fspec_out"], 9)
            pe.wait_ge(S["filt_pair"], TT)
            for k in range(KD):
                if k >= 4:
                    pe.wait_ge(S["hT_ok"], k - 3)
                for t in range(TT):
                    last = tr(bank[2 + k % 4][:, t * P:(t + 1) * P], xn[:, t, k * P:(k + 1) * P], ident)
                last.then_inc(S["hT_mm"], 1)
            pe.wait_ge(S["cn_ok"], CT)
            for k in range(KD):
                if k >= 2:
                    pe.wait_ge(S["hcT_ok"], k - 1)
                for t in range(CT):
                    last = tr(bank[6 + k % 2][:, t * P:(t + 1) * P], cn[:, t, k * P:(k + 1) * P], ident)
                last.then_inc(S["hcT_mm"], 1)
            pe.wait_ge(S["hT_ok"], KD)
            pe.wait_ge(S["hcT_ok"], KD)
            pe.wait_ge(S["moda_out"], 1)
            pe.wait_ge(S["nsum_out"], 1)
            for n, (i, kind, c) in enumerate(UNITS):
                if n >= 4:
                    pe.wait_ge(S["unit_out"], n - 3)
                if n == 0 or UNITS[n - 1][0] != i:
                    piece_ready(pe, "W", i)
                w = piece("W", i).rearrange("p (k n) -> p k n", k=KD)
                for k in range(KD):
                    a, z0 = k == 0, k == KD - 1
                    if kind == "u":
                        last = mm(bank[n % 4][:, :], w[:, k, c * P:(c + 1) * P], hT[:, k, :], start=a, stop=z0)
                    elif kind == "q":
                        last = mm(bank[n % 4][:, 0:256], hT[:, k, c * P:(c + 1) * P], w[:, k, :], start=a, stop=z0)
                    else:
                        last = mm(bank[n % 4][:, 0:256], hcT[:, k, c * P:(c + 1) * P], w[:, k, :], start=a, stop=z0)
                last.then_inc(S["unit_mm"], 1)
                if n == Z_AT:
                    pe.wait_ge(S["mrow_ok"], 3)
                    pe.wait_ge(S["z_ok"], HC)
                    for t in range(TT):
                        for d in range(HC):
                            last = tr(bank[4 + t][:, d * P:(d + 1) * P], z[:, d, t * P:(t + 1) * P], ident)
                        last.then_inc(S["zT_mm"], 1)
                n_w = WS.index(i)
                if n_w < 8 and UNITS[n + 1][0] != i:
                    for m in (2 * n_w, 2 * n_w + 1):
                        k, h = m // 2, m % 2
                        piece_ready(pe, "B", m)
                        for j in range(4):
                            last = mm(bank[6 + h][32 * j:32 * j + 32, :], cs[:, k, :], piece("B", m)[:, j * 512:(j + 1) * 512],
                                      start=k == 0, stop=k == 7)
                        last.then_inc(S["piece_used"], 1)
            pe.wait_ge(S["zT_ok"], TT)
            pe.wait_ge(S["unit_out"], len(UNITS))
            for n in range(8):
                f = n // 2 + 4 * (n % 2)
                if n >= 4:
                    pe.wait_ge(S["uspec_out"], n - 3)
                for t in range(TT):
                    last = mm(bank[n % 4][:, :], dft[:, t, f * P:(f + 1) * P], ztok[:, t, :], start=t == 0, stop=t == TT - 1)
                last.then_inc(S["uspec_mm"], 1)
            for h in range(2):
                for q in range(4):
                    last = tr(bank[4 + h][:, q * P:(q + 1) * P], mrow_b[h][:, q * P:(q + 1) * P], ident)
            pe.wait_ge(S["uspec_out"], 8)
            pe.wait_ge(S["sel_ok"], 1)
            for n, (h, j) in enumerate(((0, 0), (0, 1), (1, 2), (1, 3))):
                last = mm(bank[(6, 7, 0, 1)[n]][:, :], sel[:, j, :], mrow_b[h], start=True, stop=True)
            last.then_inc(S["modb_mm"], 1)
            pe.wait_ge(S["yspec"], 4)
            pe.wait_ge(S["idft_in"], 16)
            for c in range(HC):
                if c >= 2:
                    pe.wait_ge(S["y_ok"], c - 1)
                for f in range(8):
                    last = mm(bank[2 + c % 2][:, :], uspec[:, f, c * P:(c + 1) * P], idft[:, f, :], start=f == 0, stop=f == 7)
                last.then_inc(S["inv_mm"], 1)
            pe.wait_ge(S["ysq"], HC)
            for c in range(HC):
                last = mm(bank[7][:, :], ones[:, :], ztok[:, c, :], start=c == 0, stop=c == HC - 1)
            last.then_inc(S["ysum_mm"], 1)
            pe.wait_ge(S["qk_ok"], 1)
            pe.wait_ge(S["modb_out"], 1)
            n = 0
            for j in range(8):
                if j >= 4:
                    pe.wait_ge(S["qkT_ok"], j - 3)
                dst = bank[j % 4]
                if j < 4:
                    for t in range(TT):
                        last = tr(dst[:, t * P:(t + 1) * P], qkv[:, t, j * P:(j + 1) * P], ident)
                else:
                    kv, part = (j - 4) // 2, (j - 4) % 2
                    for t in range(TT if part == 0 else CT):
                        last = tr(dst[:, t * P:(t + 1) * P], kd[:, t + TT * part, kv].rearrange("p r d -> p (r d)"), ident)
                last.then_inc(S["qkT_mm"], 1)
            pe.wait_ge(S["qkT_ok"], 8)
            pe.wait_ge(S["y_ok"], HC)
            pe.wait_ge(S["ysum_out"], 1)

            pe.wait_ge(S["kz_ok"], 2)

            def scores(u):
                qb, h = ATT[u]
                lo, hi = local_keys(qb)
                if u >= 2:
                    pe.wait_ge(S["p_exp"], u - 1)
                q, k = qT[:, h // 2, qb * P:(qb + 1) * P], kz[h % 2]
                mm(bank[2 * (u % 2)][:, 0:hi - lo], q, k[:, h // 4, lo:hi], start=True, stop=True)
                mm(bank[2 * (u % 2) + 1][:, 0:LC], q, k[:, h // 4, L:L + LC], start=True, stop=True)\
                    .then_inc(S["s_mm"], 1)

            def weights_T(u):
                qb, h = ATT[u]
                lo, hi = local_keys(qb)
                pe.wait_ge(S["p_ok"], u + 1)
                if u >= 1:
                    pe.wait_ge(S["pT_ok"], u)
                for j in range((hi - lo + LC) // P):
                    dst = bank[4][:, j * P:(j + 1) * P] if j < 4 else bank[5][:, 0:P]
                    last = tr(dst, pbuf(u)[:, 1 + j * P:1 + (j + 1) * P], ident)
                last.then_inc(S["pT_mm"], 1)

            def values(qb):
                lo, hi = local_keys(qb)
                pe.wait_ge(S["pT_ok"], NQ * qb + NQ)
                if qb >= 2:
                    pe.wait_ge(S["a_ok"], qb - 1)
                n = (hi - lo) // P
                for j in range(n + CT):
                    for kv in range(NKV):
                        v = (qkv[:, lo // P + j, AW + KVW + kv * HD:AW + KVW + (kv + 1) * HD] if j < n
                             else kvc[:, j - n, KVW + kv * HD:KVW + (kv + 1) * HD])
                        last = mm(bank[6 + qb % 2][64 * kv:64 * kv + 64, :], v, pt[kv][:, j, :],
                                  start=j == 0, stop=j == n + CT - 1)
                last.then_inc(S["pv_mm"], 1)

            scores(0)
            for u in range(len(ATT) + 2):
                if u + 1 < len(ATT):
                    scores(u + 1)
                if u >= 2:
                    weights_T(u - 2)
                if u > NQ and u % NQ == 2:
                    values(u // NQ - 1)
            values(TT - 1)
            pe.wait_ge(S["asq"], 4)
            for c in range(4):
                last = mm(bank[0][:, :], ones[:, :], asq[:, c, :], start=c == 0, stop=c == 3)
            last.then_inc(S["asum_mm"], 1)
            pe.wait_ge(S["yT_ok"], HC)
            for i in range(4):
                piece_ready(pe, "O", i)
            for part in range(2):
                for t in range(TT):
                    if part == 0 and t == 3:
                        pe.wait_ge(S["asum_out"], 1)
                    if part == 1 and t == 0:
                        pe.wait_ge(S["aT_ok"], 4)
                    for n in range(2):
                        for c in range(4):
                            w = piece("O", 2 * (1 - part) + c // 2)[:, (c % 2) * D + n * 512:(c % 2) * D + (n + 1) * 512]
                            src = (v2, aT)[part][:, c, t * P:(t + 1) * P]
                            last = mm(bank[(2 * t + 2 + n) % 8][:, :], src, w, start=part == 0 and c == 0, stop=part == 1 and c == 3)
                    if part == 1:
                        last.then_inc(S["wo_mm"], 1)
            pe.wait_ge(S["hn_ok"], TT)
            for k in range(KD):
                if k >= 4:
                    pe.wait_ge(S["h2T_ok"], k - 3)
                for t in range(TT):
                    last = tr(bank[k % 4][:, t * P:(t + 1) * P], hn[:, t, k * P:(k + 1) * P], ident)
                last.then_inc(S["h2T_mm"], 1)
            pe.wait_ge(S["h2T_ok"], KD)
            pe.wait_ge(S["late_in"], 48)
            for k in range(KD):
                g = NE * (k % 4)
                last = mm(bank[5][g:g + NE, :], wr[:, k, :], hT[:, k, :], start=k < 4, stop=k >= 4)
            last.then_inc(S["lgq_mm"], 1)
            pe.wait_ge(S["lgq_ok"], 1)
            for t in range(TT):
                last = mm(bank[4][:, t * NE:(t + 1) * NE], lgq[:, t * P:(t + 1) * P], konst[:, K_S4:K_S4 + NE], start=True, stop=True)
            last.then_inc(S["lg_mm"], 1)
            pe.wait_ge(S["onehot"], 1)
            for t in range(TT):
                last = mm(bank[5][0:NE, 0:1], R.M[:, t, :], ones[:, 0:1], start=t == 0, stop=t == TT - 1)
            last.then_inc(S["cntc_mm"], 1)
            for t in range(TT):
                for s in range(t + 1):
                    last = mm(bank[6][:, t * NE:(t + 1) * NE], ones[:, :] if s < t else konst[:, K_TRI:K_TRI + P],
                              R.M[:, s, :], start=s == 0, stop=s == t)
            last.then_inc(S["pos_mm"], 1)
            pe.wait_ge(S["nbrep"], 1)
            mm(bank[7][:, 0:2 * NE], R.nbrep, konst[0:NE, K_TRE:K_TRE + 2 * NE], start=True, stop=True).then_inc(S["bs_mm"], 1)
            pe.wait_ge(S["onehot"], 2)
            for i in range(TT * TOPK):
                last = mm(bank[5][:, 0:2 * BW], R.S1[:, i, :], R.B2[:, i, :], start=i == 0, stop=i == TT * TOPK - 1)
            last.then_inc(S["tab_mm"], 1)
            def slots_T():
                for k in range(KD):
                    last = tr(bank[6 + k // 4][:, (k % 4) * P:(k % 4 + 1) * P], xs[:, k * P:(k + 1) * P], ident)
                last.then_inc(S["xsT_mm"], 1)

            pe.wait_ge(S["tables"], 2)
            pe.wait_ge(S["gathered"], 16)
            slots_T()
            nblk = pe.value_load(blk[0:1, BW + NE - 1:BW + NE], min_val=0, max_val=BLOCKS - 1) + 1
            with blocks(pe, nblk) as b:
                e = pe.value_load(blk[0:1, bass.ds(b, 1)], min_val=0, max_val=NE - 1)
                many = pe.value_load(more[HALF:HALF + 1, bass.ds(b, 1)], min_val=0, max_val=1)
                pe.wait_ge(S["xsT_ok"], 2 * b + 2)
                with pe.If(many > 0):
                    for k in range(KD):
                        pe.wait_ge(full[k], 16 * e + 16)
                        for i in range(4):
                            if k == 0:
                                pe.wait_ge(S["gate_ready"], 4 * b + i + 1)
                            for q in range(4):
                                f = (q % 2) * FF + (2 * i + q // 2) * P
                                last = mm(bank[i][:, q * P:(q + 1) * P], ring[:, k, f:f + P], xsT[:, k, :],
                                          start=k == 0 and q == 0, stop=k == KD - 1, skip_group_check=True)
                            if k == KD - 1:
                                last.then_inc(S["gu_mm"], 1)
                        if k < KD - 1:
                            last.then_inc(S["free_ring"], 1)
                    pe.sem_inc(S["gu_T"], 4)
                    pe.wait_ge(S["gathered"], 16 * b + 32)
                    slots_T()
                    pe.wait_ge(S["y_out"], b + 1)
                    pe.wait_ge(S["ecur_ok"], b + 1)
                    for n in range(2):
                        mm(bank[4 + n][:, :], ecur, bd[:, n * 512:(n + 1) * 512], start=True, stop=False)
                    for s in range(4):
                        pe.wait_ge(S["h_ok"], 4 * b + s + 1)
                        pe.wait_ge(full[KD + s], 16 * e + 16)
                        for c in range(2):
                            for n in range(2):
                                last = mm(bank[4 + n][:, :], gh[:, 2 * s + c, :],
                                          ring[:, KD + s, c * D + n * 512:c * D + (n + 1) * 512],
                                          start=False, stop=s + c == 4)
                        last.then_inc(S["free_ring" if s < 3 else "down_mm"], 1)
                with pe.Else():
                    some = pe.value_load(more[QUART:QUART + 1, bass.ds(b, 1)], min_val=0, max_val=1)
                    with pe.If(some > 0):
                        for k in range(KD):
                            pe.wait_ge(full[k], 16 * e + 16)
                            for g in range(2):
                                if k == 0:
                                    pe.wait_ge(S["gate_ready"], 4 * b + g + 1)
                                for n in range(2):
                                    last = mm(bank[g][HALF * n:HALF * (n + 1), :], xsT[:, k, 0:HALF],
                                              ring[:, k, g * FF + n * 512:g * FF + (n + 1) * 512],
                                              start=k == 0, stop=k == KD - 1)
                                if k == KD - 1:
                                    last.then_inc(S["gu_mm"], 2)
                            if k < KD - 1:
                                last.then_inc(S["free_ring"], 1)
                        pe.wait_ge(S["gathered"], 16 * b + 32)
                        slots_T()
                        for i in range(2):
                            pe.wait_ge(S["gate_ready"], 4 * b + 3 + i)
                            pe.wait_ge(S["gu_sb"], 2 * b + 2)
                            for q in range(4):
                                last = tr(bank[2 + i][:, q * P:(q + 1) * P],
                                          gusb[:, q % 2, (2 * i + q // 2) * P:(2 * i + q // 2 + 1) * P], ident)
                            last.then_inc(S["gu_T"], 2)
                        pe.wait_ge(S["y_out"], b + 1)
                        pe.wait_ge(S["ecur_ok"], b + 1)
                        for n in range(2):
                            mm(bank[4][HALF * n:HALF * (n + 1), :], ecur[:, 0:HALF], bd[:, n * 512:(n + 1) * 512], start=True, stop=False)
                        for s in range(4):
                            pe.wait_ge(S["h_ok"], 4 * b + (2 if s == 0 else 4))
                            pe.wait_ge(full[KD + s], 16 * e + 16)
                            for c in range(2):
                                f = 2 * s + c
                                for n in range(2):
                                    last = mm(bank[4][HALF * n:HALF * (n + 1), :], gh[:, f % 4, HALF * (f // 4):HALF * (f // 4 + 1)],
                                              ring[:, KD + s, c * D + n * 512:c * D + (n + 1) * 512],
                                              start=False, stop=f == KF - 1)
                            last.then_inc(S["free_ring" if s < 3 else "down_mm"], 1)
                    with pe.Else():
                        for k in range(KD):
                            pe.wait_ge(full[k], 16 * e + 16)
                            if k == 0:
                                pe.wait_ge(S["gate_ready"], 4 * b + 4)
                            for m in range(4):
                                last = mm(bank[0][QUART * m:QUART * (m + 1), :], xsT[:, k, 0:QUART],
                                          ring[:, k, m * 512:(m + 1) * 512], start=k == 0, stop=k == KD - 1)
                            last.then_inc(*((S["free_ring"], 1) if k < KD - 1 else (S["gu_mm"], 4)))
                        pe.wait_ge(S["gathered"], 16 * b + 32)
                        slots_T()
                        pe.wait_ge(S["gu_sb"], 2 * b + 2)
                        for q in range(4):
                            last = tr(bank[2][:, q * P:(q + 1) * P], gusb[:, 0, q * P:(q + 1) * P], ident)
                        last.then_inc(S["gu_T"], 4)
                        pe.wait_ge(S["y_out"], b + 1)
                        pe.wait_ge(S["ecur_ok"], b + 1)
                        pe.sem_inc(S["pe_step"], 1)
                        for m in range(4):
                            mm(bank[4][QUART * m:QUART * (m + 1), 0:256], ecur[:, 0:QUART], bd[:, m * 256:(m + 1) * 256], start=True, stop=False)
                        pe.wait_ge(S["h_ok"], 4 * b + 4)
                        for s in range(4):
                            pe.wait_ge(full[KD + s], 16 * e + 16)
                            for c in range(2):
                                f = 2 * s + c
                                for m in range(4):
                                    last = mm(bank[4][QUART * m:QUART * (m + 1), 0:256], gq[:, f % 4, QUART * (f // 4):QUART * (f // 4 + 1)],
                                              ring[:, KD + s, c * D + m * 256:c * D + (m + 1) * 256],
                                              start=False, stop=f == KF - 1)
                            last.then_inc(S["free_ring" if s < 3 else "down_mm"], 1)

        @block.vector
        def _(v):
            dve = nc.vector
            steps = [0]

            def link(ins):
                steps[0] += 1
                ins.then_inc(S["chain_v"], 1)
                v.wait_ge(S["chain_v"], steps[0])

            v.wait_ge(S["filter_in"], 80)
            for i in range(3):
                v.wait_ge(S["fnet_mm"], i + 1)
                a, n = ftmp
                link(dve.tensor_scalar(a, bank[7][0:64, :], fcol[:, i:i + 1], fcol[:, 3:4], ALU.add, ALU.mult))
                link(dve.tensor_scalar(n, a, 1.0 / (TWO_PI_HI + TWO_PI_LO), ROUND, ALU.mult, ALU.add))
                link(dve.tensor_scalar(n, n, -ROUND, None, ALU.add))
                link(dve.scalar_tensor_tensor(a, n, -TWO_PI_HI, a, ALU.mult, ALU.add))
                link(dve.scalar_tensor_tensor(a, n, -TWO_PI_LO, a, ALU.mult, ALU.add))
                dve.tensor_scalar(a, a, PI_BOUND, -PI_BOUND, ALU.min, ALU.max).then_inc(S["fnet_lin"], 1)
                if i == 0:
                    v.wait_ge(S["silu_s"], 1)
                    link(dve.memset(cs, 0.0))
                    dve.tensor_tensor(cs[:, :, 0:2], cc[:, :, :], sig_c[:, :, :], ALU.mult).then_inc(S["silu"], 1)
            v.wait_ge(S["small_in"], 48)
            for j in range(4):
                last = dve.tensor_copy(sel[:, j], konst[:, K_ID + 32 * j:K_ID + 32 * j + 1].to_broadcast([P, P]))
            last.then_inc(S["sel_ok"], 1)
            v.wait_ge(S["xs_sq"], 1)
            dve.tensor_scalar(st[:, 0:6], st[:, 0:6], 1.0 / D, EPS, ALU.mult, ALU.add).then_inc(S["x_lin"], 1)
            v.wait_ge(S["decay_in"], 16)
            for t in range(TT):
                v.wait_ge(S["filt_mm"], t + 1)
                dve.tensor_tensor(fpair[:, 0], bank[1 + 2 * (t % 2)][:, :], decay[:, t], ALU.mult)
                dve.tensor_tensor(fpair[:, 1], bank[2 + 2 * (t % 2)][:, :], decay[:, t], ALU.mult).then_inc(S["filt_pair"], 1)
                v.wait_ge(S["filt_pair"], t + 1)
                if t == 0:
                    link(dve.memset(fpair[0:1, 1, :], 0.0))
                link(dve.tensor_tensor(fa[:, t], fpair[:, 0], fpair[:, 1], ALU.add))
                dve.tensor_tensor(fb[:, t], fpair[:, 0], fpair[:, 1], ALU.subtract).then_inc(S["filt_tile"], 1)
                v.wait_ge(S["filt_tile"], t + 1)
            v.wait_ge(S["x_sqrt"], 1)
            link(dve.reciprocal(st[:, 8:14], st[:, 0:6]))
            for t in range(TT):
                dve.tensor_scalar(xn[:, t], xt[:, t], st[:, 8 + t:9 + t], None, ALU.mult).then_inc(S["xn_ok"], 1)
            for t in range(CT):
                dve.tensor_scalar(cn[:, t], ctxt[:, t], st[:, 12 + t:13 + t], None, ALU.mult).then_inc(S["cn_ok"], 1)
            v.wait_ge(S["nsum_mm"], 2)
            dve.tensor_scalar(st[:, 16:20], bank[1][:, 0:HC], 0.5, EPS, ALU.mult, ALU.add).then_inc(S["ns_lin"], 1)
            v.wait_ge(S["ns_sqrt"], 1)
            dve.reciprocal(st[:, 20:24], st[:, 16:20]).then_inc(S["nsum_out"], 1)
            v.wait_ge(S["mcol_mm"], 1)
            def by_chunk(ap, j):
                return ap.rearrange("p (q j m) -> p j q m", q=4, j=4)[:, j:j + 2, :, 0:2] if j is not None else \
                    ap.rearrange("p (q j m) -> p j q m", q=4, j=4)[:, :, :, 0:2]

            def chunks(ap, n):
                return ap.rearrange("p (j q) -> p j q", q=4).unsqueeze(3).to_broadcast([P, n, 4, 2])

            link(dve.tensor_tensor(modc[:, 0:16, :].rearrange("p (j q) m -> p j q m", q=4), by_chunk(bank[0][:, :], None),
                                   chunks(cols[:, C_BMOD:C_BMOD + 16], 4), ALU.add))
            link(dve.tensor_scalar(modc[:, 8:16, :], modc[:, 8:16, :], 1.0, None, ALU.add))
            dve.tensor_tensor(modc[:, 8:16, :], modc[:, 8:16, :],
                              cols[:, C_N1:C_N1 + 8].unsqueeze(2).to_broadcast([P, 8, 2]), ALU.mult).then_inc(S["moda_out"], 1)
            v.wait_ge(S["moda_out"], 1)
            for k in range(KD):
                v.wait_ge(S["hT_mm"], k + 1)
                dve.tensor_scalar(hT[:, k, :], bank[2 + k % 4][:, :], modc[:, 8 + k, 0:1], modc[:, k, 0:1],
                                  ALU.mult, ALU.add).then_inc(S["hT_ok"], 1)
            uflat = uT[:, :, :, :].rearrange("p a c n -> p (a c) n")
            for n in range(3 * HC):
                v.wait_ge(S["unit_mm"], n + 1)
                src, dst = bank[n % 4], uflat[:, n]
                tap = [cols[:, C_CW + 12 * i + n:C_CW + 12 * i + n + 1] for i in range(3)]
                link(dve.tensor_scalar(dst, src[:, :], tap[1], cols[:, C_CB + n:C_CB + n + 1], ALU.mult, ALU.add))
                link(dve.scalar_tensor_tensor(dst[:, 1:L], src[:, 0:L - 1], tap[0], dst[:, 1:L], ALU.mult, ALU.add))
                dve.scalar_tensor_tensor(dst[:, 0:L - 1], src[:, 1:L], tap[2], dst[:, 0:L - 1], ALU.mult, ALU.add)\
                   .then_inc(S["unit_out"], 1)
                v.wait_ge(S["unit_out"], n + 1)
            for c in range(HC):
                dve.tensor_tensor(z[:, c], z[:, c], v2[:, c], ALU.mult).then_inc(S["z_ok"], 1)
            v.wait_ge(S["unit_out"], len(UNITS))
            qk = qkv[:, :, 0:AW + KVW]
            qk4 = qk.rearrange("p t (h d) -> p t h d", d=HD)
            kc = kvc[:, :, 0:KVW]
            kc4 = kc.rearrange("p t (h d) -> p t h d", d=HD)
            kc_sq = rot[1][:, 0:CT, 0:KVW]
            dve.tensor_tensor(rot[0], qk, qk, ALU.mult)
            link(dve.tensor_tensor(kc_sq, kc, kc, ALU.mult))
            dve.tensor_reduce(st[:, 32:72].rearrange("p (t h) -> p t h", t=TT), rot[0].rearrange("p t (h d) -> p t h d", d=HD), X, ALU.add)
            link(dve.tensor_reduce(st[:, 72:76].rearrange("p (t h) -> p t h", t=CT), kc_sq.rearrange("p t (h d) -> p t h d", d=HD), X, ALU.add))
            dve.tensor_scalar(st[:, 32:76], st[:, 32:76], 1.0 / HD, EPS, ALU.mult, ALU.add).then_inc(S["qk_lin"], 1)
            v.wait_ge(S["qk_sqrt"], 1)
            dve.reciprocal(st[:, 80:124], st[:, 32:76]).then_inc(S["qk_factor"], 1)
            v.wait_ge(S["fspec_out"], 9)
            t1, t2, keep = v2[:, 0], v2[:, 1], v2[0:1, 2]
            for f in range(4):
                v.wait_ge(S["uspec_out"], 2 * f + 2)
                ur, ui, kr, ki = uspec[:, f], uspec[:, 4 + f], kspec[:, f], kspec[:, 4 + f]
                dve.tensor_tensor(t1, ui, ki, ALU.mult)
                link(dve.tensor_tensor(t2, ur, ki, ALU.mult))
                if f == 0:
                    link(dve.tensor_copy(keep, t1[0:1, :]))
                    link(dve.memset(t1[0:1, :], 0.0))
                dve.tensor_tensor(ur, ur, kr, ALU.mult)
                link(dve.tensor_tensor(ui, ui, kr, ALU.mult))
                dve.tensor_tensor(ur, ur, t1, ALU.subtract)
                if f == 0:
                    link(dve.tensor_tensor(ui, ui, t2, ALU.add))
                    dve.tensor_copy(ui[0:1, :], keep).then_inc(S["yspec"], 1)
                else:
                    dve.tensor_tensor(ui, ui, t2, ALU.add).then_inc(S["yspec"], 1)
                v.wait_ge(S["yspec"], f + 1)
            v.wait_ge(S["modb_mm"], 1)
            v.wait_ge(S["brow_in"], 16)
            for h in range(2):
                for n in range(2):
                    g = gB[:, h, n * 512:(n + 1) * 512]
                    dve.tensor_tensor(g, g, bank[(6, 7, 0, 1)[2 * h + n]][:, :], ALU.add)
            for h in range(2):
                dst = modc[:, 16 + 8 * h:24 + 8 * h, :].rearrange("p (j q) m -> p j q m", q=4)
                last = dve.tensor_tensor(dst, by_chunk(bank[4 + h][:, :], 2 - 2 * h),
                                         chunks(cols[:, C_BMOD + 24 + 8 * h:C_BMOD + 32 + 8 * h], 2), ALU.add)
            link(last)
            link(dve.tensor_scalar(modc[:, 24:32, :], modc[:, 24:32, :], 1.0, None, ALU.add))
            dve.tensor_tensor(modc[:, 24:32, :], modc[:, 24:32, :],
                              cols[:, C_N2:C_N2 + 8].unsqueeze(2).to_broadcast([P, 8, 2]), ALU.mult).then_inc(S["modb_out"], 1)
            for c in range(HC):
                link(dve.tensor_scalar(z[:, c], z[:, c], cols[:, C_FB + c:C_FB + c + 1], None, ALU.mult))
                v.wait_ge(S["inv_mm"], c + 1)
                dve.scalar_tensor_tensor(v2[:, c], bank[2 + c % 2][:, :], st[:, 20 + c:21 + c], z[:, c], ALU.mult, ALU.add).then_inc(S["y_ok"], 1)
                v.wait_ge(S["y_ok"], c + 1)
                dve.tensor_tensor(v2[:, c], v2[:, c], x0[:, c], ALU.mult).then_inc(S["y_mul"], 1)
            yr = half[:, 0:512]
            v.wait_ge(S["ysum_mm"], 1)
            dve.tensor_scalar(yr, bank[7][:, :], 1.0 / HW, EPS, ALU.mult, ALU.add).then_inc(S["ysum_out"], 1)
            v.wait_ge(S["yr_sqrt"], 1)
            link(dve.reciprocal(yr, yr))
            for c in range(HC):
                dve.scalar_tensor_tensor(v2[:, c], v2[:, c], cols[:, C_HG + c:C_HG + c + 1], yr, ALU.mult, ALU.mult).then_inc(S["yT_ok"], 1)
            sink8 = st[:, 124:132]
            link(dve.tensor_scalar(sink8, rows[:, R_SINK:R_SINK + NQ], 1.0 / ATTN_SCALE, None, ALU.mult))
            top, top2, neg = att_m, att_m2, att_neg

            def maxima(u):
                qb, h = ATT[u]
                lo, hi = local_keys(qb)
                v.wait_ge(S["s_mm"], u + 1)
                if u >= 3:
                    v.wait_ge(S["pT_mm"], u - 2)
                m0 = K_MASK + (P if qb == 0 else 0)
                dve.tensor_copy(pbuf(u)[:, 0:1], sink8[:, h:h + 1])
                dve.tensor_tensor_reduce(out=pbuf(u)[:, 1:1 + hi - lo], in0=bank[2 * (u % 2)][:, 0:hi - lo],
                                         in1=konst[:, m0:m0 + hi - lo], scale=1.0, scalar=sink8[:, h:h + 1],
                                         op0=ALU.add, op1=ALU.max, accum_out=top[:, u:u + 1])
                link(dve.tensor_reduce(top2[:, u:u + 1], bank[2 * (u % 2) + 1][:, 0:LC], X, ALU.max))
                dve.tensor_scalar(neg[:, u:u + 1], top[:, u:u + 1], top2[:, u:u + 1], -ATTN_SCALE, ALU.max, ALU.mult)\
                   .then_inc(S["s_max"], 1)

            def factor(u):
                v.wait_ge(S["p_exp"], u + 1)
                link(dve.tensor_tensor(att_l[:, 2, u:u + 1], att_l[:, 0, u:u + 1], att_l[:, 1, u:u + 1], ALU.add))
                dve.reciprocal(att_l[:, 2, u:u + 1], att_l[:, 2, u:u + 1]).then_inc(S["rl_ok"], 1)

            for u in range(len(ATT) + 1):
                if u < len(ATT):
                    maxima(u)
                if u >= 1:
                    factor(u - 1)
            v.wait_ge(S["asum_mm"], 1)
            dve.tensor_scalar(ar, bank[0][:, :], 1.0 / AW, EPS, ALU.mult, ALU.add).then_inc(S["asum_out"], 1)
            v.wait_ge(S["ar_sqrt"], 1)
            link(dve.reciprocal(ar, ar))
            for c in range(4):
                dve.scalar_tensor_tensor(aT[:, c], aT[:, c], cols[:, C_AG + c:C_AG + c + 1], ar, ALU.mult, ALU.mult).then_inc(S["aT_ok"], 1)
            for t in range(TT):
                v.wait_ge(S["wo_mm"], t + 1)
                for n in range(2):
                    last = dve.tensor_tensor(wtmp[:, n], bank[(2 * t + 2 + n) % 8][:, :], gB[:, 0, n * 512:(n + 1) * 512], ALU.mult)
                link(last)
                dve.tensor_tensor(xt[:, t], xt[:, t], wtmp.rearrange("p a n -> p (a n)"), ALU.add).then_inc(S["xnew"], 1)
                v.wait_ge(S["xnew"], t + 1)
            v.wait_ge(S["n2_sq"], 1)
            dve.tensor_scalar(st[:, 0:4], st[:, 0:4], 1.0 / D, EPS, ALU.mult, ALU.add).then_inc(S["n2_lin"], 1)
            v.wait_ge(S["n2_sqrt"], 1)
            link(dve.reciprocal(st[:, 8:12], st[:, 0:4]))
            for t in range(TT):
                dve.tensor_scalar(hn[:, t], xt[:, t], st[:, 8 + t:9 + t], None, ALU.mult).then_inc(S["hn_ok"], 1)
            for k in range(KD):
                v.wait_ge(S["h2T_mm"], k + 1)
                dve.tensor_scalar(hT[:, k, :], bank[k % 4][:, :], modc[:, 24 + k, 0:1], modc[:, 16 + k, 0:1],
                                  ALU.mult, ALU.add).then_inc(S["h2T_ok"], 1)
            v.wait_ge(S["lg_mm"], 1)
            link(dve.tensor_tensor(R.lg, bank[4][:, 0:TT * NE].rearrange("p (t e) -> p t e", t=TT),
                                   rows[:, R_BR:R_BR + NE].unsqueeze(1).to_broadcast([P, TT, NE]), ALU.add))
            for t in range(TT):
                last = dve.max(R.v8[:, t], R.lg[:, t])
            link(last)
            for t in range(TT):
                last = dve.max_index(R.i8[:, t], R.v8[:, t], R.lg[:, t])
            link(last)
            dve.tensor_tensor(R.ex, R.v8[:, :, 0:TOPK], R.v8[:, :, 0:1].to_broadcast([P, TT, TOPK]), ALU.subtract).then_inc(S["route_shift"], 1)
            link(dve.tensor_copy(R.i8f, R.i8))
            link(dve.tensor_tensor(R.OH, R.i8f[:, :, 0:TOPK].unsqueeze(3).to_broadcast([P, TT, TOPK, NE]),
                                   konst[:, K_SLOT:K_SLOT + NE].unsqueeze(1).unsqueeze(1).to_broadcast([P, TT, TOPK, NE]), ALU.is_equal))
            dve.tensor_reduce(R.M, R.OH.rearrange("p t k e -> p t e k"), X, ALU.add).then_inc(S["onehot"], 1)
            v.wait_ge(S["cntc_mm"], 1)
            link(dve.tensor_tensor(R.nb4, bank[5][0:NE, 0:1].to_broadcast([NE, 4]), konst[0:NE, K_JN:K_JN + 4], ALU.is_gt))
            link(dve.tensor_reduce(R.nb, R.nb4, X, ALU.add))
            dve.tensor_copy(R.nbrep, R.nb.to_broadcast([NE, P])).then_inc(S["nbrep"], 1)
            v.wait_ge(S["route_exp"], 1)
            link(dve.tensor_reduce(R.sums[:, 0:4], R.ex, X, ALU.add))
            link(dve.reciprocal(R.sums[:, 4:8], R.sums[:, 0:4]))
            link(dve.tensor_tensor(R.gate, R.ex, R.sums[:, 4:8].unsqueeze(2).to_broadcast([P, TT, TOPK]), ALU.mult))
            v.wait_ge(S["bs_mm"], 1)
            link(dve.tensor_copy(R.bs, bank[7][:, 0:2 * NE]))
            link(dve.scalar_tensor_tensor(R.slot_of, R.bs[:, 0:NE].unsqueeze(1).to_broadcast([P, TT, NE]), float(SLOTS),
                                          bank[6][:, 0:TT * NE].rearrange("p (t e) -> p t e", t=TT), ALU.mult, ALU.add))
            link(dve.tensor_tensor(R.OHS, R.OH, R.slot_of.unsqueeze(2).to_broadcast([P, TT, TOPK, NE]), ALU.mult))
            link(dve.tensor_reduce(R.slot, R.OHS.rearrange("p t k e -> p (t k) e"), X, ALU.add))
            link(dve.tensor_tensor(R.GE, R.slot.unsqueeze(2).to_broadcast([P, 16, BW + 1]),
                                   konst[:, K_BN:K_BN + BW + 1].unsqueeze(1).to_broadcast([P, 16, BW + 1]), ALU.is_ge))
            link(dve.tensor_reduce(R.within, R.GE, X, ALU.add))
            link(dve.tensor_scalar(R.within, R.within, -float(SLOTS), float(SLOTS), ALU.mult, ALU.add))
            link(dve.tensor_tensor(R.within, R.within, R.slot, ALU.add))
            link(dve.tensor_tensor(R.S1, R.within.unsqueeze(2).to_broadcast([P, 16, SLOTS]),
                                   konst[:, K_SLOT:K_SLOT + SLOTS].unsqueeze(1).to_broadcast([P, 16, SLOTS]), ALU.is_equal))
            link(dve.tensor_tensor(R.B2[:, :, 0:BW], R.GE[:, :, 0:BW], R.GE[:, :, 1:BW + 1], ALU.subtract))
            link(dve.tensor_tensor(R.B2[:, :, BW:2 * BW], R.B2[:, :, 0:BW],
                                   R.gate.rearrange("p t k -> p (t k)").unsqueeze(2).to_broadcast([P, 16, BW]), ALU.mult))
            B4 = R.B2[:, :, 0:BW].rearrange("p (t k) b -> p t k b", t=TT)
            dve.tensor_tensor(B4, B4, konst[:, K_VAL:K_VAL + TT].unsqueeze(2).unsqueeze(3).to_broadcast([P, TT, TOPK, BW]),
                              ALU.mult).then_inc(S["onehot"], 1)
            link(dve.tensor_tensor(R.blkcmp, R.bs[0:1, NE:2 * NE].unsqueeze(1).to_broadcast([1, BW, NE]),
                                   konst[0:1, K_SLOT:K_SLOT + BW].unsqueeze(2).to_broadcast([1, BW, NE]), ALU.is_le))
            link(dve.tensor_reduce(R.blkf[:, 0:BW], R.blkcmp, X, ALU.add))
            link(dve.tensor_scalar(R.blkf[:, 0:BW], R.blkf[:, 0:BW], float(NE - 1), None, ALU.min))
            dve.tensor_copy(blk[:, 0:BW], R.blkf[:, 0:BW])
            dve.tensor_scalar(blk[:, BW:BW + NE], R.bs[0:1, NE:2 * NE], -1.0, None, ALU.add).then_inc(S["tables"], 1)
            v.wait_ge(S["tab_mm"], 1)
            link(dve.tensor_scalar(R.tok, bank[5][:, 0:BW], float(2 * L), None, ALU.add))
            dve.tensor_scalar(idx[:, 0], R.tok, float(L - 1), None, ALU.min)
            dve.tensor_scalar(idx[:, 1], R.tok, konst[:, K_ROW:K_ROW + 1], None, ALU.min)
            for n in (QUART, HALF):
                dve.tensor_scalar(more[n:n + 1, :], R.tok[n:n + 1, :], float(L), None, ALU.is_lt)
            dve.tensor_copy(tabs[:, :], bank[5][:, BW:2 * BW]).then_inc(S["tables"], 1)

            v.sem_inc(S["gate_ready"], 4)
            v.sem_inc(S["y_out"], 1)
            v.wait_ge(S["tables"], 2)
            nblk = v.value_load(blk[0:1, BW + NE - 1:BW + NE], min_val=0, max_val=BLOCKS - 1) + 1
            base = steps[0]
            PER = 10
            with blocks(v, nblk) as b:
                n = [0]

                def step(ins):
                    n[0] += 1
                    ins.then_inc(S["chain_v"], 1)
                    v.wait_ge(S["chain_v"], b * PER + (base + n[0]))

                def bounds(i, src, bias, by, n=SLOTS):
                    s = gu[:, i % 2]
                    if i >= 2:
                        v.wait_ge(S["h_ok"], 4 * b + i - 1)
                    s = s.rearrange("p q s -> p (q s)")
                    dve.tensor_tensor(s.rearrange("p (q h s) -> p q h s", h=2, s=n // 2),
                                      src[:, :].rearrange("p (q h s) -> p q h s", h=2, s=n // 2), bias, ALU.add).then_inc(S["gate_ready"], by)
                    v.wait_ge(S["gate_ready"], 4 * b + by * (i + 1) + 4)
                    g = s.rearrange("p (c r s) -> p c r s", r=2, s=n)
                    dve.tensor_scalar(g[:, :, 0], g[:, :, 0], LIMIT, None, ALU.min).then_inc(S["glu_p"], by)
                    step(dve.tensor_scalar(g[:, :, 1], g[:, :, 1], LIMIT, -LIMIT, ALU.min, ALU.max))

                def gates(i, by, n=SLOTS, dst=None):
                    g = gu[:, i % 2].rearrange("p q s -> p (q s)").rearrange("p (c r s) -> p c r s", r=2, s=n)
                    v.wait_ge(S["sig"], 4 * b + by * (i + 1))
                    step(dve.tensor_tensor(g[:, :, 0], g[:, :, 0],
                                           sg[:, i % 2].rearrange("p q s -> p (q s)").rearrange("p (c s) -> p c s", s=n), ALU.mult))
                    dve.scalar_tensor_tensor(gh[:, 2 * i:2 * i + 2, :] if dst is None else dst, g[:, :, 1], 1.0, g[:, :, 0], ALU.add, ALU.mult)\
                       .then_inc(S["h_ok"], by)

                e = v.value_load(blk[0:1, bass.ds(b, 1)], min_val=0, max_val=NE - 1)
                many = v.value_load(more[HALF:HALF + 1, bass.ds(b, 1)], min_val=0, max_val=1)
                dve.tensor_copy(gcur, tabs[:, bass.ds(b, 1)])
                dve.tensor_copy(ecur, ident[0:NE, bass.ds(e, 1)].to_broadcast([NE, P])).then_inc(S["ecur_ok"], 1)
                step(dve.tensor_copy(bcur, bgu[:, bass.ds(e, 1), :].rearrange("p o j -> p (o j)")))
                v.sem_inc(S["dve_step"], 1)
                n0 = n[0]
                with v.If(many > 0):
                    for i in range(4):
                        v.wait_ge(S["gu_mm"], 4 * b + i + 1)
                        bounds(i, bank[i], bcur[:, 4 * i:4 * i + 4].unsqueeze(2).unsqueeze(3).to_broadcast([P, 4, 2, HALF]), 1)
                        if i >= 1:
                            gates(i - 1, 1)
                    gates(3, 1)
                    v.wait_ge(S["down_mm"], b + 1)
                    v.wait_ge(S["scattered"], 16 * b + 16)
                    dve.scalar_tensor_tensor(yb[:, 0:512], bank[4][:, :], gcur, gB[:, 1, 0:512], ALU.mult, ALU.mult)
                    dve.scalar_tensor_tensor(yb[:, 512:D], bank[5][:, :], gcur, gB[:, 1, 512:D], ALU.mult, ALU.mult)\
                       .then_inc(S["y_out"], 1)
                    v.wait_ge(S["y_out"], b + 2)
                    for _ in range(PER - n[0]):
                        v.sem_inc(S["chain_v"], 1)
                with v.Else():
                    some = v.value_load(more[QUART:QUART + 1, bass.ds(b, 1)], min_val=0, max_val=1)
                    with v.If(some > 0):
                        n[0] = n0
                        halves = bcur.rearrange("p (h j) -> p j h", h=2)
                        step(dve.tensor_copy(gcur2[HALF:P], gcur[0:HALF]))
                        for i in range(2):
                            v.wait_ge(S["gu_T"], 4 * b + 2 * i + 2)
                            bounds(i, bank[2 + i], halves[:, 4 * i:4 * i + 4].unsqueeze(3).to_broadcast([P, 4, 2, HALF]), 2)
                            if i >= 1:
                                gates(i - 1, 2)
                        gates(1, 2)
                        v.wait_ge(S["down_mm"], b + 1)
                        v.wait_ge(S["scattered"], 16 * b + 16)
                        dve.scalar_tensor_tensor(yb[0:HALF, 0:512], bank[4][0:HALF, :], gcur[0:HALF], gB[0:HALF, 1, 0:512], ALU.mult, ALU.mult)
                        dve.scalar_tensor_tensor(yb[0:HALF, 512:D], bank[4][HALF:P, :], gcur2[HALF:P], gB[HALF:P, 1, 512:D], ALU.mult, ALU.mult)\
                           .then_inc(S["y_out"], 1)
                        v.wait_ge(S["y_out"], b + 2)
                        for _ in range(PER - n[0]):
                            v.sem_inc(S["chain_v"], 1)
                    with v.Else():
                        n[0] = n0
                        for m in range(1, 4):
                            last = dve.tensor_copy(gcur2[QUART * m:QUART * (m + 1)], gcur[0:QUART])
                        step(last)
                        v.wait_ge(S["gu_T"], 4 * b + 4)
                        bounds(0, bank[2], bcur.rearrange("p (h j) -> p j h", h=2).unsqueeze(3).to_broadcast([P, 8, 2, QUART]), 4, HALF)
                        gates(0, 4, HALF, gq)
                        v.wait_ge(S["down_mm"], b + 1)
                        v.wait_ge(S["scattered"], 16 * b + 16)
                        for m in range(4):
                            at, to = slice(QUART * m, QUART * (m + 1)), slice(256 * m, 256 * (m + 1))
                            last = dve.scalar_tensor_tensor(yb[0:QUART, to], bank[4][at, 0:256], (gcur2 if m else gcur)[at], gB[at, 1, to],
                                                            ALU.mult, ALU.mult)
                        last.then_inc(S["y_out"], 1)
                        v.wait_ge(S["y_out"], b + 2)
                        for _ in range(PER - n[0]):
                            v.sem_inc(S["chain_v"], 1)

        @block.scalar
        def _(act):
            f = nc.scalar.activation
            steps = [0]

            def link(ins):
                steps[0] += 1
                ins.then_inc(S["chain_a"], 1)
                act.wait_ge(S["chain_a"], steps[0])

            act.wait_ge(S["cc_in"], 16)
            f(sig_c[:, :, :], cc[:, :, :], ACT.Sigmoid).then_inc(S["silu_s"], 1)
            for i in range(3):
                act.wait_ge(S["fnet_lin"], i + 1)
                f(fh[i % 2], ftmp[0], ACT.Sin).then_inc(S["fnet_sin"], 1)
            act.wait_ge(S["x_in"], 16)
            act.wait_ge(S["ctx_in"], 16)
            for t in range(TT + CT):
                src = xt[:, t] if t < TT else ctxt[:, t - TT]
                last = f(square, src, ACT.Square, accum_out=st[:, t:t + 1])
                if t < TT + CT - 1:
                    link(last)
            last.then_inc(S["xs_sq"], 1)
            act.wait_ge(S["x_lin"], 1)
            f(st[:, 0:6], st[:, 0:6], ACT.Sqrt).then_inc(S["x_sqrt"], 1)
            act.wait_ge(S["piece_used"], 8)
            f(mrow_a, bank[0][:, :], ACT.Copy).then_inc(S["mrow_ok"], 1)
            for n in range(9):
                act.wait_ge(S["fspec_mm"], n + 1)
                if n < 8:
                    f(kspec[:, n], bank[5 + n % 3][:, :], ACT.Copy).then_inc(S["fspec_out"], 1)
                else:
                    act.wait_ge(S["fspec_out"], 8)
                    f(kspec[0:1, 4], bank[5 + n % 3][0:1, :], ACT.Copy).then_inc(S["fspec_out"], 1)
            act.wait_ge(S["nsum_mm"], 1)
            f(nrow, bank[1][:, :], ACT.Copy).then_inc(S["nrow_ok"], 1)
            act.wait_ge(S["ns_lin"], 1)
            f(st[:, 16:20], st[:, 16:20], ACT.Sqrt).then_inc(S["ns_sqrt"], 1)
            act.wait_ge(S["moda_out"], 1)
            for k in range(KD):
                act.wait_ge(S["hcT_mm"], k + 1)
                f(hcT[:, k, :], bank[6 + k % 2][:, 0:LC], ACT.Identity, bias=modc[:, k, 1:2], scale=modc[:, 8 + k, 1:2])\
                    .then_inc(S["hcT_ok"], 1)
            act.wait_ge(S["unit_out"], 3 * HC)
            for n in range(3 * HC, len(UNITS)):
                i, kind, t = UNITS[n]
                act.wait_ge(S["unit_mm"], n + 1)
                dst = kvc[:, t] if kind == "c" else qkv[:, t, i * 256:(i + 1) * 256]
                f(dst, bank[n % 4][:, 0:256], ACT.Copy).then_inc(S["unit_out"], 1)
                if n == B_END:
                    act.wait_ge(S["piece_used"], 24)
                    for h in range(2):
                        f(mrow_b[h], bank[6 + h][:, :], ACT.Copy).then_inc(S["mrow_ok"], 1)
                if n == Z_AT:
                    for t in range(TT):
                        act.wait_ge(S["zT_mm"], t + 1)
                        f(ztok[:, t], bank[4 + t][:, :], ACT.Copy).then_inc(S["zT_ok"], 1)
            act.wait_ge(S["qk_lin"], 1)
            f(st[:, 32:76], st[:, 32:76], ACT.Sqrt).then_inc(S["qk_sqrt"], 1)
            for n in range(8):
                act.wait_ge(S["uspec_mm"], n + 1)
                f(uspec[:, n // 2 + 4 * (n % 2)], bank[n % 4][:, :], ACT.Copy).then_inc(S["uspec_out"], 1)
            for c in range(HC):
                act.wait_ge(S["y_mul"], c + 1)
                f(ztok[:, c], v2[:, c], ACT.Square).then_inc(S["ysq"], 1)
            act.wait_ge(S["ysum_out"], 1)
            f(half[:, 0:512], half[:, 0:512], ACT.Sqrt).then_inc(S["yr_sqrt"], 1)
            for j in range(8):
                act.wait_ge(S["qkT_mm"], j + 1)
                if j < 4:
                    f(qT[:, j], bank[j % 4][:, :], ACT.Copy).then_inc(S["qkT_ok"], 1)
                else:
                    kv, part = (j - 4) // 2, (j - 4) % 2
                    keys = slice(0, L) if part == 0 else slice(L, L + LC)
                    n = keys.stop - keys.start
                    f(kz[0][0:64, kv, keys], bank[j % 4][0:64, 0:n], ACT.Copy)
                    f(kz[1][64:P, kv, keys], bank[j % 4][64:P, 0:n], ACT.Copy).then_inc(S["qkT_ok"], 1)

            def out_T(qb):
                act.wait_ge(S["pv_mm"], qb + 1)
                f(aT[:, :, qb * P:(qb + 1) * P], bank[6 + qb % 2][:, :].rearrange("p (h q) -> p h q", h=4), ACT.Copy)\
                    .then_inc(S["a_ok"], 1)

            def copy_T(u):
                qb, h = ATT[u]
                lo, hi = local_keys(qb)
                act.wait_ge(S["pT_mm"], u + 1)
                if qb >= 1 and h == 0:
                    act.wait_ge(S["pv_mm"], qb)
                dst, at = pt[h // 4], (h % 4) * P
                last = f(dst[:, 0:4, at:at + P], bank[4][:, :].rearrange("p (j q) -> p j q", j=4), ACT.Copy)
                if (hi - lo + LC) // P > 4:
                    last = f(dst[:, 4, at:at + P], bank[5][:, 0:P], ACT.Copy)
                last.then_inc(S["pT_ok"], 1)

            def exponentials(u):
                qb, h = ATT[u]
                lo, hi = local_keys(qb)
                w = 1 + hi - lo
                act.wait_ge(S["s_max"], u + 1)
                f(pbuf(u)[:, 0:w], pbuf(u)[:, 0:w], ACT.Exp, bias=att_neg[:, u:u + 1], scale=ATTN_SCALE, accum_out=att_l[:, 0, u:u + 1])
                f(pbuf(u)[:, w:w + LC], bank[2 * (u % 2) + 1][:, 0:LC], ACT.Exp, bias=att_neg[:, u:u + 1], scale=ATTN_SCALE,
                  accum_out=att_l[:, 1, u:u + 1]).then_inc(S["p_exp"], 1)

            for u in range(len(ATT) + 3):
                if u >= 3:
                    copy_T(u - 3)
                if u < len(ATT):
                    exponentials(u)
                if u > NQ and u % NQ == 4 and u < len(ATT):
                    out_T(u // NQ - 1)
            out_T(TT - 1)
            act.wait_ge(S["a_ok"], TT)
            for c in range(4):
                f(asq[:, c], aT[:, c], ACT.Square).then_inc(S["asq"], 1)
            act.wait_ge(S["asum_out"], 1)
            f(ar, ar, ACT.Sqrt).then_inc(S["ar_sqrt"], 1)
            for t in range(TT):
                act.wait_ge(S["xnew"], t + 1)
                last = f(slab[:, 0:D], xt[:, t], ACT.Square, accum_out=st[:, t:t + 1])
                if t < TT - 1:
                    link(last)
            last.then_inc(S["n2_sq"], 1)
            act.wait_ge(S["n2_lin"], 1)
            f(st[:, 0:4], st[:, 0:4], ACT.Sqrt).then_inc(S["n2_sqrt"], 1)
            for t in range(TT):
                act.wait_ge(S["hn_ok"], t + 1)
                act.dma_start(d_hn[t * P:(t + 1) * P, :], hn[:, t]).then_inc(S["hn_stored"], 16)
            for t in range(TT - 1):
                act.dma_start(t_out[t * P:(t + 1) * P, :], xt[:, t]).then_inc(S["acc_in"], 16)
            act.wait_ge(S["lgq_mm"], 1)
            f(lgq, bank[5][:, :], ACT.Copy).then_inc(S["lgq_ok"], 1)
            act.wait_ge(S["route_shift"], 1)
            f(R.ex, R.ex, ACT.Exp).then_inc(S["route_exp"], 1)

            def modulate(at):
                act.wait_ge(S["xsT_mm"], at)
                for k in range(KD):
                    last = f(xsT[:, k], bank[6 + k // 4][:, (k % 4) * P:(k % 4 + 1) * P], ACT.Identity,
                             bias=modc[:, 16 + k, 0:1], scale=modc[:, 24 + k, 0:1])
                    if k % 4 == 3:
                        last.then_inc(S["xsT_ok"], 1)

            f(sig_c[:, :, :], cc[:, :, :], ACT.Sigmoid)
            modulate(1)
            act.wait_ge(S["tables"], 2)
            nblk = act.value_load(blk[0:1, BW + NE - 1:BW + NE], min_val=0, max_val=BLOCKS - 1) + 1
            with blocks(act, nblk) as b:
                many = act.value_load(more[HALF:HALF + 1, bass.ds(b, 1)], min_val=0, max_val=1)

                def sigmoid(i, by, n=SLOTS):
                    g = gu[:, i % 2].rearrange("p q s -> p (q s)").rearrange("p (c r s) -> p c r s", r=2, s=n)
                    act.wait_ge(S["glu_p"], 4 * b + by * (i + 1))
                    f(sg[:, i % 2].rearrange("p q s -> p (q s)").rearrange("p (c s) -> p c s", s=n), g[:, :, 0], ACT.Sigmoid, scale=ALPHA).then_inc(S["sig"], by)

                with act.If(many > 0):
                    act.sem_inc(S["gu_sb"], 2)
                    for i in range(4):
                        sigmoid(i, 1)
                with act.Else():
                    some = act.value_load(more[QUART:QUART + 1, bass.ds(b, 1)], min_val=0, max_val=1)
                    with act.If(some > 0):
                        for g in range(2):
                            act.wait_ge(S["gu_mm"], 4 * b + 2 * g + 2)
                            f(gusb[:, g], bank[g][:, :], ACT.Identity).then_inc(S["gu_sb"], 1)
                        for i in range(2):
                            sigmoid(i, 2)
                    with act.Else():
                        act.wait_ge(S["gu_mm"], 4 * b + 4)
                        f(gusb[:, 0], bank[0][:, :], ACT.Identity).then_inc(S["gu_sb"], 2)
                        sigmoid(0, 4, HALF)
                modulate(b + 2)
            act.wait_ge(S["scattered"], 32)

        @block.gpsimd
        def _(pool):
            nc.gpsimd.memset(ones[:, :], 1.0).then_inc(S["ones_ok"], 1)
            for t in range(TT):
                pool.wait_ge(S["filt_tile"], t + 1)
                nc.gpsimd.tensor_tensor(sq[:, t], fa[:, t], fa[:, t], ALU.mult).then_inc(S["filt_sq"], 1)
                nc.gpsimd.tensor_tensor(sq[:, TT + t], fb[:, t], fb[:, t], ALU.mult).then_inc(S["filt_sq"], 1)

            pool_ = nc.gpsimd
            steps = [0]

            def link(ins):
                steps[0] += 1
                ins.then_inc(S["chain_p"], 1)
                pool.wait_ge(S["chain_p"], steps[0])

            pool.wait_ge(S["qk_factor"], 1)
            qk = qkv[:, :, 0:AW + KVW]
            qk4 = qk.rearrange("p t (h d) -> p t h d", d=HD)
            kc4 = kvc[:, :, 0:KVW].rearrange("p t (h d) -> p t h d", d=HD)
            pool_.tensor_tensor(qk4, qk4, st[:, 80:120].rearrange("p (t h) -> p t h", t=TT).unsqueeze(3).to_broadcast([P, TT, NQ + NKV, HD]), ALU.mult)
            link(pool_.tensor_tensor(kc4, kc4, st[:, 120:124].rearrange("p (t h) -> p t h", t=CT).unsqueeze(3).to_broadcast([P, CT, NKV, HD]), ALU.mult))

            def gain(at, t, h):
                return rows[:, at:at + HD].unsqueeze(1).unsqueeze(1).to_broadcast([P, t, h, HD])

            pool_.tensor_tensor(qk4[:, :, 0:NQ], qk4[:, :, 0:NQ], gain(R_QN, TT, NQ), ALU.mult)
            pool_.tensor_tensor(qk4[:, :, NQ:], qk4[:, :, NQ:], gain(R_KN, TT, NKV), ALU.mult)
            link(pool_.tensor_tensor(kc4, kc4, gain(R_KN, CT, NKV), ALU.mult))
            pairs = qk.rearrange("p t (g j i) -> p t g j i", j=2, i=HD // 4)
            swapped = rot[0].rearrange("p t (g j i) -> p t g j i", j=2, i=HD // 4)
            pool_.tensor_copy(swapped[:, :, :, 0], pairs[:, :, :, 1])
            link(pool_.tensor_copy(swapped[:, :, :, 1], pairs[:, :, :, 0]))

            def turn(at):
                return konst[:, at:at + TT * HD].rearrange("p (t d) -> p t d", t=TT).unsqueeze(2).to_broadcast([P, TT, NQ + NKV, HD])

            rot4 = [r.rearrange("p t (h d) -> p t h d", d=HD) for r in rot]
            pool_.tensor_tensor(rot4[0], rot4[0], turn(K_RS), ALU.mult)
            link(pool_.tensor_tensor(rot4[1], qk4, turn(K_RC), ALU.mult))
            link(pool_.tensor_tensor(qk4, rot4[0], rot4[1], ALU.add))
            for r in range(2):
                pool_.tensor_copy(kd[:, 0:TT, :, r], qk4[:, :, NQ:])
                last = pool_.tensor_copy(kd[:, TT:, :, r], kc4)
            last.then_inc(S["qk_ok"], 1)
            pool.wait_ge(S["qk_ok"], 1)
            pool.wait_ge(S["modb_out"], 1)
            nc.gpsimd.memset(kz[0][64:P, :, :], 0.0).then_inc(S["kz_ok"], 1)
            pool.wait_ge(S["kz_ok"], 1)
            pool.wait_ge(S["ysum_mm"], 1)
            nc.gpsimd.memset(kz[1][0:64, :, :], 0.0).then_inc(S["kz_ok"], 1)
            pool.wait_ge(S["kz_ok"], 2)
            for u in range(len(ATT)):
                lo, hi = local_keys(ATT[u][0])
                pool.wait_ge(S["rl_ok"], u + 1)
                w = pbuf(u)[:, 1:1 + hi - lo + LC]
                nc.gpsimd.tensor_scalar(w, w, att_l[:, 2, u:u + 1], 1.0, ALU.mult, ALU.mult).then_inc(S["p_ok"], 1)

            def gather(n):
                pool.indirect_dma_start(out=xs[0:n], out_offset=None, in_=d_hn,
                                        in_offset=bass.IndirectOffsetOnAxis(ap=icur[0:n, 0:1].bitcast(u32), axis=0)).then_inc(S["gathered"], 16)

            def add_rows(n):
                pool.indirect_dma_start(out=t_out, out_offset=bass.IndirectOffsetOnAxis(ap=icur[0:n, 1:2].bitcast(u32), axis=0),
                                        in_=yb[0:n], in_offset=None, compute_op=ALU.add,
                                        bounds_check=L - 1, oob_is_err=False).then_inc(S["scattered"], 16)

            pool.wait_ge(S["wo_mm"], TT)
            nc.gpsimd.memset(xs, 0.0).then_inc(S["chain_p"], 1)
            done = steps[0]
            pool.wait_ge(S["tables"], 2)
            pool.wait_ge(S["hn_stored"], 16 * TT)
            nc.gpsimd.tensor_copy(icur[:, 0:1], idx[:, 0, 0:1]).then_inc(S["chain_p"], 1)
            pool.wait_ge(S["chain_p"], done + 2)
            gather(SLOTS)
            pool.wait_ge(S["xnew"], TT)
            pool.dma_start(t_out[(TT - 1) * P:, :], xt[:, TT - 1]).then_inc(S["scattered"], 16)
            pool.wait_ge(S["scattered"], 16)
            pool.wait_ge(S["acc_in"], 16 * (TT - 1))
            nblk = pool.value_load(blk[0:1, BW + NE - 1:BW + NE], min_val=0, max_val=BLOCKS - 1) + 1
            pool.wait_ge(S["xsT_mm"], 1)
            nc.gpsimd.tensor_copy(icur[:, 0:1], idx[:, 0, 1:2]).then_inc(S["chain_p"], 1)
            pool.wait_ge(S["chain_p"], done + 3)
            gather(SLOTS)
            with blocks(pool, nblk) as b:
                many = pool.value_load(more[HALF:HALF + 1, bass.ds(b, 1)], min_val=0, max_val=1)
                some = pool.value_load(more[QUART:QUART + 1, bass.ds(b, 1)], min_val=0, max_val=1)
                after_many = pool.value_load(more[HALF:HALF + 1, bass.ds(b + 2, 1)], min_val=0, max_val=1)
                after_some = pool.value_load(more[QUART:QUART + 1, bass.ds(b + 2, 1)], min_val=0, max_val=1)
                pool.wait_ge(S["xsT_mm"], b + 2)
                pool.sem_inc(S["pool_step"], 1)
                nc.gpsimd.tensor_copy(icur[:, 0:1], idx[:, 0, bass.ds(b + 2, 1)]).then_inc(S["chain_p"], 1)
                pool.wait_ge(S["chain_p"], 2 * b + (done + 4))
                pool.sem_inc(S["pool_step"], 1)
                with pool.If(after_many > 0):
                    gather(SLOTS)
                with pool.Else():
                    with pool.If(after_some > 0):
                        gather(HALF)
                    with pool.Else():
                        gather(QUART)
                pool.wait_ge(S["scattered"], 16 * b + 16)
                pool.sem_inc(S["pool_step"], 1)
                nc.gpsimd.tensor_copy(icur[:, 1:2], idx[:, 1, bass.ds(b, 1)]).then_inc(S["chain_p"], 1)
                pool.wait_ge(S["chain_p"], 2 * b + (done + 5))
                pool.wait_ge(S["y_out"], b + 2)
                pool.sem_inc(S["pool_step"], 1)
                with pool.If(many > 0):
                    add_rows(SLOTS)
                with pool.Else():
                    with pool.If(some > 0):
                        add_rows(HALF)
                    with pool.Else():
                        add_rows(QUART)
                pool.sem_inc(S["pool_step"], 1)
            pool.wait_ge(S["scattered"], nblk * 16 + 16)
            pool.sem_inc(S["pool_step"], 1)
            pool.wait_ge(S["gathered"], nblk * 16 + 32)
            pool.sem_inc(S["pool_step"], 1)


def _constants():
    import numpy as np
    f32 = np.float32
    n = 2 * L
    t = np.arange(L)
    ang = 2.0 * np.pi * ((t[:, None] * np.arange(L)[None, :]) % n) / n
    nyq = np.where(t % 2 == 0, 1.0, -1.0)
    cos, sin = np.cos(ang), -np.sin(ang)
    sin[:, 0] = nyq
    dft = np.concatenate([cos, sin], axis=1)
    scale = np.full((n, 1), 2.0 / n)
    scale[0] = scale[L] = 1.0 / n
    idft = dft.T * scale
    konst = np.zeros((P, NK), f32)
    i = np.arange(P)
    konst[:, K_ID:K_ID + P] = np.eye(P)
    konst[:, K_TRI:K_TRI + P] = i[:, None] < i[None, :]
    konst[:, K_MASK:K_MASK + P] = np.where(i[None, :] >= i[:, None], 0.0, -1e30)
    konst[:, K_MASK + 2 * P:K_MASK + 3 * P] = np.where(i[None, :] <= i[:, None], 0.0, -1e30)
    nf = HD // 4
    inv = (f32(10000.0) ** (-np.arange(nf, dtype=f32) / f32(nf))).astype(f32)
    for tile in range(TT):
        pos = tile * P + i
        for j, p in enumerate((pos // 64, pos % 64)):
            a = (p[:, None].astype(f32) * inv[None, :]).astype(f32)
            at = tile * HD + j * 2 * nf
            for r in range(2):
                konst[:, K_RC + at + r * nf:K_RC + at + (r + 1) * nf] = np.cos(a)
                konst[:, K_RS + at + r * nf:K_RS + at + (r + 1) * nf] = (-1.0, 1.0)[r] * np.sin(a)
    konst[:, K_SLOT:K_SLOT + SLOTS] = np.arange(SLOTS)
    konst[:, K_BN:K_BN + 64] = SLOTS * np.arange(64)
    konst[:, K_VAL:K_VAL + TT] = np.arange(TT)[None, :] * P + i[:, None] - 2 * L
    konst[:, K_ROW] = L + i
    e = np.arange(NE)
    konst[0:NE, K_TRE:K_TRE + NE] = e[:, None] < e[None, :]
    konst[0:NE, K_TRE + NE:K_TRE + 2 * NE] = e[:, None] <= e[None, :]
    konst[:, K_JN:K_JN + 4] = SLOTS * np.arange(4)
    konst[:, K_JN] = -1.0
    konst[0:P:32, K_Q4] = 1.0
    konst[:, K_S4:K_S4 + NE] = np.tile(np.eye(NE), (4, 1))
    tl = np.linspace(0.0, 1.0, L, dtype=f32)[:, None]
    w = (f32(2.0 * np.pi) * np.arange(L, dtype=f32)[:, None] / f32(L)).astype(f32)
    bands = np.linspace(1e-4, 15, 16, dtype=f32)[None, :]
    zf = np.concatenate([tl, np.cos(bands * w), -np.sin(bands * w)], axis=1).astype(f32)
    lo, hi = -np.log(1e-2) / 1.5, -np.log(1e-2) / 0.3
    deltas = np.linspace(lo, hi, HW, dtype=f32)
    decay = np.exp(-tl * deltas[None, :]).astype(f32)
    return konst, zf.T.copy(), decay, dft.astype(f32), idft.astype(f32)


def kernel(**inputs):
    import numpy as np
    import concourse.bacc as bacc
    from concourse.bass_utils import run_bass_kernel_spmd

    g = {k: np.asarray(v) for k, v in inputs.items()}
    konst, zf, decay, dft, idft = _constants()

    def columns(a):
        return a.reshape(-1, P).T

    def by_head(a):
        return a.reshape(NKV, NQ // NKV, HD, -1).transpose(1, 0, 2, 3).reshape(AW, -1)

    g["attn_out_norm"] = by_head(g["attn_out_norm"][0])
    g["w_out"] = np.concatenate([by_head(g["w_out"][0, :AW]), g["w_out"][0, AW:]], axis=0)[None]
    cols = np.concatenate([columns(g[k]) for k in ("b_mod", "norm1", "norm2", "conv_w", "conv_b", "filt_bias",
                                                    "attn_out_norm", "hyena_out_norm")], axis=1)
    rows = np.concatenate([g[k].reshape(1, -1) for k in ("q_norm", "k_norm", "sink", "b_router")], axis=1)
    cc = np.stack([g["c"].reshape(KD, P), g["c_ctx"].reshape(KD, P)], axis=-1).transpose(1, 0, 2)
    bgu = g["b_gu"].reshape(NE, 2, KF, P).transpose(3, 0, 2, 1).reshape(P, NE, 2 * KF)
    arrays = {
        "x": g["x"].reshape(L, D), "ctx": g["ctx"].reshape(LC, D), "cc": cc, "cols": cols, "rows": rows,
        "konst": konst, "z": zf, "w1": g["filt_w1"][0], "w23": np.stack([g["filt_w2"][0], g["filt_w3"][0]], axis=1),
        "fcol": np.stack([g[k][0] for k in ("filt_b1", "filt_b2", "filt_b3", "filt_freq")], axis=1),
        "w4": g["filt_w4"][0], "decay": decay, "dft": dft, "idft": idft, "wmod": g["w_mod"][0],
        "brows": np.concatenate([g["b_mod"][:, 2 * D:3 * D], g["b_mod"][:, 5 * D:6 * D]], axis=1),
        "win": g["w_in"][0], "wout": g["w_out"][0], "wr": g["w_router"][0], "bgu": bgu,
        "wgu": g["w_gu"].reshape(NE * KD, P, 2 * FF), "wdown": g["w_down"].reshape(NE * 4, 2, P, D),
        "bdown": g["b_down"][0],
    }
    nc = bacc.Bacc("TRN2", target_bir_lowering=False, num_devices=1)
    arrays = {f"in_{k}": np.ascontiguousarray(a) for k, a in arrays.items()}
    args = [nc.dram_tensor(k, a.shape, mybir.dt.from_np(a.dtype), kind="ExternalInput").ap() for k, a in arrays.items()]
    args.append(nc.dram_tensor("out", (L, D), mybir.dt.float32, kind="ExternalOutput").ap())
    layer_kernel(nc, *args)
    r = run_bass_kernel_spmd(nc, [arrays], core_ids=[0])
    return r.results[0]["out"].reshape(1, L, D)
```
